# Optimizing a Trainium2 kernel written in Bass

```python
import jax, jax.numpy as jnp
from jax import lax
import numpy as np

D_MODEL = 1024
BATCH = 1
SEQ = 1024
DEPTH = 2
DEC_BATCH = 8
DEC_SEQ = 4
PAST_LEN = 8192
PAGE_SIZE = 128

N_EVEN = (DEPTH + 1) // 2
N_ODD = DEPTH // 2
EPS = 1e-6
A_CH = 256
A_CONV = 31
B_HEAD_DIM = 64
B_HPG = 4
B_WINDOWS = (128, 512, 2048)
B_DILATIONS = (1, 4, 16)
B_GROUPS = 3
B_HEADS = B_GROUPS * B_HPG
B_SUB_WINDOW = 128
B_BLOCK = 128
N_BUCKETS = 32
MAX_DISTANCE = 2048
C_CH = 512
C_CONV = 3
D_CH = 512
D_GROUPS = 4
D_GROUP_CH = D_CH // D_GROUPS
D_CHUNK = 128
FFN_HIDDEN = -(-8 * D_MODEL // (3 * 256)) * 256
E_IN = 2 * A_CH + 3 * B_HEADS * B_HEAD_DIM
E_OUT_IN = A_CH + B_HPG * B_HEAD_DIM
O_IN = 3 * C_CH + 2 * D_CH
O_OUT_IN = C_CH + D_CH

kernel_name = "hybrid_confconv_dilattn_shortconv_gmlp_step"

def _rmsnorm(x, g):
    xf = x.astype(jnp.float32)
    y = xf * lax.rsqrt(jnp.mean(xf * xf, axis=-1, keepdims=True) + EPS)
    return (y * g.astype(jnp.float32)).astype(x.dtype)

def _layernorm(x, g, b):
    xf = x.astype(jnp.float32)
    mu = jnp.mean(xf, axis=-1, keepdims=True)
    var = jnp.mean(jnp.square(xf - mu), axis=-1, keepdims=True)
    y = (xf - mu) * lax.rsqrt(var + EPS)
    return (y * g.astype(jnp.float32) + b.astype(jnp.float32)).astype(x.dtype)

def _t5_bucket(dist):
    n = np.maximum(np.asarray(dist, dtype=np.int64), 0)
    max_exact = N_BUCKETS // 2
    large = max_exact + (np.log(np.maximum(n, 1) / max_exact) / np.log(MAX_DISTANCE / max_exact)
                         * (N_BUCKETS - max_exact)).astype(np.int32)
    return np.where(n < max_exact, n, np.minimum(large, N_BUCKETS - 1)).astype(np.int32)

def _group_bias(rel_bias_table, grp, dist):
    tab = rel_bias_table[:, grp * B_HPG:(grp + 1) * B_HPG]
    return jnp.moveaxis(tab[_t5_bucket(dist)], -1, 0).astype(jnp.float32)

def _causal_dwconv(x_ext, w, b):
    y = lax.conv_general_dilated(x_ext, w[:, None, :], window_strides=(1,), padding='VALID',
                                 dimension_numbers=('NWC', 'WIO', 'NWC'),
                                 feature_group_count=w.shape[1])
    return y + b

def _dilated_attn_prompt(q, k, v, d, rel_bias_table, grp):
    N, T, H, Dh = q.shape
    L = T // d
    nb = -(-L // B_BLOCK)
    Lp = nb * B_BLOCK

    def to_sub(x):
        x = x.reshape(N, L, d, H, Dh).transpose(0, 2, 1, 3, 4).reshape(N * d, L, H, Dh)
        x = jnp.pad(x, ((0, 0), (0, Lp - L), (0, 0), (0, 0)))
        return x.reshape(N * d, nb, B_BLOCK, H, Dh)

    def with_prev(xb):
        prev = jnp.pad(xb, ((0, 0), (1, 0), (0, 0), (0, 0), (0, 0)))[:, :-1]
        return jnp.concatenate([prev, xb], axis=2)

    qb = to_sub(q)
    kk = with_prev(to_sub(k))
    vv = with_prev(to_sub(v))
    qi = np.arange(B_BLOCK)[:, None]
    ki = np.arange(2 * B_BLOCK)[None, :]
    rel = qi + B_BLOCK - ki
    band = (rel >= 0) & (rel <= B_SUB_WINDOW)
    key_ok = (np.arange(nb)[:, None, None] > 0) | (ki >= B_BLOCK)[None]
    mask = band[None] & key_ok
    bias = _group_bias(rel_bias_table, grp, np.clip(rel, 0, None) * d)
    s = jnp.einsum('znqhd,znkhd->znhqk', qb, kk).astype(jnp.float32) * (Dh ** -0.5) + bias[None, None]
    s = jnp.where(mask[None, :, None], s, -jnp.inf)
    lse = jax.nn.logsumexp(s, axis=-1)
    p = jnp.exp(s - lse[..., None])
    o = jnp.einsum('znhqk,znkhd->znqhd', p.astype(v.dtype), vv)
    o = o.reshape(N * d, Lp, H, Dh)[:, :L].reshape(N, d, L, H, Dh).transpose(0, 2, 1, 3, 4).reshape(N, T, H, Dh)
    lse = lse.transpose(0, 1, 3, 2).reshape(N * d, Lp, H)[:, :L]
    lse = lse.reshape(N, d, L, H).transpose(0, 2, 1, 3).reshape(N, T, H)
    return o, lse

def _dilated_attn_sample(q, k_ext, v_ext, d, rel_bias_table, grp):
    N, S, H, Dh = q.shape
    Wb = k_ext.shape[1] - S
    steps = np.arange(B_SUB_WINDOW + 1)
    idx = Wb + np.arange(S)[:, None] - steps[None, :] * d
    valid = idx >= 0
    idx_c = np.maximum(idx, 0)
    kg = k_ext[:, idx_c]
    vg = v_ext[:, idx_c]
    bias = _group_bias(rel_bias_table, grp, steps * d)
    s = jnp.einsum('nshd,nskhd->nhsk', q, kg).astype(jnp.float32) * (Dh ** -0.5) + bias[None, :, None, :]
    s = jnp.where(valid[None, None], s, -jnp.inf)
    lse = jax.nn.logsumexp(s, axis=-1)
    p = jnp.exp(s - lse[..., None])
    o = jnp.einsum('nhsk,nskhd->nshd', p.astype(v_ext.dtype), vg)
    return o, lse.transpose(0, 2, 1)

def _even_mixer(h, P, e, a_buf, kv_bufs):
    N, T, _ = h.shape
    proj = h @ P['e_w_in'][e]
    a_in = proj[..., :2 * A_CH]
    qkv = proj[..., 2 * A_CH:].reshape(N, T, 3, B_GROUPS, B_HPG, B_HEAD_DIM)
    glu = a_in[..., :A_CH] * jax.nn.sigmoid(a_in[..., A_CH:])
    if a_buf is None:
        a_ext = jnp.pad(glu, ((0, 0), (A_CONV - 1, 0), (0, 0)))
    else:
        a_ext = jnp.concatenate([a_buf.astype(glu.dtype), glu], axis=1)
    a_state = a_ext[:, -(A_CONV - 1):]
    a = _causal_dwconv(a_ext, P['a_conv_w'][e], P['a_conv_b'][e])
    a = jax.nn.silu(_layernorm(a, P['a_ln_g'][e], P['a_ln_b'][e]))
    outs, lses, kv_states = [], [], []
    for grp in range(B_GROUPS):
        q, k, v = qkv[:, :, 0, grp], qkv[:, :, 1, grp], qkv[:, :, 2, grp]
        d = B_DILATIONS[grp]
        if kv_bufs is None:
            o, lse = _dilated_attn_prompt(q, k, v, d, P['rel_bias_table'], grp)
            kv_states.append(jnp.stack([k, v], axis=2)[:, -min(B_WINDOWS[grp], T):])
        else:
            kv_ext = jnp.concatenate([kv_bufs[grp].astype(q.dtype), jnp.stack([k, v], axis=2)], axis=1)
            o, lse = _dilated_attn_sample(q, kv_ext[:, :, 0], kv_ext[:, :, 1], d, P['rel_bias_table'], grp)
            kv_states.append(kv_ext[:, T:])
        outs.append(o)
        lses.append(lse)
    alpha = jax.nn.softmax(jnp.stack(lses, axis=0), axis=0)
    attn = jnp.sum(alpha[..., None] * jnp.stack(outs, axis=0).astype(jnp.float32), axis=0)
    attn = attn.astype(h.dtype).reshape(N, T, B_HPG * B_HEAD_DIM)
    out = jnp.concatenate([a, attn], axis=-1) @ P['e_w_out'][e]
    return out, a_state, kv_states

def _odd_mixer(h, P, oi, c_buf):
    N, T, _ = h.shape
    proj = h @ P['o_w_in'][oi]
    bg = proj[..., :C_CH]
    cg = proj[..., C_CH:2 * C_CH]
    xi = proj[..., 2 * C_CH:3 * C_CH]
    uv = jax.nn.gelu(proj[..., 3 * C_CH:])
    ci = cg * xi
    if c_buf is None:
        c_ext = jnp.pad(ci, ((0, 0), (C_CONV - 1, 0), (0, 0)))
    else:
        c_ext = jnp.concatenate([c_buf.astype(ci.dtype), ci], axis=1)
    c_state = c_ext[:, -(C_CONV - 1):]
    yc = bg * _causal_dwconv(c_ext, P['c_conv_w'][oi], P['c_conv_b'][oi])
    u = uv[..., :D_CH]
    v = _layernorm(uv[..., D_CH:], P['d_ln_g'][oi], P['d_ln_b'][oi])
    ws = jnp.where(np.tril(np.ones((D_CHUNK, D_CHUNK), dtype=bool))[None], P['d_spatial_w'][oi], 0)
    bs = P['d_spatial_b'][oi]
    if c_buf is None:
        vb = v.reshape(N, T // D_CHUNK, D_CHUNK, D_GROUPS, D_GROUP_CH)
        mix = jnp.einsum('gij,nkjgc->nkigc', ws, vb) + bs.T[None, None, :, :, None]
    else:
        vb = v.reshape(N, T, D_GROUPS, D_GROUP_CH)
        mix = jnp.einsum('gij,njgc->nigc', ws[:, :T, :T], vb) + bs.T[None, :T, :, None]
    yd = u * mix.reshape(N, T, D_CH)
    out = jnp.concatenate([yc, yd], axis=-1) @ P['o_w_out'][oi]
    return out, c_state, v

def _trunk(x, c, P, a_bufs, kv_bufs, c_bufs):
    N = x.shape[0]
    a_st, kv_st, c_st, d_st = [], [[] for _ in range(B_GROUPS)], [], []
    cs = jax.nn.silu(c)
    for layer in range(DEPTH):
        mod = (cs @ P['ada_w'][layer] + P['ada_b'][layer]).reshape(N, 6, 1, D_MODEL)
        h = _rmsnorm(x, P['norm_mix_g'][layer]) * (1 + mod[:, 1]) + mod[:, 0]
        if layer % 2 == 0:
            e = layer // 2
            mix, a_new, kv_new = _even_mixer(h, P, e, None if a_bufs is None else a_bufs[e],
                                             None if kv_bufs is None else [buf[e] for buf in kv_bufs])
            a_st.append(a_new)
            for grp in range(B_GROUPS):
                kv_st[grp].append(kv_new[grp])
        else:
            oi = layer // 2
            mix, c_new, v_new = _odd_mixer(h, P, oi, None if c_bufs is None else c_bufs[oi])
            c_st.append(c_new)
            d_st.append(v_new)
        x = x + mod[:, 2] * mix
        h = _rmsnorm(x, P['norm_ffn_g'][layer]) * (1 + mod[:, 4]) + mod[:, 3]
        gu = h @ P['ffn_w_gate_up'][layer]
        x = x + mod[:, 5] * ((jax.nn.silu(gu[..., :FFN_HIDDEN]) * gu[..., FFN_HIDDEN:]) @ P['ffn_w_down'][layer])
    y = _rmsnorm(x, P['final_norm_g'])
    return y, jnp.stack(a_st), [jnp.stack(s) for s in kv_st], jnp.stack(c_st), d_st

def setup_inputs(seed: int = 0) -> dict:
    key = jax.random.key(seed)
    ks = jax.random.split(key, 40)
    nrm = jax.random.normal
    f32 = jnp.float32
    out = {}
    out['x_prompt'] = nrm(ks[0], (BATCH, SEQ, D_MODEL), f32)
    out['x_sample'] = nrm(ks[1], (DEC_BATCH, DEC_SEQ, D_MODEL), f32)
    out['c_prompt'] = nrm(ks[2], (BATCH, D_MODEL), f32)
    out['c_sample'] = nrm(ks[3], (DEC_BATCH, D_MODEL), f32)
    out['state_a_conv'] = 0.5 * nrm(ks[4], (N_EVEN, DEC_BATCH, A_CONV - 1, A_CH), f32)
    for grp in range(B_GROUPS):
        wb = min(B_WINDOWS[grp], PAST_LEN)
        out['cache_b_kv%d' % grp] = nrm(ks[5 + grp], (N_EVEN, DEC_BATCH, wb, 2, B_HPG, B_HEAD_DIM), f32)
    out['state_c_conv'] = 0.5 * nrm(ks[8], (N_ODD, DEC_BATCH, C_CONV - 1, C_CH), f32)
    out['rel_bias_table'] = 0.3 * nrm(ks[9], (N_BUCKETS, B_HEADS), f32)
    out['ada_w'] = 0.5 * D_MODEL ** -0.5 * nrm(ks[10], (DEPTH, D_MODEL, 6 * D_MODEL), f32)
    out['ada_b'] = 0.02 * nrm(ks[11], (DEPTH, 6 * D_MODEL), f32)
    out['norm_mix_g'] = 1.0 + 0.1 * nrm(ks[12], (DEPTH, D_MODEL), f32)
    out['norm_ffn_g'] = 1.0 + 0.1 * nrm(ks[13], (DEPTH, D_MODEL), f32)
    out['ffn_w_gate_up'] = D_MODEL ** -0.5 * nrm(ks[14], (DEPTH, D_MODEL, 2 * FFN_HIDDEN), f32)
    out['ffn_w_down'] = FFN_HIDDEN ** -0.5 * nrm(ks[15], (DEPTH, FFN_HIDDEN, D_MODEL), f32)
    out['final_norm_g'] = 1.0 + 0.1 * nrm(ks[16], (D_MODEL,), f32)
    out['e_w_in'] = D_MODEL ** -0.5 * nrm(ks[17], (N_EVEN, D_MODEL, E_IN), f32)
    out['a_conv_w'] = A_CONV ** -0.5 * nrm(ks[18], (N_EVEN, A_CONV, A_CH), f32)
    out['a_conv_b'] = 0.02 * nrm(ks[19], (N_EVEN, A_CH), f32)
    out['a_ln_g'] = 1.0 + 0.1 * nrm(ks[20], (N_EVEN, A_CH), f32)
    out['a_ln_b'] = 0.02 * nrm(ks[21], (N_EVEN, A_CH), f32)
    out['e_w_out'] = E_OUT_IN ** -0.5 * nrm(ks[22], (N_EVEN, E_OUT_IN, D_MODEL), f32)
    out['o_w_in'] = D_MODEL ** -0.5 * nrm(ks[23], (N_ODD, D_MODEL, O_IN), f32)
    out['c_conv_w'] = C_CONV ** -0.5 * nrm(ks[24], (N_ODD, C_CONV, C_CH), f32)
    out['c_conv_b'] = 0.02 * nrm(ks[25], (N_ODD, C_CH), f32)
    out['d_ln_g'] = 1.0 + 0.1 * nrm(ks[26], (N_ODD, D_CH), f32)
    out['d_ln_b'] = 0.02 * nrm(ks[27], (N_ODD, D_CH), f32)
    out['d_spatial_w'] = D_CHUNK ** -0.5 * nrm(ks[28], (N_ODD, D_GROUPS, D_CHUNK, D_CHUNK), f32)
    out['d_spatial_b'] = 1.0 + 0.1 * nrm(ks[29], (N_ODD, D_GROUPS, D_CHUNK), f32)
    out['o_w_out'] = O_OUT_IN ** -0.5 * nrm(ks[30], (N_ODD, O_OUT_IN, D_MODEL), f32)
    return out

def reference(x_prompt, x_sample, c_prompt, c_sample, state_a_conv, cache_b_kv0, cache_b_kv1, cache_b_kv2,
              state_c_conv, rel_bias_table, ada_w, ada_b, norm_mix_g, norm_ffn_g, ffn_w_gate_up, ffn_w_down,
              final_norm_g, e_w_in, a_conv_w, a_conv_b, a_ln_g, a_ln_b, e_w_out, o_w_in, c_conv_w, c_conv_b,
              d_ln_g, d_ln_b, d_spatial_w, d_spatial_b, o_w_out):
    P = {'rel_bias_table': rel_bias_table, 'ada_w': ada_w, 'ada_b': ada_b, 'norm_mix_g': norm_mix_g,
         'norm_ffn_g': norm_ffn_g, 'ffn_w_gate_up': ffn_w_gate_up, 'ffn_w_down': ffn_w_down,
         'final_norm_g': final_norm_g, 'e_w_in': e_w_in, 'a_conv_w': a_conv_w, 'a_conv_b': a_conv_b,
         'a_ln_g': a_ln_g, 'a_ln_b': a_ln_b, 'e_w_out': e_w_out, 'o_w_in': o_w_in, 'c_conv_w': c_conv_w,
         'c_conv_b': c_conv_b, 'd_ln_g': d_ln_g, 'd_ln_b': d_ln_b, 'd_spatial_w': d_spatial_w,
         'd_spatial_b': d_spatial_b, 'o_w_out': o_w_out}
    y_prompt, a_p, kv_p, c_p, _ = _trunk(x_prompt, c_prompt, P, None, None, None)
    y_sample, a_s, kv_s, c_s, d_s = _trunk(x_sample, c_sample, P, state_a_conv,
                                           [cache_b_kv0, cache_b_kv1, cache_b_kv2], state_c_conv)
    return (y_prompt, y_sample, a_p, a_s, kv_p[0], kv_s[0], kv_p[1], kv_s[1], kv_p[2], kv_s[2],
            c_p, c_s, jnp.stack(d_s))


_drawn_inputs = setup_inputs


def setup_inputs(seed=0):
    import zlib

    import numpy as np

    out = dict(_drawn_inputs(seed))
    spreads = {}
    factors = {'rel_bias_table': 5.427,
     'a_conv_b': 8.0,
     'a_ln_b': 8.0,
     'c_conv_b': 8.0,
     'd_ln_b': 3.028,
     'd_spatial_b': 3.905,
     'a_ln_g': 2.773}
    for name, (base, spread) in spreads.items():
        noise = np.random.default_rng([zlib.crc32(name.encode()), seed]).standard_normal(out[name].shape)
        drawn = base * np.exp(spread * noise) if base else spread * noise
        out[name] = __import__('jax').numpy.asarray(drawn.astype(out[name].dtype))
    for name, factor in factors.items():
        out[name] = (out[name] * factor).astype(out[name].dtype)
    return out
```

```python
from contextlib import ExitStack
from dataclasses import dataclass

import numpy as np

import concourse.bass as bass
from concourse import mybir

F32 = mybir.dt.float32
F32R = mybir.dt.float32r
ALU = mybir.AluOpType
ACT = mybir.ActivationFunctionType
AX_X = mybir.AxisListType.X

P = 128
D_MODEL = 1024
KT = D_MODEL // P
SEQ = 1024
NB, NS = 8, 4
S_TOK = NB * NS
TOK = SEQ + S_TOK
BLK = TOK // 3
LAST = SEQ - 2 * BLK
DILATIONS = (1, 4, 16)
WINDOWS = (128, 512, 2048)
HPG, DH = 4, 64
A_CH, A_CONV = 256, 31
C_CONV = 3
FFN = 2816
GROUPS = FFN // 256
N_BUCKETS, MAX_DISTANCE = 32, 2048
EPS = 1e-6
MASKED = -1e30
REL = 383
EXT_A = A_CONV - 1
EXT_C = C_CONV - 1

V_ADA, V_MIX, V_FFN, V_FIN, V_AW, V_AB, V_ALG, V_ALB, V_CW, V_CB, V_DLG, V_DLB, V_ALL = (
    0, 96, 112, 128, 136, 198, 200, 202, 204, 216, 220, 224, 228)


def t5_bucket(dist):
    n = np.maximum(np.asarray(dist, dtype=np.int64), 0)
    exact = N_BUCKETS // 2
    large = exact + (np.log(np.maximum(n, 1) / exact) / np.log(MAX_DISTANCE / exact)
                     * (N_BUCKETS - exact)).astype(np.int32)
    return np.where(n < exact, n, np.minimum(large, N_BUCKETS - 1)).astype(np.int32)


def shape_constants():
    ident = np.eye(P, dtype=np.float32)
    rel = 255 - np.arange(REL)
    ok = (rel >= 0) & (rel <= P)
    prompt = np.zeros((N_BUCKETS + 1, 3, REL), np.float32)
    for g, d in enumerate(DILATIONS):
        prompt[t5_bucket(rel * d)[ok], g, np.nonzero(ok)[0]] = 1.0
        prompt[N_BUCKETS, g, ~ok] = MASKED
    onehot = np.zeros((N_BUCKETS, 6, 160), np.float32)
    mask = np.zeros((P, 3, 160), np.float32)
    steps = np.zeros((P, NS), np.float32)
    row_b, row_s = np.arange(P) % S_TOK // NS, np.arange(P) % NS
    j = np.arange(P)
    col_b, col_s = np.arange(S_TOK) // NS, np.arange(S_TOK) % NS
    for s in range(NS):
        steps[row_s == s, s] = 1.0
        dist = np.clip(np.concatenate([P + s - j, s - col_s]), 0, P)
        onehot[t5_bucket(dist), s, np.arange(160)] = 1.0
    for g in (1, 2):
        dist = np.concatenate([(P - j) * DILATIONS[g], np.zeros(S_TOK, np.int64)])
        onehot[t5_bucket(dist), 3 + g, np.arange(160)] = 1.0
    mask[:, 0, :P] = np.where(j[None, :] >= row_s[:, None], 0.0, MASKED)
    mask[:, 0, P:] = np.where((col_b[None] == row_b[:, None]) & (col_s[None] <= row_s[:, None]), 0.0, MASKED)
    own = (col_b[None] == row_b[:, None]) & (col_s[None] == row_s[:, None])
    mask[:, 1:, P:] = np.where(own, 0.0, MASKED)[:, None]
    return {"ident": ident, "rel_prompt": prompt, "rel_sample": onehot, "mask_sample": mask, "row_step": steps}


@dataclass(eq=False)
class Item:
    kind: str
    raw: int = None
    unit: int = None
    big: int = None
    misc: int = None
    weights: str = ""
    col: int = 0
    role: str = ""
    layer: int = 0
    gate: int = 0
    src: str = ""
    slot: int = 0
    ready: int = 0
    first: int = None
    g: int = None
    j: int = None
    n: int = 0
    which: object = 0
    nt: int = 0
    taps: tuple = ()
    k: int = 0
    k_tiles: list = None
    vec: int = 0
    c: int = 0
    ext: int = 0
    rel: int = 0
    rels: int = 0
    x: int = 0
    v: int = 0
    new: int = 0
    qk: object = None
    tr: dict = None
    pv: object = None
    kt: int = 0
    rows: int = 0
    tp: int = 0
    tn: int = 0
    tok: int = 0
    out: int = 0


def key_tiles(g, sb):
    return 2 if (g == 0 and sb > 0) or (g == 1 and sb % 2 == 1) else 1


def make_plan():
    n = {"raw": 0, "unit": 0, "big": 0, "misc": 0, "norm": 0}

    def take(what, count=1):
        n[what] += count
        return n[what] - count

    items = []
    ada_next = [0]

    waiting = []

    def load_waiting():
        while waiting:
            waiting.pop(0).raw = take("raw")

    def ada(count):
        for _ in range(count):
            if ada_next[0] < 48:
                items.append(Item("ada", k=ada_next[0], raw=None, misc=take("misc")))
                waiting.append(items[-1])
                ada_next[0] += 1

    def dense(kind, weights, col, **kw):
        items.append(Item(kind, weights=weights, col=col, raw=take("raw"), unit=take("unit"),
                          big=take("big", 2 if kind == "project" else 8), **kw))
        load_waiting()

    items.append(Item("setup", vec=take("misc"), c=take("misc"), ext=take("misc"), rel=take("misc", 12),
                      rels=take("misc", 2), x=take("big", KT)))
    ada(8)
    load_waiting()

    def norm(layer, which):
        items.append(Item("norm", layer=layer, which=which, n=take("norm"), big=take("big")))

    norm(0, 0)
    dense("project", "e_w_in", 1, role="a_gate", first=0)
    ada(4)
    dense("project", "e_w_in", 0, role="a_lin")
    ada(4)
    items.append(Item("a_state", misc=take("misc", 2)))
    tap = 0
    for g in range(3):
        for j, role in enumerate("qkv"):
            dense("project", "e_w_in", 2 + 3 * j + g, role=role, g=g)
            if tap < A_CONV:
                items.append(Item("conv", taps=(tap, min(A_CONV, tap + 4))))
                tap += 4
            ada(4)
        k_tiles = {0: [7], 1: [1, 3, 5, 7], 2: list(range(8))}[g]
        items.append(Item("tokens", g=g, v=take("misc", 8), new=take("misc"), k_tiles=k_tiles,
                          k=take("misc", len(k_tiles))))
        if g == 2:
            items.append(Item("ln", which="a", nt=2, big=take("big", 2)))
        qk, tr, pv = {}, {}, {}
        for i in range(16 + 2):
            if i < 16:
                qk[i] = take("misc")
            if 0 <= i - 1 < 16:
                tr[i - 1] = take("misc")
            if 0 <= i - 2 < 16:
                pv[i - 2] = take("misc")
        items.append(Item("attend", g=g, qk=qk, tr=tr, pv=pv))
    ada(48)
    items.append(Item("x_back"))
    dense("down", "e_w_out", 0, layer=0, gate=2, src="mid", slot=0, ready=1)
    items.append(Item("sample", new=take("misc"), qk=take("big"), kt=take("misc", 8 * 5), rows=take("misc"),
                      tp=take("misc"), tn=take("misc"), pv=take("big")))
    items.append(Item("combine", big=take("big", 2)))
    dense("down", "e_w_out", 1, layer=0, gate=2, src="mid", slot=1, ready=2)
    items.append(Item("gate_sample", layer=0, gate=2))

    def ffn(layer):
        norm(layer, 1)
        items.append(Item("ffn", layer=layer, first=n["norm"] - 1, raw=take("raw", 3 * GROUPS),
                          unit=take("unit", 3 * GROUPS), big=take("big", 12 * GROUPS)))
        items.append(Item("gate_sample", layer=layer, gate=5))

    ffn(0)
    norm(1, 0)
    items.append(Item("c_load"))
    for j in range(2):
        dense("project", "o_w_in", 2 + j, role="c_gate", j=j, **({"first": n["norm"] - 1} if j == 0 else {}))
        items.append(Item("c_state_in", j=j, misc=take("misc")))
        dense("project", "o_w_in", 4 + j, role="c_in", j=j)
        items.append(Item("c_conv", j=j, misc=take("misc", 2)))
        dense("project", "o_w_in", 0 + j, role="c_out", j=j)
    for j in range(2):
        dense("down", "o_w_out", j, layer=1, gate=2, src="mid", slot=j, ready=3 + j)
    for j in range(2):
        dense("project", "o_w_in", 8 + j, role="d_v", j=j)
    items.append(Item("d_load", misc=take("misc")))
    for j in range(2):
        dense("project", "o_w_in", 6 + j, role="d_u", j=j)
        if j == 0:
            items.append(Item("ln", which="d", nt=4, big=take("big", 2)))
    items.append(Item("spatial", tok=take("misc", 9), big=take("big", 4)))
    for j in range(2):
        dense("down", "o_w_out", 2 + j, layer=1, gate=2, src="h", slot=j, ready=5 + j)
    items.append(Item("gate_sample", layer=1, gate=2))
    ffn(1)
    items.append(Item("final", n=take("norm"), big=take("big"), out=take("big", 9)))
    user = {}
    for it in items:
        if it.kind == "ada":
            user[it.raw] = ("misc", it.misc)
        elif it.kind in ("project", "down"):
            user[it.raw] = ("unit", it.unit)
        elif it.kind == "ffn":
            for i in range(3 * GROUPS):
                user[it.raw + i] = ("unit", it.unit + i)
    return items, user, n


def build_trunk(nc: bass.Bass, A: dict, O: dict):
    plan, raw_user, totals = make_plan()
    NRAW = 2

    def align(n):
        return (n + 31) // 32 * 32

    base = (nc.sbuf_base + 31) // 32 * 32
    top = [base]
    TILE4 = TOK * 4

    def region(nbytes):
        top[0] += nbytes
        return top[0] - nbytes

    R_X, R_HH, R_HL = region(KT * TILE4), region(KT * TILE4), region(KT * TILE4)
    R_MH, R_ML = region(4 * TILE4), region(4 * TILE4)
    R_W = region(6 * 8192)
    R_T = region(17152)

    def at(name, off, shape, dt=F32):
        return nc.alloc_sbuf_tensor_at(name, shape, dt, offset=off)[:]

    small = [top[0]]

    def keep(name, shape, dt=F32):
        size = (int(np.prod(shape[1:])) * 4 + 31) // 32 * 32
        small[0] += size
        return at(name, small[0] - size, shape, dt)

    x = at("x", R_X, [P, KT, TOK])
    h_hi = at("h_hi", R_HH, [P, KT, TOK], F32R)
    h_lo = at("h_lo", R_HL, [P, KT, TOK], F32R)
    mid_hi = at("mid_hi", R_MH, [P, 2, 2, TOK], F32R)
    mid_lo = at("mid_lo", R_ML, [P, 2, 2, TOK], F32R)
    w_raw = [at(f"w_raw{s}", R_W + 8192 * s, [P, 2048]) for s in range(NRAW)]
    w_hi = [at(f"w_hi{s}", R_W + 8192 * (2 + s), [P, 2048], F32R) for s in range(2)]
    w_lo = [at(f"w_lo{s}", R_W + 8192 * (4 + s), [P, 2048], F32R) for s in range(2)]
    tmp = at("tmp", R_T, [P, 4, TOK])
    ident = keep("ident_sb", [P, P])
    mean_w = keep("mean_w", [P, P])
    eps = keep("eps", [P, 1])
    vecs = keep("vecs", [P, V_ALL])
    csT = keep("csT", [P, KT, 9])
    mod = keep("mod", [P, 12, KT, 9])
    acc_s = keep("acc_s", [P, KT, S_TOK])
    new_qk = keep("new_qk", [P, 512])
    q_new = at("q_new", small[0] - 2048, [P, 3, 2, S_TOK])
    k_new = at("k_new", small[0] - 2048 + 768, [P, 3, 2, S_TOK])
    cst_out = at("cst_out", small[0] - 2048, [NB * EXT_C, 2, 256])
    v_new = keep("v_new", [P, 2, S_TOK])
    c_pack = keep("c_pack", [P, 2 * NB * EXT_C])
    stage = keep("stage", [P, 512])
    kv_rows = at("kv_rows", small[0] - 2048, [S_TOK, 2, 256])
    cst_rows = at("cst_rows", small[0] - 2048, [NB * EXT_C, 512])
    assert small[0] <= nc.sbuf_usable_end, (small[0], nc.sbuf_usable_end)

    x_tok = at("x_tok", R_MH, [P, 8, D_MODEL])
    xs_tok = at("xs_tok", R_T, [S_TOK, D_MODEL])
    c_rows = at("c_rows", R_T + 4096, [9, D_MODEL])
    st_fm = at("st_fm", small[0] - 2048, [P, 2 * NB * EXT_A])
    st_rows = at("st_rows", R_HH + 22528, [120, 2, A_CH])
    vrow = at("vrow", R_HH, [P, 3, P])
    tab = at("tab", R_HH + 1536, [N_BUCKETS, 12])
    tab_b = at("tab_b", R_HH + 2048, [N_BUCKETS + 1, 12, P])
    oh_p = at("oh_p", R_HH + 8192, [N_BUCKETS + 1, 3, REL])
    oh_s = at("oh_s", R_HH + 12800, [N_BUCKETS, 6, 160])
    mask_s = at("mask_s", R_HH + 16640, [P, 3, 160])
    row_step = at("row_step", R_HH + 18560, [P, NS])
    bias_s0 = at("bias_s0", R_HH + 18592, [P, 3, 160])
    tab_s = at("tab_s", R_HH + 20512, [N_BUCKETS, 3, HPG, S_TOK])
    rel_rep = at("rel_rep", R_HL, [P, 12, 384])

    qkv = at("qkv", R_X, [P, 6, SEQ])
    v_tok = at("v_tok", R_X + 24576, [P, 8, 256])
    conv_a = at("conv_a", R_MH + 2 * TILE4, [P, 2, TOK])
    sig = at("sig", R_ML + 2 * TILE4, [P, 2, TOK])
    st_out = at("st_out", R_ML + 2 * TILE4, [P, 3, 256])
    k_rows = at("k_rows", R_ML + 2 * TILE4, [P, 8, 256])
    sc = at("sc", R_ML + 2 * TILE4, [P, 2, 512])
    pt = at("pt", R_ML + 2 * TILE4 + 4096, [P, 2, 512])
    ext_p = at("ext_p", R_T, [P, 2, EXT_A + SEQ])
    ext_s = at("ext_s", R_T + align(2 * (EXT_A + SEQ) * 4), [P, 2, NB, EXT_A + NS])
    bias = at("bias", R_T + 10624, [P, HPG, 256])
    o_rows = at("o_rows", R_T + 14720, [P, 4, 132])
    cache = at("cache", R_HH, [P, 3, 9, 256])
    kTs = at("kTs", R_HH + 27648, [P, 2, 512])
    q_diag = at("q_diag", R_HH + 31744, [P, 3, 2, 2, S_TOK])
    kv_s = at("kv_s", R_T, [S_TOK, 3, 2, 256])
    bias_s = at("bias_s", R_T + 6144, [P, 3, 160])
    p_s = at("p_s", R_T + 8064, [P, 3, 160])
    pT_s = at("pT_s", R_T + 9984, [P, 3, P])
    pT_n = at("pT_n", R_T + 11520, [S_TOK, 3, P])
    sT_s = at("sT_s", R_T + 13056, [P, 3, P])
    att_s = at("att_s", R_T + 14592, [P, 2, S_TOK])
    den_s = at("den_s", R_T + 14848, [P, 4])
    nat = at("nat", R_HL, [P, 3, 8, 2, 132])
    comb = at("comb", R_HL + 25344, [P, 8, 16, 2])
    cext_p = at("cext_p", R_T + 2 * TILE4, [P, 2, EXT_C + SEQ])
    cext_s = at("cext_s", R_T + 2 * TILE4 + align(2 * (EXT_C + SEQ) * 4), [P, 2, NB, EXT_C + NS])
    u_fm = at("u_fm", R_MH, [P, 4, TOK])
    ln_t = at("ln_t", R_ML, [P, 2, TOK])
    ws_raw = at("ws_raw", R_ML + 2 * TILE4, [P, 4, P])
    wsT = at("wsT", R_ML + 2 * TILE4 + 2048, [P, 4, P])
    wsS = at("wsS", R_ML + 2 * TILE4 + 4096, [S_TOK, 4, S_TOK])
    bs_b = at("bs_b", R_ML + 2 * TILE4 + 4608, [P, 4, P])
    vd_tok = at("vd_tok", R_HH + 4 * TILE4, [P, 8, 512])
    vd_new = at("vd_new", R_HL + 4 * TILE4, [S_TOK, 512])
    nt = at("nt", R_MH, [P, KT, TOK])
    y_rows = at("y_rows", R_HH, [P, 9, D_MODEL])
    assert small[0] <= nc.sbuf_usable_end, (small[0], nc.sbuf_usable_end)

    d_x = nc.dram_tensor("scratch_x", (P, KT * TOK), F32, kind="Internal").ap()
    d_rel = nc.dram_tensor("scratch_rel", (12, P * 384), F32, kind="Internal").ap()
    d_bias = nc.dram_tensor("scratch_bias_s", (P, 480), F32, kind="Internal").ap()
    d_o = nc.dram_tensor("scratch_o", (3, SEQ, 264), F32, kind="Internal").ap()
    d_kv = nc.dram_tensor("scratch_kv", (3, S_TOK, 512), F32, kind="Internal").ap()

    with ExitStack() as ctx:
        ps = ctx.enter_context(nc.psum_tensor("ps", [P, 8, 512], F32))

        def big(t):
            return ps[:, 3 * (t % 2):3 * (t % 2) + 3, :]

        def misc(q):
            return ps[:, 6 + q % 2, :]

        def sem(name):
            return ctx.enter_context(nc.semaphore(name))

        in_loaded, x_loaded, tabs_loaded = sem("in_loaded"), sem("x_loaded"), sem("tabs_loaded")
        raw_loaded = [sem(f"raw_loaded{s}") for s in range(NRAW)]
        w_hi_done, w_lo_done = sem("w_hi_done"), sem("w_lo_done")
        x_done = sem("x_done")
        big_ready, misc_ready = sem("big_ready"), sem("misc_ready")
        big_free = [sem(f"big_free{s}") for s in range(2)]
        misc_free = [sem(f"misc_free{s}") for s in range(2)]
        act_link, dve_link, pool_link = sem("act_link"), sem("dve_link"), sem("pool_link")
        c_silu, consts_made, tab_made, rel_made = sem("c_silu"), sem("consts_made"), sem("tab_made"), sem("rel_made")
        rel_stored, x_stored, x_back = sem("rel_stored"), sem("x_stored"), sem("x_back")
        sq_made, sq_summed, rs_made, xn_made = sem("sq_made"), sem("sq_summed"), sem("rs_made"), sem("xn_made")
        scales_made, aff_made, affs_made = sem("scales_made"), sem("aff_made"), sem("affs_made")
        nhi_made, h_ready = sem("nhi_made"), sem("h_ready")
        ln_sum, ln_sq, ln_sqsum, ln_scaled, ln_out = (
            sem("ln_sum"), sem("ln_sq"), sem("ln_sqsum"), sem("ln_scaled"), sem("ln_out"))
        mixed_hi, mixed_ready = sem("mixed_hi"), sem("mixed_ready")
        hid_hi, hid_lo = sem("hid_hi"), sem("hid_lo")
        st_packed, c_packed = sem("st_packed"), sem("c_packed")
        conv_step, st_stored = sem("conv_step"), sem("st_stored")
        bias_loaded, bias_fixed, k_stored, kv_stored = (
            sem("bias_loaded"), sem("bias_fixed"), sem("k_stored"), sem("kv_stored"))
        qk_half, sc_max, exp_done = sem("qk_half"), sem("sc_max"), sem("exp_done")
        o_stored = [sem(f"o_stored{s}") for s in range(4)]
        smp_loaded, qd_zero, qd_made = sem("smp_loaded"), sem("qd_zero"), sem("qd_made")
        cache_loaded = [sem(f"cache_loaded{s}") for s in range(3)]
        s_max, s_exp, s_norm, v_used = sem("s_max"), sem("s_exp"), sem("s_norm"), sem("v_used")
        nat_loaded, comb_m, comb_e, comb_done = sem("nat_loaded"), sem("comb_m"), sem("comb_e"), sem("comb_done")
        c_loaded, cpad_made, cst_stored, cconv_done = sem("c_loaded"), sem("cpad_made"), sem("cst_stored"), sem("cconv_done")
        d_loaded, wsT_made, wsS_loaded, vd_stored, yd_made = (
            sem("d_loaded"), sem("wsT_made"), sem("wsS_loaded"), sem("vd_stored"), sem("yd_made"))
        y_scaled, y_stored, caches_moved = sem("y_scaled"), sem("y_stored"), sem("caches_moved")

        def big_evacuated(e, t):
            e.wait_ge(big_free[t % 2], t // 2 + 1)

        def misc_evacuated(e, q):
            e.wait_ge(misc_free[q % 2], q // 2 + 1)

        def in_blocks(dst, tile, do):
            do(dst[:, 0:2 * BLK].rearrange("p (b n) -> p b n", b=2), tile[:, 0:2, 0:BLK])
            return do(dst[:, 2 * BLK:TOK], tile[:, 2, 0:BLK])

        def blocks(ap):
            return ap.rearrange("p (b n) -> p b n", b=3)

        unit_raw, unit_big = {}, {}
        for it in plan:
            if it.kind in ("project", "down"):
                unit_raw[it.unit], unit_big[it.unit] = it.raw, it.big
            elif it.kind == "ffn":
                for n in range(3 * GROUPS):
                    unit_raw[it.unit + n] = it.raw + n
                unit_big[it.unit], unit_big[it.unit + 1] = it.big, it.big + 2
                for g in range(1, GROUPS + 1):
                    for n, t in enumerate((0, 2, 4) if g < GROUPS else (0,)):
                        unit_big[it.unit + 3 * g - 1 + n] = it.big + 4 + 12 * (g - 1) + t
        attends = [it for it in plan if it.kind == "attend"]
        dense_items = [it for it in plan if it.kind in ("project", "down")]
        by_role = {(it.role, it.j or it.g or 0): it for it in dense_items if it.kind == "project"}
        K_STORES = (2, 4, 8)
        PAIRS = (GROUPS - 1) // 2

        def steps(i, first, per_turn):
            return first if i is None else i * per_turn + first

        def positions(g, ap):
            return ap.rearrange("p (r n) -> p r n", r=DILATIONS[g])

        def cache_cols(ap, g, a, b, s):
            v = ap.rearrange("p (h t) -> p h t", h=HPG)[:, 2 * a:2 * a + 2, :]
            return v[:, :, NS * b:NS * b + NS] if g == 0 else v[:, :, NS * b + s:NS * b + s + 1]

        CACHE_TILES = [(0, 0)] + [(1, s) for s in range(NS)] + [(2, s) for s in range(NS)]

        state_item = next(it for it in plan if it.kind == "a_state")
        c_in_misc = {it.j: it.misc for it in plan if it.kind == "c_state_in"}
        c_conv_misc = {it.j: it.misc for it in plan if it.kind == "c_conv"}

        def o_stores(step):
            return 16 * sum(2 if n >= 32 else 1 for n in range(step % 4, step + 1, 4))

        block = ctx.enter_context(nc.Block())

        @block.sync
        def _(sp):
            def as_project(w):
                return w.rearrange("p (k n) -> p k n", k=KT)

            def as_down(w):
                return w.rearrange("p (k n) -> p k n", k=2)

            def load_raw(r, view, src):
                if r >= NRAW:
                    kind, number = raw_user[r - NRAW]
                    sp.wait_ge(w_lo_done if kind == "unit" else misc_ready, number + 1)
                sp.dma_start(view(w_raw[r % NRAW]), src).then_inc(raw_loaded[r % NRAW], 16)

            def columns(w, c):
                return w.rearrange("(k p) n -> p k n", p=P)[:, :, 256 * c:256 * c + 256]

            sp.dma_start(ident, A["ident"]).then_inc(in_loaded, 16)
            for set_, names in enumerate((
                    ("ada_b",), ("norm_mix_g", "norm_ffn_g", "final_norm_g"),
                    ("a_conv_w", "a_conv_b", "a_ln_g", "a_ln_b", "c_conv_w", "c_conv_b", "d_ln_g", "d_ln_b"))):
                row = 0
                for name in names:
                    flat = A[name]
                    if len(flat.shape) == 2:
                        flat = flat.rearrange("a b -> (a b)")
                    elif len(flat.shape) == 3:
                        flat = flat.rearrange("a b c -> (a b c)")
                    k = flat.shape[0] // P
                    sp.dma_start(vrow[row:row + k, set_, :], flat.rearrange("(r n) -> r n", n=P)).then_inc(in_loaded, 16)
                    row += k
            sp.dma_start(c_rows[0:1, :], A["c_prompt"]).then_inc(in_loaded, 16)
            sp.dma_start(c_rows[1:9, :], A["c_sample"]).then_inc(in_loaded, 16)
            for n in range(8):
                sp.dma_start(x_tok[:, n, :], A["x_prompt"][0, n * P:(n + 1) * P, :]).then_inc(x_loaded, 16)
            sp.dma_start(xs_tok, A["x_sample"].rearrange("b s d -> (b s) d")).then_inc(x_loaded, 16)

            loads = sorted((it for it in plan if it.raw is not None), key=lambda it: it.raw)
            smp = next(it for it in plan if it.kind == "sample")
            last_before_sample = next(it for it in dense_items if it.weights == "e_w_out" and it.col == 1)
            for it in loads:
                if it.kind == "ada":
                    layer, cb = divmod(it.k, 24)
                    load_raw(it.raw, as_project, columns(A["ada_w"][layer], cb))
                elif it.kind == "project":
                    load_raw(it.raw, as_project, columns(A[it.weights][0], it.col))
                elif it.kind == "down":
                    load_raw(it.raw, as_down, A[it.weights][0][256 * it.col:256 * it.col + 256, :]
                             .rearrange("(k p) n -> p k n", p=P))
                elif it.kind == "ffn":
                    up = A["ffn_w_gate_up"][it.layer].rearrange("(k p) n -> p k n", p=P)
                    down = A["ffn_w_down"][it.layer].rearrange("(k p) n -> p k n", p=P)
                    load_raw(it.raw, as_project, up[:, :, 0:256])
                    load_raw(it.raw + 1, as_project, up[:, :, FFN:FFN + 256])
                    with sp.Fori(0, PAIRS) as i:
                        for n in range(6):
                            r, k = it.raw + 2 + n, n // 3
                            sp.wait_ge(w_lo_done, i * 6 + (it.unit + 3 + n - NRAW))
                            if n % 3 == 2:
                                sp.dma_start(as_down(w_raw[r % NRAW]), down[:, bass.ds(i * 4 + 2 * k, 2), :])\
                                    .then_inc(raw_loaded[r % NRAW], 16)
                            else:
                                col = i * 512 + (256 * (1 + k) + (FFN if n % 3 else 0))
                                sp.dma_start(as_project(w_raw[r % NRAW]), up[:, :, bass.ds(col, 256)])\
                                    .then_inc(raw_loaded[r % NRAW], 16)
                    load_raw(it.raw + 3 * GROUPS - 1, as_down, down[:, 2 * GROUPS - 2:2 * GROUPS, :])
                if it is last_before_sample:
                    sp.wait_ge(big_ready, by_role["v", 2].big + 2)
                    for c in range(2 * NB):
                        kv, b = divmod(c, NB)
                        if 3 <= c < NB + 3:
                            sp.wait_ge(misc_ready, smp.kt + 5 * (c - 3) + 5)
                        elif c >= NB + 3:
                            sp.wait_ge(v_used, c - 3 - NB + 1)
                        rows = [A[f"cache_b_kv{g}"][0, b, :, kv].rearrange("w h e -> w (h e)") for g in range(3)]
                        sp.dma_start(cache[:, c % 3, 0, :], rows[0]).then_inc(cache_loaded[c % 3], 16)
                        sp.dma_start(cache[:, c % 3, 1:5, :], rows[1].rearrange("(j s) e -> j s e", s=4))\
                            .then_inc(cache_loaded[c % 3], 16)
                        sp.dma_start(cache[:, c % 3, 5:9, :], rows[2].rearrange("(j s) e -> j s e", s=16)[:, 0:NS, :])\
                            .then_inc(cache_loaded[c % 3], 16)
            fin = plan[-1]
            for n in range(9):
                big_evacuated(sp, fin.out + n)
                if n < 8:
                    sp.dma_start(O["y_prompt"][0, n * P:(n + 1) * P, :], y_rows[:, n, :]).then_inc(y_stored, 16)
                else:
                    sp.dma_start(O["y_sample"].rearrange("b s d -> (b s) d"), y_rows[0:S_TOK, n, :])\
                        .then_inc(y_stored, 16)
            sp.wait_ge(y_stored, 16 * 9)
            sp.wait_ge(st_stored, 16 * 2)
            sp.wait_ge(kv_stored, 16 * 6)
            sp.wait_ge(k_stored, 16 * K_STORES[2])
            sp.wait_ge(cst_stored, 16 * 4)
            sp.wait_ge(vd_stored, 16)
            sp.wait_ge(caches_moved, 16 * 3 * NB)
            sp.wait_ge(x_stored, 16)
            sp.wait_ge(rel_stored, 32)
            for s in range(4):
                sp.wait_ge(o_stored[s], o_stores(47 - 3 + s))

        @block.scalar
        def _(act):
            link = [0]

            def own(ins):
                link[0] += 1
                ins.then_inc(act_link, 1)
                act.wait_ge(act_link, link[0])

            def split_hi(u, i=None, raw_turn=0):
                r = unit_raw[u]
                act.wait_ge(raw_loaded[r % NRAW], steps(i, 16 * (r // NRAW + 1), 16 * 6 // NRAW))
                if u >= 2:
                    act.wait_ge(big_ready, steps(i, unit_big[u - 1], 24))
                act.activation(w_hi[u % 2], w_raw[r % NRAW], ACT.Copy).then_inc(w_hi_done, 1)

            def evacuate(t, func, dst, i=None, **kw):
                act.wait_ge(big_ready, steps(i, t + 1, 24))
                return act.activation(blocks(dst), big(t)[:, :, 0:BLK], func, **kw).then_inc(big_free[t % 2], 1)

            for it in plan:
                if it.kind == "setup":
                    act.wait_ge(in_loaded, 16 * 15)
                    act.activation(c_rows, c_rows, ACT.Silu).then_inc(c_silu, 1)
                    for k in range(KT):
                        if k % 2 == 0:
                            continue
                        act.wait_ge(big_ready, it.x + k + 1)
                        act.activation(x[:, k, 0:SEQ].rearrange("p (b n) -> p b n", b=2), big(it.x + k)[:, 0:2, :], ACT.Copy)
                        act.activation(x[:, k, SEQ:TOK], big(it.x + k)[:, 2, 0:S_TOK], ACT.Copy)\
                            .then_inc(big_free[(it.x + k) % 2], 1)
                elif it.kind in ("norm", "final"):
                    n = it.n
                    if n == 0:
                        split_hi(0)
                        for k in range(KT):
                            big_evacuated(act, plan[0].x + k)
                    else:
                        act.wait_ge(x_done, n)
                    for k in range(KT):
                        act.activation(tmp[:, 2, :] if k == 0 else nt[:, k, :], x[:, k, :], ACT.Square).then_inc(sq_made, 1)
                    evacuate(it.big, ACT.Sqrt, tmp[:, 3, :], bias=eps[:, 0:1])
                    for k in range(KT):
                        act.wait_ge(xn_made, 8 * n + k + 1)
                        if it.kind == "final":
                            act.activation(nt[:, k, :], nt[:, k, :], ACT.Identity,
                                           scale=vecs[:, V_FIN + k:V_FIN + k + 1]).then_inc(y_scaled, 1)
                            continue
                        c = 6 * it.layer + 3 * it.which
                        if k == 0:
                            act.wait_ge(scales_made, n + 1)
                        act.activation(nt[:, k, 0:SEQ], nt[:, k, 0:SEQ], ACT.Identity, bias=mod[:, c, k, 0:1],
                                       scale=mod[:, c + 1, k, 0:1]).then_inc(aff_made, 1)
                    if it.kind == "final":
                        for m in range(1, 9, 2):
                            t = it.out + m
                            act.wait_ge(big_ready, t + 1)
                            act.activation(y_rows[:, m, :].rearrange("p (b n) -> p b n", b=2), big(t)[:, 0:2, :], ACT.Copy)\
                                .then_inc(big_free[t % 2], 1)
                elif it.kind == "project":
                    if it.unit + 1 in unit_raw:
                        split_hi(it.unit + 1)
                    for m in range(2):
                        t = it.big + m
                        if it.role == "a_gate":
                            evacuate(t, ACT.Sigmoid, sig[:, m, :])
                        elif it.role == "q":
                            d, g = DILATIONS[it.g], it.g
                            if m == 0 and g == 0:
                                act.wait_ge(x_stored, 16)
                            act.wait_ge(big_ready, t + 1)
                            for b, n in enumerate((BLK, BLK, LAST)):
                                act.activation(positions(g, qkv[:, m, :])[:, :, BLK // d * b:BLK // d * b + n // d],
                                               big(t)[:, b, 0:n].rearrange("p (j r) -> p r j", r=d), ACT.Copy, scale=DH ** -0.5)
                            act.activation(q_new[:, g, m, :], big(t)[:, 2, LAST:BLK], ACT.Copy, scale=DH ** -0.5)\
                                .then_inc(big_free[t % 2], 1)
                        elif it.role == "c_gate":
                            if it.j and m == 0:
                                act.wait_ge(mixed_ready, 3)
                            evacuate(t, ACT.Copy, tmp[:, m, :])
                        elif it.role == "d_v":
                            if it.j == 0 and m == 0:
                                act.wait_ge(mixed_ready, 4)
                            evacuate(t, ACT.Gelu_apprx_tanh, tmp[:, 2 * it.j + m, :])
                        elif it.role == "d_u":
                            evacuate(t, ACT.Gelu_apprx_tanh, u_fm[:, 2 * it.j + m, :])
                        elif it.role == "c_out":
                            big_evacuated(act, t)
                            act.activation(mid_hi[:, it.j, m, :], tmp[:, m, :], ACT.Copy).then_inc(mixed_hi, 1)
                elif it.kind == "down":
                    if it.unit + 1 in unit_raw:
                        split_hi(it.unit + 1)
                elif it.kind == "a_state":
                    for m, (n, w) in enumerate(((EXT_A, 256), (120, 512))):
                        act.wait_ge(misc_ready, it.misc + m + 1)
                        act.activation(st_out[0:n, m:m + w // 256, :].rearrange("p a n -> p (a n)"),
                                       misc(it.misc + m)[0:n, 0:w], ACT.Copy).then_inc(misc_free[(it.misc + m) % 2], 1)
                    misc_evacuated(act, it.misc)
                    act.dma_start(O["a_conv_prompt"][0, 0], st_out[0:EXT_A, 0, :]).then_inc(st_stored, 16)
                    misc_evacuated(act, it.misc + 1)
                    act.dma_start(O["a_conv_sample"][0].rearrange("(h b) t c -> (b t) h c", h=2), st_out[0:120, 1:3, :])\
                        .then_inc(st_stored, 16)
                elif it.kind == "tokens":
                    g = it.g
                    if g == 0:
                        act.wait_ge(st_stored, 32)
                    for n in range(len(it.k_tiles)):
                        q = it.k + n
                        act.wait_ge(misc_ready, q + 1)
                        act.activation(k_rows[:, n, :], misc(q)[:, 0:256], ACT.Copy).then_inc(misc_free[q % 2], 1)
                    for q in (it.v + 6, it.v + 7, it.new, it.k + len(it.k_tiles) - 1, it.k + max(0, len(it.k_tiles) - 2)):
                        misc_evacuated(act, q)
                    dst = O[f"kv{g}_prompt"][0, 0].rearrange("t k h e -> t k (h e)")
                    for kv, src in ((0, k_rows), (1, v_tok)):
                        if g == 0:
                            act.dma_start(dst[:, kv, :], src[:, 0 if kv == 0 else 7, :]).then_inc(k_stored, 16)
                        elif g == 1:
                            rows = src[:, 0:4, :] if kv == 0 else src[:, 1:8:2, :]
                            act.dma_start(dst[:, kv, :].rearrange("(i r) c -> i r c", r=4), rows).then_inc(k_stored, 16)
                        else:
                            to = dst[:, kv, :].rearrange("(i n r) c -> r i n c", n=8, r=2)
                            for r in range(2):
                                act.dma_start(to[r], src[64 * r:64 * r + 64, :, :]).then_inc(k_stored, 16)
                    act.dma_start(d_kv[g], kv_rows.rearrange("p k c -> p (k c)")).then_inc(kv_stored, 16)
                    W = WINDOWS[g]
                    act.dma_start(O[f"kv{g}_sample"][0, :, W - NS:W].rearrange("b s k h e -> b s (k h e)"),
                                  kv_rows.rearrange("p k c -> p (k c)")).then_inc(kv_stored, 16)
                elif it.kind == "attend":
                    g = it.g

                    def store(j):
                        step, sb, a = 16 * g + j, j // 2, j % 2
                        misc_evacuated(act, it.pv[j])
                        rows = d_o[g][:, 132 * a:132 * a + 132]
                        src = o_rows[:, step % 4, :]
                        if g == 0:
                            act.dma_start(rows[P * sb:P * sb + P, :], src).then_inc(o_stored[step % 4], 16)
                        elif g == 1:
                            act.dma_start(rows.rearrange("(i r) c -> r i c", r=4)[sb // 2, P * (sb % 2):P * (sb % 2) + P, :],
                                          src).then_inc(o_stored[step % 4], 16)
                        else:
                            for r in range(2):
                                act.dma_start(rows.rearrange("(i r) c -> r i c", r=16)[2 * sb + r], src[64 * r:64 * r + 64, :])\
                                    .then_inc(o_stored[step % 4], 16)

                    for i in range(16 + 3):
                        if 0 <= i - 1 < 16:
                            j = i - 1
                            w = 256 * key_tiles(g, j // 2)
                            act.wait_ge(misc_ready, it.tr[j] + 1)
                            act.activation(pt[:, j % 2, 0:w], misc(it.tr[j])[:, 0:w], ACT.Copy)\
                                .then_inc(misc_free[it.tr[j] % 2], 1)
                        if i < 16:
                            step, nk = 16 * g + i, P * key_tiles(g, i // 2)
                            act.wait_ge(sc_max, step + 1)
                            for h in range(2):
                                o = o_rows[:, step % 4, :]
                                last = act.activation(sc[:, i % 2, h * nk:h * nk + nk], sc[:, i % 2, h * nk:h * nk + nk],
                                                      ACT.Exp, bias=o[:, 130 + h:131 + h], accum_out=o[:, 128 + h:129 + h])
                            last.then_inc(exp_done, 1)
                        if 0 <= i - 3:
                            store(i - 3)
                elif it.kind == "ln":
                    nt_, C, first = it.nt, it.nt * P, 0 if it.which == "a" else 2
                    v, s, q = (conv_a, tmp[:, 0, :], tmp[:, 1, :]) if it.which == "a" else (tmp, ln_t[:, 0, :], ln_t[:, 1, :])
                    big_evacuated(act, it.big)
                    for m in range(nt_):
                        if m >= 2:
                            act.wait_ge(ln_sqsum, (0 if it.which == "a" else 1) + m - 1)
                        act.activation(s if m == 0 else q, v[:, m, :], ACT.Square).then_inc(ln_sq, 1)
                    evacuate(it.big + 1, ACT.Sqrt, q, bias=eps[:, 0:1], scale=float(D_MODEL // C))
                    for m in range(nt_):
                        act.wait_ge(ln_scaled, 2 if it.which == "a" else first + m + 1)
                        G, B = (V_ALG, V_ALB) if it.which == "a" else (V_DLG, V_DLB)
                        if it.which == "a":
                            act.activation(s if m == 0 else q, v[:, m, :], ACT.Silu, bias=vecs[:, B + m:B + m + 1],
                                           scale=vecs[:, G + m:G + m + 1]).then_inc(ln_out, 1)
                            act.wait_ge(ln_out, m + 1)
                            act.activation(mid_hi[:, 0, m, :], s if m == 0 else q, ACT.Copy).then_inc(mixed_hi, 1)
                        else:
                            act.activation(v[:, m, :], v[:, m, :], ACT.Identity, bias=vecs[:, B + m:B + m + 1],
                                           scale=vecs[:, G + m:G + m + 1]).then_inc(ln_out, 1)
                elif it.kind == "sample":
                    for n in range(1, 40, 2):
                        q = it.kt + n
                        act.wait_ge(misc_ready, q + 1)
                        w = P * (2 if n % 5 == 4 else 4)
                        act.activation(kTs[:, n % 2, 0:w], misc(q)[:, 0:w], ACT.Copy).then_inc(misc_free[q % 2], 1)
                    act.wait_ge(s_max, 1)
                    act.activation(p_s, p_s, ACT.Exp, bias=den_s[:, 0:1], accum_out=den_s[:, 1:2]).then_inc(s_exp, 1)
                    act.wait_ge(misc_ready, it.tp + 1)
                    act.activation(pT_s.rearrange("p g r -> p (g r)"), misc(it.tp)[:, 0:384], ACT.Copy)\
                        .then_inc(misc_free[it.tp % 2], 1)
                elif it.kind == "combine":
                    act.wait_ge(comb_m, 1)
                    act.activation(comb[:, 1:4, :, :], comb[:, 1:4, :, :], ACT.Exp).then_inc(comb_e, 1)
                    for a in range(2):
                        t = it.big + a
                        act.wait_ge(big_ready, t + 1)
                        act.activation(mid_hi[:, 1, a, 0:SEQ].rearrange("p (b n) -> p b n", b=2), big(t)[:, 0:2, :], ACT.Copy)
                        if a == 0:
                            big_evacuated(act, plan[plan.index(it) - 1].pv)
                        act.activation(mid_hi[:, 1, a, SEQ:TOK], att_s[:, a, :], ACT.Copy).then_inc(mixed_hi, 1)
                elif it.kind == "ffn":
                    first = 2 * GROUPS * it.layer

                    def hidden(g, t, i, later):
                        for m in range(2):
                            if g:
                                act.wait_ge(hid_lo, steps(i, first + 2 * (g - 1) + m + 1, 4))
                            evacuate(t + m, ACT.Silu, tmp[:, m, :], i)
                        later()
                        for m in range(2):
                            act.wait_ge(big_free[t % 2] if m == 0 else big_free[(t + 1) % 2],
                                        steps(i, (t + 2 + m) // 2 + 1, 12))
                            act.activation(mid_hi[:, g % 2, m, :], tmp[:, m, :], ACT.Copy).then_inc(hid_hi, 1)

                    u = it.unit
                    split_hi(u + 1)
                    hidden(0, it.big, None, lambda: split_hi(u + 2))
                    with act.Fori(0, PAIRS) as i:
                        for k in range(2):
                            v0 = u + 2 + 3 * k
                            split_hi(v0 + 1, i)
                            hidden(1 + k, it.big + 4 + 12 * k, i, lambda: split_hi(v0 + 2, i))
                            split_hi(v0 + 3, i)
                    if u + 3 * GROUPS in unit_raw:
                        split_hi(u + 3 * GROUPS)
                elif it.kind == "c_conv":
                    if it.j:
                        act.wait_ge(cst_stored, 32)
                    for m, n in enumerate((EXT_C, NB * EXT_C)):
                        act.wait_ge(misc_ready, it.misc + m + 1)
                        act.activation(cst_out[0:n, m, :], misc(it.misc + m)[0:n, 0:256], ACT.Copy)\
                            .then_inc(misc_free[(it.misc + m) % 2], 1)
                    misc_evacuated(act, it.misc)
                    act.dma_start(O["c_conv_prompt"][0, 0][:, 256 * it.j:256 * it.j + 256], cst_out[0:EXT_C, 0, :])\
                        .then_inc(cst_stored, 16)
                    misc_evacuated(act, it.misc + 1)
                    act.dma_start(O["c_conv_sample"][0].rearrange("b t c -> (b t) c")[:, 256 * it.j:256 * it.j + 256],
                                  cst_out[:, 1, :]).then_inc(cst_stored, 16)
                elif it.kind == "spatial":
                    for n in range(1, 8, 2):
                        q = it.tok + n
                        act.wait_ge(misc_ready, q + 1)
                        act.activation(vd_tok[:, n, :], misc(q), ACT.Copy).then_inc(misc_free[q % 2], 1)
                    misc_evacuated(act, it.tok + 8)
                    act.dma_start(O["d_v_sample"][0].rearrange("b s c -> (b s) c"), vd_new).then_inc(vd_stored, 16)
                    for g in range(4):
                        act.wait_ge(yd_made, g + 1)
                        act.activation(h_hi[:, g, :], ln_t[:, g % 2, :], ACT.Copy).then_inc(mixed_hi, 1)

        @block.vector
        def _(dve):
            link = [0]

            def own(ins):
                link[0] += 1
                ins.then_inc(dve_link, 1)
                dve.wait_ge(dve_link, link[0])

            ln_adds, x_dones = [0], [0]

            def evacuate_down(t0, layer, gate, i=None):
                for m in range(KT):
                    t, g = t0 + m, mod[:, 6 * layer + gate, m, 0:1]
                    dve.wait_ge(big_ready, steps(i, t + 1, 24))
                    for dst, src in ((x[:, m, 0:2 * BLK].rearrange("p (b n) -> p b n", b=2), big(t)[:, 0:2, 0:BLK]),
                                     (x[:, m, 2 * BLK:SEQ], big(t)[:, 2, 0:LAST])):
                        dve.scalar_tensor_tensor(dst, src, g, dst, ALU.mult, ALU.add)
                    dve.tensor_tensor(acc_s[:, m, :], big(t)[:, 2, LAST:BLK], acc_s[:, m, :], ALU.add)\
                        .then_inc(big_free[t % 2], 1)

            def low(dst, hi, src):
                return dve.tensor_tensor(dst, src, hi.bitcast(F32), ALU.subtract)

            for it in plan:
                if it.kind == "setup":
                    dve.memset(mean_w, 1.0 / D_MODEL)
                    dve.memset(eps, EPS)
                    dve.memset(tab_b[N_BUCKETS:N_BUCKETS + 1, :, :], 1.0)
                    dve.memset(acc_s, 0.0).then_inc(consts_made, 1)
                    dve.wait_ge(misc_ready, it.vec + 1)
                    dve.tensor_copy(vecs, misc(it.vec)[:, 0:V_ALL]).then_inc(misc_free[it.vec % 2], 1)
                    dve.wait_ge(misc_ready, it.c + 1)
                    dve.tensor_copy(csT.rearrange("p k c -> p (k c)"), misc(it.c)[:, 0:9 * KT]).then_inc(misc_free[it.c % 2], 1)
                    dve.wait_ge(tabs_loaded, 16 * 6)
                    dve.wait_ge(misc_ready, it.ext + 1)
                    own(dve.tensor_copy(st_fm, misc(it.ext)[:, 0:2 * NB * EXT_A]))
                    dve.tensor_copy(tab_s, tab.rearrange("k (g h) -> k g h", g=3).unsqueeze(3)
                                    .to_broadcast([N_BUCKETS, 3, HPG, S_TOK])).then_inc(misc_free[it.ext % 2], 1)
                    dve.tensor_copy(tab_b[0:N_BUCKETS], tab.unsqueeze(2).to_broadcast([N_BUCKETS, 12, P])).then_inc(tab_made, 1)
                    for k in range(0, KT, 2):
                        dve.wait_ge(big_ready, it.x + k + 1)
                        dve.tensor_copy(x[:, k, 0:SEQ].rearrange("p (b n) -> p b n", b=2), big(it.x + k)[:, 0:2, :])
                        dve.tensor_copy(x[:, k, SEQ:TOK], big(it.x + k)[:, 2, 0:S_TOK]).then_inc(big_free[(it.x + k) % 2], 1)
                    for n in range(12):
                        q = it.rel + n
                        dve.wait_ge(misc_ready, q + 1)
                        dve.tensor_copy(rel_rep[:, n, 0:REL], misc(q)[:, 0:REL]).then_inc(misc_free[q % 2], 1)
                    for n in range(2):
                        q = it.rels + n
                        dve.wait_ge(misc_ready, q + 1)
                        for s in range(3 * n, min(3 * n + 3, NS)):
                            own(dve.scalar_tensor_tensor(bias_s0[:, 0, :], misc(q)[:, 160 * (s % 3):160 * (s % 3) + 160],
                                                         row_step[:, s:s + 1], mask_s[:, 0, :] if s == 0 else bias_s0[:, 0, :],
                                                         ALU.mult, ALU.add))
                        if n == 1:
                            own(dve.tensor_tensor(bias_s0[:, 1:3, :], misc(q)[:, 160:480].rearrange("p (g n) -> p g n", g=2),
                                                  mask_s[:, 1:3, :], ALU.add))
                        dve.engine_nop().then_inc(misc_free[q % 2], 1)
                elif it.kind == "ada":
                    layer, cb = divmod(it.k, 24)
                    dve.wait_ge(misc_ready, it.misc + 1)
                    col = V_ADA + 48 * layer + 2 * cb
                    dve.tensor_tensor(mod[:, 6 * layer + cb // 4, 2 * (cb % 4):2 * (cb % 4) + 2, :],
                                      misc(it.misc)[:, 0:18].rearrange("p (m c) -> p m c", m=2),
                                      vecs[:, col:col + 2].unsqueeze(2).to_broadcast([P, 2, 9]), ALU.add)\
                        .then_inc(misc_free[it.misc % 2], 1)
                elif it.kind in ("norm", "final"):
                    n, final = it.n, it.kind == "final"
                    total, root = tmp[:, 2, :], tmp[:, 3, :]
                    for k in range(1, KT):
                        dve.wait_ge(sq_made, 8 * n + k + 1)
                        dve.tensor_tensor(total, total, nt[:, k, :], ALU.add).then_inc(sq_summed, 1)
                        dve.wait_ge(sq_summed, 7 * n + k)
                    if not final:
                        c = 6 * it.layer + 3 * it.which + 1
                        g0 = (V_FFN if it.which else V_MIX) + 8 * it.layer
                        ada_last = [a for a in plan if a.kind == "ada" and a.k // 4 == c][-1]
                        misc_evacuated(dve, ada_last.misc)
                        misc_evacuated(dve, ada_last.misc - 1)
                        dve.scalar_tensor_tensor(mod[:, c, :, :], mod[:, c, :, :], 1.0,
                                                 vecs[:, g0:g0 + KT].unsqueeze(2).to_broadcast([P, KT, 9]), ALU.add, ALU.mult)\
                            .then_inc(scales_made, 1)
                    big_evacuated(dve, it.big)
                    dve.reciprocal(total, root).then_inc(rs_made, 1)
                    dve.wait_ge(rs_made, n + 1)
                    if n == 0:
                        for k in range(KT):
                            big_evacuated(dve, plan[0].x + k)
                        dve.wait_ge(rel_stored, 32)

                    def scaled(k):
                        dve.tensor_tensor(nt[:, k, :], x[:, k, :], total, ALU.mult).then_inc(xn_made, 1)

                    if final:
                        for k in range(KT):
                            scaled(k)
                        for m in range(0, 9, 2):
                            t = it.out + m
                            dve.wait_ge(big_ready, t + 1)
                            rows = P if m < 8 else S_TOK
                            dve.tensor_copy(y_rows[0:rows, m, :].rearrange("p (b n) -> p b n", b=2), big(t)[0:rows, 0:2, :])\
                                .then_inc(big_free[t % 2], 1)
                        continue
                    scaled(0)
                    scaled(1)
                    for k in range(KT):
                        dve.wait_ge(aff_made, 8 * n + k + 1)
                        dve.wait_ge(affs_made, 8 * n + k + 1)
                        dve.tensor_copy(h_hi[:, k, :], nt[:, k, :]).then_inc(nhi_made, 1)
                        if k + 2 < KT:
                            scaled(k + 2)
                elif it.kind == "project":
                    for m in range(2):
                        t = it.big + m
                        if it.role in ("a_gate", "q", "c_gate", "d_v", "d_u"):
                            continue
                        dve.wait_ge(big_ready, t + 1)
                        T = big(t)
                        if it.role in ("k", "v"):
                            d, g, place = DILATIONS[it.g], it.g, (2 if it.role == "k" else 4) + m
                            if g == 0 and it.role == "k" and m == 0:
                                dve.wait_ge(x_stored, 16)
                            for b, n in enumerate((BLK, BLK, LAST)):
                                dve.tensor_copy(positions(g, qkv[:, place, :])[:, :, BLK // d * b:BLK // d * b + n // d],
                                                T[:, b, 0:n].rearrange("p (j r) -> p r j", r=d))
                            dve.tensor_copy(k_new[:, g, m, :] if it.role == "k" else v_new[:, m, :], T[:, 2, LAST:BLK])\
                                .then_inc(big_free[t % 2], 1)
                        elif it.role in ("a_lin", "c_in"):
                            if it.role == "a_lin":
                                ep, es, gate, E = ext_p[:, m], ext_s[:, m], sig[:, m, :], EXT_A
                                if m == 0:
                                    own(dve.memset(ext_p[:, :, 0:EXT_A], 0.0))
                                    own(dve.tensor_copy(ext_s[:, :, :, 0:EXT_A],
                                                        st_fm.rearrange("p (m b t) -> p m b t", m=2, b=NB)))
                                big_evacuated(dve, t - 2)
                            else:
                                ep, es, gate, E = cext_p[:, m], cext_s[:, m], tmp[:, m, :], EXT_C
                                big_evacuated(dve, by_role["c_gate", it.j].big + m)
                            dve.tensor_tensor(ep[:, E:E + 2 * BLK].rearrange("p (b n) -> p b n", b=2), T[:, 0:2, 0:BLK],
                                              gate[:, 0:2 * BLK].rearrange("p (b n) -> p b n", b=2), ALU.mult)
                            dve.tensor_tensor(ep[:, E + 2 * BLK:E + SEQ], T[:, 2, 0:LAST], gate[:, 2 * BLK:SEQ], ALU.mult)
                            dve.tensor_tensor(es[:, :, E:E + NS], T[:, 2, LAST:BLK].rearrange("p (b s) -> p b s", b=NB),
                                              gate[:, SEQ:TOK].rearrange("p (b s) -> p b s", b=NB), ALU.mult)\
                                .then_inc(big_free[t % 2], 1)
                        elif it.role == "c_out":
                            if m == 0:
                                dve.wait_ge(cconv_done, 4 * C_CONV * (it.j + 1))
                            dve.tensor_tensor(blocks(tmp[:, m, :]), T[:, :, 0:BLK], blocks(tmp[:, m, :]), ALU.mult)\
                                .then_inc(big_free[t % 2], 1)
                    if it.role == "c_out":
                        for m in range(2):
                            dve.wait_ge(mixed_hi, 4 + 2 * it.j + m + 1)
                            ins = low(mid_lo[:, it.j, m, :], mid_hi[:, it.j, m, :], tmp[:, m, :])
                        ins.then_inc(mixed_ready, 1)
                elif it.kind == "a_state":
                    for m in range(2):
                        big_evacuated(dve, by_role["a_lin", 0].big + m)
                    dve.tensor_copy(st_fm.rearrange("p (m b t) -> p m b t", m=2, b=NB), ext_s[:, :, :, NS:NS + EXT_A])\
                        .then_inc(st_packed, 1)
                elif it.kind in ("conv", "c_conv"):
                    if it.kind == "conv":
                        ep, es, out, done, w0, width, b0 = ext_p, ext_s, conv_a, conv_step, V_AW, 2, V_AB
                        taps, before, col = range(*it.taps), 4 * it.taps[0], 0
                        for s in range(2):
                            big_evacuated(dve, by_role["a_lin", 0].big + s)
                    else:
                        ep, es, out, done, w0, width, b0 = cext_p, cext_s, tmp, cconv_done, V_CW, 4, V_CB
                        taps, before, col = range(C_CONV), 4 * C_CONV * it.j, 2 * it.j
                        for s in range(2):
                            big_evacuated(dve, by_role["c_in", it.j].big + s)
                            misc_evacuated(dve, c_in_misc[it.j])
                        if it.j:
                            misc_evacuated(dve, c_conv_misc[0] + 1)
                        dve.tensor_copy(c_pack.rearrange("p (m b t) -> p m b t", m=2, b=NB), cext_s[:, :, :, NS:NS + EXT_C])\
                            .then_inc(c_packed, 1)
                    for k in taps:
                        for m in range(2):
                            w = vecs[:, w0 + width * k + col + m:w0 + width * k + col + m + 1]
                            for sample in range(2):
                                if sample:
                                    src, dst = es[:, m, :, k:k + NS], out[:, m, SEQ:TOK].rearrange("p (b s) -> p b s", b=NB)
                                else:
                                    src, dst = ep[:, m, k:k + SEQ], out[:, m, 0:SEQ]
                                if k == 0:
                                    ins = dve.tensor_scalar(dst, src, w, vecs[:, b0 + col + m:b0 + col + m + 1], ALU.mult, ALU.add)
                                else:
                                    dve.wait_ge(done, before - 4 + 2 * m + sample + 1)
                                    ins = dve.scalar_tensor_tensor(dst, src, w, dst, ALU.mult, ALU.add)
                                ins.then_inc(done, 1)
                        before += 4
                elif it.kind == "tokens":
                    g = it.g
                    if g:
                        dve.wait_ge(k_stored, 16 * K_STORES[g - 1])
                        dve.wait_ge(kv_stored, 32 * g)
                    for sb in range(8):
                        q = it.v + sb
                        dve.wait_ge(misc_ready, q + 1)
                        dve.tensor_copy(v_tok[:, sb, :], misc(q)[:, 0:256]).then_inc(misc_free[q % 2], 1)
                    dve.wait_ge(misc_ready, it.new + 1)
                    dve.tensor_copy(kv_rows.rearrange("p k c -> p (k c)"), misc(it.new)[0:S_TOK, :])\
                        .then_inc(misc_free[it.new % 2], 1)
                elif it.kind == "attend":
                    g = it.g
                    dve.wait_ge(k_stored, 16 * K_STORES[g])
                    if g == 2:
                        dve.wait_ge(bias_fixed, 1)
                    else:
                        dve.wait_ge(bias_loaded, 16 * (g + 1))
                    for i in range(16 + 2):
                        if i < 16:
                            step, a, n = 16 * g + i, i % 2, key_tiles(g, i // 2)
                            nk, q = P * n, it.qk[i]
                            s = sc[:, i % 2, 0:2 * nk].rearrange("p (h k) -> p h k", h=2)
                            dve.wait_ge(misc_ready, q + 1)
                            ins = dve.tensor_tensor(s, misc(q)[:, 0:2 * nk].rearrange("p (h k) -> p h k", h=2),
                                                    bias[:, 2 * a:2 * a + 2, 256 - nk:256], ALU.add)
                            ins.then_inc(misc_free[q % 2], 1)
                            misc_evacuated(dve, q)
                            if step >= 4:
                                dve.wait_ge(o_stored[step % 4], o_stores(step - 4))
                            dve.tensor_reduce(o_rows[:, step % 4, 130:132], s, AX_X, ALU.max, negate=True).then_inc(sc_max, 1)
                        if i >= 2:
                            step, q = 16 * g + i - 2, it.pv[i - 2]
                            dve.wait_ge(misc_ready, q + 1)
                            dve.tensor_copy(o_rows[:, step % 4, 0:128], misc(q)[:, 0:128]).then_inc(misc_free[q % 2], 1)
                elif it.kind == "ln":
                    C, first = it.nt * P, 0 if it.which == "a" else 2
                    v, s, q = (conv_a, tmp[:, 0, :], tmp[:, 1, :]) if it.which == "a" else (tmp, ln_t[:, 0, :], ln_t[:, 1, :])
                    if it.which == "a":
                        dve.wait_ge(conv_step, 4 * A_CONV)
                        misc_evacuated(dve, state_item.misc)
                        misc_evacuated(dve, state_item.misc + 1)
                    else:
                        for m in range(4):
                            big_evacuated(dve, by_role["d_v", m // 2].big + m % 2)
                    for m in range(1, it.nt):
                        ins = dve.tensor_tensor(s, v[:, 0, :] if m == 1 else s, v[:, m, :], ALU.add)
                        if m < it.nt - 1:
                            own(ins)
                    ins.then_inc(ln_sum, 1)
                    dve.wait_ge(big_ready, it.big + 1)
                    for m in range(it.nt):
                        ins = dve.scalar_tensor_tensor(blocks(v[:, m, :]), big(it.big)[:, :, 0:BLK], -float(D_MODEL // C),
                                                       blocks(v[:, m, :]), ALU.mult, ALU.add)
                    ins.then_inc(big_free[it.big % 2], 1)
                    for m in range(1, it.nt):
                        dve.wait_ge(ln_sq, first + m + 1)
                        dve.tensor_tensor(s, s, q, ALU.add).then_inc(ln_sqsum, 1)
                        ln_adds[0] += 1
                        dve.wait_ge(ln_sqsum, ln_adds[0])
                    big_evacuated(dve, it.big + 1)
                    own(dve.reciprocal(s, q))
                    for m in range(it.nt):
                        dve.tensor_tensor(v[:, m, :], v[:, m, :], s, ALU.mult).then_inc(ln_scaled, 1)
                    if it.which == "a":
                        for m in range(2):
                            dve.wait_ge(mixed_hi, m + 1)
                            ins = low(mid_lo[:, 0, m, :], mid_hi[:, 0, m, :], s if m == 0 else q)
                        ins.then_inc(mixed_ready, 1)
                elif it.kind == "down":
                    if it.weights == "e_w_out" and it.col == 0:
                        dve.wait_ge(x_back, 16)
                    evacuate_down(it.big, it.layer, it.gate)
                elif it.kind == "gate_sample":
                    gate = mod[:, 6 * it.layer + it.gate, :, 1:9].unsqueeze(3).to_broadcast([P, KT, NB, NS])
                    last = plan[plan.index(it) - 1]
                    tail = last.big + (8 if last.kind == "down" else 12 * GROUPS)
                    big_evacuated(dve, tail - 1)
                    big_evacuated(dve, tail - 2)
                    own(dve.tensor_tensor(acc_s.rearrange("p k (b s) -> p k b s", b=NB),
                                          acc_s.rearrange("p k (b s) -> p k b s", b=NB), gate, ALU.mult))
                    dve.tensor_tensor(x[:, :, SEQ:TOK], x[:, :, SEQ:TOK], acc_s, ALU.add).then_inc(x_done, 1)
                    x_dones[0] += 1
                    dve.wait_ge(x_done, x_dones[0])
                    own(dve.memset(acc_s, 0.0))
                elif it.kind == "sample":
                    dve.wait_ge(qd_zero, 1)
                    dve.tensor_copy(q_diag[0:64, :, :, 0, :], q_new[0:64])
                    dve.tensor_copy(q_diag[64:128, :, :, 1, :], q_new[64:128]).then_inc(qd_made, 1)
                    dve.wait_ge(smp_loaded, 16 * 2)
                    dve.wait_ge(misc_ready, it.new + 1)
                    dve.tensor_tensor(p_s[:, :, P:160], misc(it.new)[:, 0:96].rearrange("p (g n) -> p g n", g=3),
                                      bias_s[:, :, P:160], ALU.add).then_inc(misc_free[it.new % 2], 1)
                    for n in range(0, 40, 2):
                        q = it.kt + n
                        dve.wait_ge(misc_ready, q + 1)
                        w = P * (2 if n % 5 == 4 else 4)
                        dve.tensor_copy(kTs[:, n % 2, 0:w], misc(q)[:, 0:w]).then_inc(misc_free[q % 2], 1)
                    dve.wait_ge(big_ready, it.qk + 1)
                    dve.tensor_copy(sT_s.rearrange("p g r -> p (g r)"), big(it.qk)[:, 0, 0:384]).then_inc(big_free[it.qk % 2], 1)
                    dve.wait_ge(misc_ready, it.rows + 1)
                    dve.tensor_tensor(p_s[:, :, 0:P], misc(it.rows)[:, 0:384].rearrange("p (g n) -> p g n", g=3),
                                      bias_s[:, :, 0:P], ALU.add).then_inc(misc_free[it.rows % 2], 1)
                    misc_evacuated(dve, it.new)
                    misc_evacuated(dve, it.rows)
                    dve.tensor_reduce(den_s[:, 0:1], p_s.rearrange("p g n -> p (g n)"), AX_X, ALU.max, negate=True)\
                        .then_inc(s_max, 1)
                    dve.wait_ge(s_exp, 1)
                    own(dve.reciprocal(den_s[:, 2:3], den_s[:, 1:2]))
                    dve.tensor_scalar(p_s, p_s, den_s[:, 2:3], None, ALU.mult).then_inc(s_norm, 1)
                    dve.wait_ge(misc_ready, it.tn + 1)
                    dve.tensor_copy(pT_n.rearrange("p g r -> p (g r)"), misc(it.tn)[0:S_TOK, 0:384])\
                        .then_inc(misc_free[it.tn % 2], 1)
                    dve.wait_ge(big_ready, it.pv + 1)
                    acc = big(it.pv)[:, 0, 0:128].rearrange("p (a h t) -> p a h t", a=2, h=2)
                    dve.tensor_copy(att_s[0:64], acc[0:64, :, 0, :])
                    dve.tensor_copy(att_s[64:128], acc[64:128, :, 1, :]).then_inc(big_free[it.pv % 2], 1)
                elif it.kind == "combine":
                    rows = nat.rearrange("p g n a c -> p g (n a) c")
                    C = comb
                    dve.wait_ge(nat_loaded, 48)
                    own(dve.tensor_tensor(C[:, 0], rows[:, 0, :, 130:132], rows[:, 1, :, 130:132], ALU.min))
                    own(dve.tensor_tensor(C[:, 0], C[:, 0], rows[:, 2, :, 130:132], ALU.min))
                    for g in range(3):
                        ins = dve.tensor_tensor(C[:, 1 + g], C[:, 0], rows[:, g, :, 130:132], ALU.subtract)
                    ins.then_inc(comb_m, 1)
                    dve.wait_ge(comb_e, 1)
                    for g in range(3):
                        ins = dve.tensor_tensor(C[:, 4 + g], C[:, 1 + g], rows[:, g, :, 128:130], ALU.mult)
                    own(ins)
                    own(dve.tensor_tensor(C[:, 4], C[:, 4], C[:, 5], ALU.add))
                    own(dve.tensor_tensor(C[:, 4], C[:, 4], C[:, 6], ALU.add))
                    own(dve.reciprocal(C[:, 7], C[:, 4]))
                    for g in range(3):
                        ins = dve.tensor_tensor(C[:, 1 + g], C[:, 1 + g], C[:, 7], ALU.mult)
                    own(ins)
                    O_ = [rows[:, g, :, 0:128].rearrange("p n (h d) -> p n h d", h=2) for g in range(3)]
                    for g in range(3):
                        ins = dve.tensor_tensor(O_[g], O_[g], C[:, 1 + g].unsqueeze(3).to_broadcast([P, 16, 2, DH]), ALU.mult)
                    own(ins)
                    own(dve.tensor_tensor(O_[0], O_[0], O_[1], ALU.add))
                    dve.tensor_tensor(O_[0], O_[0], O_[2], ALU.add).then_inc(comb_done, 1)
                    for a in range(2):
                        t = it.big + a
                        dve.wait_ge(mixed_hi, 3 + a)
                        dve.tensor_tensor(mid_lo[:, 1, a, 0:SEQ].rearrange("p (b n) -> p b n", b=2), big(t)[:, 0:2, :],
                                          mid_hi[:, 1, a, 0:SEQ].rearrange("p (b n) -> p b n", b=2).bitcast(F32), ALU.subtract)\
                            .then_inc(big_free[t % 2], 1)
                        ins = low(mid_lo[:, 1, a, SEQ:TOK], mid_hi[:, 1, a, SEQ:TOK], att_s[:, a, :])
                    ins.then_inc(mixed_ready, 1)
                elif it.kind == "ffn":
                    first = 2 * GROUPS * it.layer

                    def hidden(g, t, i):
                        for m in range(2):
                            dve.wait_ge(big_ready, steps(i, t + m + 1, 24))
                            dve.wait_ge(big_free[t % 2 if m == 0 else (t + 1) % 2], steps(i, (t - 2 + m) // 2 + 1, 12))
                            dve.tensor_tensor(blocks(tmp[:, m, :]), big(t + m)[:, :, 0:BLK], blocks(tmp[:, m, :]), ALU.mult)\
                                .then_inc(big_free[(t + m) % 2], 1)
                        for m in range(2):
                            dve.wait_ge(hid_hi, steps(i, first + 2 * g + m + 1, 4))
                            low(mid_lo[:, g % 2, m, :], mid_hi[:, g % 2, m, :], tmp[:, m, :]).then_inc(hid_lo, 1)

                    hidden(0, it.big + 2, None)
                    with dve.Fori(0, PAIRS) as i:
                        for k in range(2):
                            t = it.big + 4 + 12 * k
                            hidden(1 + k, t + 2, i)
                            evacuate_down(t + 4, it.layer, 5, i)
                    evacuate_down(it.big + 4 + 24 * PAIRS, it.layer, 5)
                elif it.kind == "c_load":
                    dve.memset(cext_p[:, :, 0:EXT_C], 0.0).then_inc(cpad_made, 1)
                    dve.wait_ge(cpad_made, 1)
                elif it.kind == "c_state_in":
                    dve.wait_ge(misc_ready, it.misc + 1)
                    if it.j:
                        misc_evacuated(dve, c_conv_misc[0])
                        misc_evacuated(dve, c_conv_misc[0] + 1)
                    dve.tensor_copy(cext_s[:, :, :, 0:EXT_C],
                                    misc(it.misc)[:, 0:2 * NB * EXT_C].rearrange("p (m b t) -> p m b t", m=2, b=NB))\
                        .then_inc(misc_free[it.misc % 2], 1)
                elif it.kind == "d_load":
                    dve.wait_ge(misc_ready, it.misc + 1)
                    dve.tensor_copy(wsT.rearrange("p g n -> p (g n)"), misc(it.misc)).then_inc(misc_free[it.misc % 2], 1)
                elif it.kind == "spatial":
                    for n in range(0, 9, 2):
                        q = it.tok + n
                        dve.wait_ge(misc_ready, q + 1)
                        if n < 8:
                            dve.tensor_copy(vd_tok[:, n, :], misc(q)).then_inc(misc_free[q % 2], 1)
                        else:
                            dve.tensor_copy(vd_new, misc(q)[0:S_TOK, :]).then_inc(misc_free[q % 2], 1)

                    def mixed(g):
                        t, y = it.big + g, ln_t[:, g % 2, :]
                        dve.wait_ge(big_ready, t + 1)
                        dve.tensor_tensor(y[:, 0:SEQ].rearrange("p (n i) -> p n i", i=P),
                                          big(t)[:, 0:2, :].rearrange("p b (n i) -> p (b n) i", i=P),
                                          bs_b[:, g, :].unsqueeze(1).to_broadcast([P, 8, P]), ALU.add)
                        dve.tensor_tensor(y[:, SEQ:TOK].rearrange("p (b s) -> p b s", b=NB),
                                          big(t)[:, 2, 0:S_TOK].rearrange("p (b s) -> p b s", b=NB),
                                          bs_b[:, g, 0:NS].unsqueeze(1).to_broadcast([P, NB, NS]), ALU.add)\
                            .then_inc(big_free[t % 2], 1)
                        big_evacuated(dve, t)
                        dve.tensor_tensor(y, y, u_fm[:, g, :], ALU.mult).then_inc(yd_made, 1)

                    def mixed_lo(g):
                        dve.wait_ge(mixed_hi, 8 + g + 1)
                        dve.wait_ge(yd_made, g + 1)
                        ins = low(h_lo[:, g, :], h_hi[:, g, :], ln_t[:, g % 2, :])
                        if g % 2:
                            ins.then_inc(mixed_ready, 1)
                        else:
                            own(ins)

                    dve.wait_ge(d_loaded, 32)
                    for s in range(2):
                        for m in range(2):
                            big_evacuated(dve, by_role["d_u", s].big + m)
                    mixed(0)
                    for g in range(1, 4):
                        if g >= 2:
                            if (g - 2) % 2:
                                dve.wait_ge(mixed_ready, 5)
                        mixed(g)
                        mixed_lo(g - 1)
                    mixed_lo(3)

        @block.gpsimd
        def _(pool):
            link = [0]

            def own(ins):
                link[0] += 1
                ins.then_inc(pool_link, 1)
                pool.wait_ge(pool_link, link[0])

            splits = [0]

            def split_lo(u, i=None):
                pool.wait_ge(w_hi_done, steps(i, u + 1, 6))
                pool.tensor_tensor(w_lo[u % 2], w_raw[unit_raw[u] % NRAW], w_hi[u % 2].bitcast(F32), ALU.subtract)\
                    .then_inc(w_lo_done, 1)
                splits[0] = u + 1

            def splits_done():
                pool.wait_ge(w_lo_done, splits[0])

            def move_caches(b):
                for g in range(3):
                    W = WINDOWS[g]
                    src = A[f"cache_b_kv{g}"][0, b, NS:W].rearrange("w k h e -> (w k h e)")
                    dst = O[f"kv{g}_sample"][0, b, 0:W - NS].rearrange("w k h e -> (w k h e)")
                    pool.dma_start(dst.rearrange("(n c) -> n c", c=2048), src.rearrange("(n c) -> n c", c=2048))\
                        .then_inc(caches_moved, 16)

            moved = [0]
            for it in plan:
                if it.kind == "setup":
                    pool.dma_start(tab, A["rel_bias_table"]).then_inc(tabs_loaded, 16)
                    pool.dma_start(oh_p, A["rel_prompt"]).then_inc(tabs_loaded, 16)
                    pool.dma_start(oh_s, A["rel_sample"]).then_inc(tabs_loaded, 16)
                    pool.dma_start(mask_s, A["mask_sample"]).then_inc(tabs_loaded, 16)
                    pool.dma_start(row_step, A["row_step"]).then_inc(tabs_loaded, 16)
                    pool.dma_start(st_rows, A["state_a_conv"][0].rearrange("(h b) t c -> (b t) h c", h=2))\
                        .then_inc(tabs_loaded, 16)
                    for k in range(KT):
                        big_evacuated(pool, it.x + k)
                    pool.dma_start(d_x, x.rearrange("p k n -> p (k n)")).then_inc(x_stored, 16)
                    misc_evacuated(pool, it.rel + 11)
                    misc_evacuated(pool, it.rel + 10)
                    pool.dma_start(d_rel.rearrange("g (p n) -> p g n", n=384)[:, :, 0:REL], rel_rep[:, :, 0:REL])\
                        .then_inc(rel_stored, 16)
                    misc_evacuated(pool, it.rels + 1)
                    misc_evacuated(pool, it.rels)
                    pool.dma_start(d_bias, bias_s0.rearrange("p g n -> p (g n)")).then_inc(rel_stored, 16)
                elif it.kind == "norm":
                    n, c = it.n, 6 * it.layer + 3 * it.which
                    if n == 0:
                        split_lo(0)
                        pool.wait_ge(rel_stored, 32)
                    if n == 3:
                        pool.wait_ge(vd_stored, 16)
                    pool.wait_ge(scales_made, n + 1)
                    for k in range(KT + 1):
                        if k < KT:
                            s = nt[:, k, SEQ:TOK].rearrange("p (b s) -> p b s", b=NB)
                            pool.wait_ge(xn_made, 8 * n + k + 1)
                            own(pool.tensor_tensor(s, s, mod[:, c + 1, k, 1:9].unsqueeze(2).to_broadcast([P, NB, NS]), ALU.mult))
                            pool.tensor_tensor(s, s, mod[:, c, k, 1:9].unsqueeze(2).to_broadcast([P, NB, NS]), ALU.add)\
                                .then_inc(affs_made, 1)
                        if k:
                            pool.wait_ge(nhi_made, 8 * n + k)
                            pool.tensor_tensor(h_lo[:, k - 1, :], nt[:, k - 1, :], h_hi[:, k - 1, :].bitcast(F32),
                                               ALU.subtract).then_inc(h_ready, 1)
                elif it.kind in ("project", "down"):
                    if it.unit + 1 in unit_raw:
                        split_lo(it.unit + 1)
                    if it.kind == "project" and it.weights == "o_w_in" and moved[0] < NB:
                        move_caches(moved[0])
                        moved[0] += 1
                elif it.kind == "tokens":
                    g = it.g
                    if g:
                        pool.wait_ge(sc_max, 16 * g)
                    else:
                        pool.wait_ge(rel_stored, 32)
                    src = d_rel[HPG * g:HPG * g + HPG, 0:P * REL].rearrange("h (p n) -> p h n", n=REL)[:, :, 127:REL]
                    pool.dma_start(bias, src).then_inc(bias_loaded, 16)
                    if g == 2:
                        pool.wait_ge(bias_loaded, 48)
                        splits_done()
                        pool.memset(bias[64:128, :, 128:192], MASKED).then_inc(bias_fixed, 1)
                elif it.kind == "x_back":
                    last = attends[-1]
                    misc_evacuated(pool, last.pv[15])
                    misc_evacuated(pool, last.pv[14])
                    pool.wait_ge(x_stored, 16)
                    pool.wait_ge(k_stored, 16 * K_STORES[2])
                    pool.dma_start(x.rearrange("p k n -> p (k n)"), d_x).then_inc(x_back, 16)
                elif it.kind == "sample":
                    pool.wait_ge(big_ready, by_role["v", 2].big + 2)
                    splits_done()
                    pool.memset(q_diag, 0.0).then_inc(qd_zero, 1)
                    for s in range(4):
                        pool.wait_ge(o_stored[s], o_stores(44 + s))
                    for g in range(3):
                        pool.dma_start(nat[:, g].rearrange("p n a c -> p n (a c)"),
                                       d_o[g].rearrange("(n p) c -> p n c", p=P)).then_inc(nat_loaded, 16)
                    pool.wait_ge(mixed_ready, 1)
                    pool.wait_ge(kv_stored, 16 * 6)
                    pool.dma_start(kv_s.rearrange("p g k c -> p g (k c)"), d_kv.rearrange("g t c -> t g c")).then_inc(smp_loaded, 16)
                    pool.dma_start(bias_s.rearrange("p g n -> p (g n)"), d_bias).then_inc(smp_loaded, 16)
                elif it.kind == "ffn":
                    u = it.unit
                    split_lo(u + 1)
                    split_lo(u + 2)
                    with pool.Fori(0, PAIRS) as i:
                        for n in range(6):
                            split_lo(u + 3 + n, i)
                    if u + 3 * GROUPS in unit_raw:
                        split_lo(u + 3 * GROUPS)
                elif it.kind == "c_load":
                    pool.dma_start(cst_rows, A["state_c_conv"][0].rearrange("b t c -> (b t) c")).then_inc(c_loaded, 16)
                elif it.kind == "d_load":
                    pool.wait_ge(big_ready, by_role["d_v", 0].big + 1)
                    pool.dma_start(ws_raw, A["d_spatial_w"][0].rearrange("g i j -> i g j")).then_inc(d_loaded, 16)
                    pool.dma_start(bs_b.rearrange("p g n -> p (g n)"),
                                   A["d_spatial_b"].rearrange("a g n -> a (g n)").to_broadcast([P, 512])).then_inc(d_loaded, 16)
                    misc_evacuated(pool, it.misc)
                    pool.affine_select(out=wsT, in_=wsT, compare_op=ALU.is_ge, fill=0.0, base=0,
                                       pattern=[[0, 4], [1, P]], channel_multiplier=-1).then_inc(wsT_made, 1)
                    pool.wait_ge(wsT_made, 1)
                    own(pool.memset(wsS, 0.0))
                    for b in range(NB):
                        pool.dma_start(wsS[NS * b:NS * b + NS, :, NS * b:NS * b + NS], wsT[0:NS, :, 0:NS]).then_inc(wsS_loaded, 16)

        @block.tensor
        def _(pe):
            def big_slot(t, i=None):
                if t >= 2:
                    pe.wait_ge(big_free[t % 2], steps(i, t // 2, 12))

            def misc_slot(q):
                if q >= 2:
                    pe.wait_ge(misc_free[q % 2], q // 2)

            def dense_tile(t, K, w, x_hi, x_lo, i=None, ready=None):
                big_slot(t, i)
                for k in range(K):
                    if ready is not None:
                        ready(k)
                    for n, (wt, xt) in enumerate(((w(w_hi_s, k), x_hi), (w(w_hi_s, k), x_lo), (w(w_lo_s, k), x_hi))):
                        for b in range(3):
                            mm = pe.matmul(big(t)[:, b, 0:BLK], wt, xt[:, k, b * BLK:b * BLK + BLK],
                                           start=(k == 0 and n == 0), stop=(k == K - 1 and n == 2))
                mm.then_inc(big_ready, 1)

            w_hi_s, w_lo_s = 0, 1

            def project(u, t, i=None, first=None):
                pe.wait_ge(w_lo_done, steps(i, u + 1, 6))
                halves = [w[u % 2].rearrange("p (k n) -> p k n", k=KT) for w in (w_hi, w_lo)]
                for m in range(2):
                    dense_tile(t + m, KT, lambda s, k: halves[s][:, k, m * P:m * P + P], h_hi, h_lo, i,
                               (lambda k: pe.wait_ge(h_ready, 8 * first + k + 1)) if first is not None and m == 0 else None)

            def down(u, t, x_hi, x_lo, i=None):
                pe.wait_ge(w_lo_done, steps(i, u + 1, 6))
                halves = [w[u % 2].rearrange("p (k n) -> p k n", k=2) for w in (w_hi, w_lo)]
                for m in range(KT):
                    dense_tile(t + m, 2, lambda s, k: halves[s][:, k, m * P:m * P + P], x_hi, x_lo, i)

            def mean(t, src):
                big_slot(t)
                for b in range(3):
                    mm = pe.matmul(big(t)[:, b, 0:BLK], mean_w, src[:, b * BLK:b * BLK + BLK], start=True, stop=True)
                mm.then_inc(big_ready, 1)

            for it in plan:
                if it.kind == "setup":
                    pe.wait_ge(in_loaded, 16 * 15)
                    pe.wait_ge(consts_made, 1)
                    col = 0
                    for set_, n in enumerate((V_MIX, V_AW - V_MIX, V_ALL - V_AW)):
                        mm = pe.transpose(misc(it.vec)[:, col:col + n], vrow[0:n, set_, :], ident[0:n, 0:n])
                        col += n
                    mm.then_inc(misc_ready, 1)
                    pe.wait_ge(c_silu, 1)
                    for k in range(KT):
                        mm = pe.transpose(misc(it.c)[:, 9 * k:9 * k + 9], c_rows[0:9, k * P:k * P + P], ident[0:9, 0:9])
                    mm.then_inc(misc_ready, 1)
                    pe.wait_ge(tabs_loaded, 16 * 6)
                    misc_slot(it.ext)
                    for m in range(2):
                        for half in range(2):
                            at_ = 240 * m + 120 * half
                            mm = pe.transpose(misc(it.ext)[:, at_:at_ + 120], st_rows[0:120, half, m * P:m * P + P],
                                              ident[0:120, 0:120])
                    mm.then_inc(misc_ready, 1)
                    pe.wait_ge(x_loaded, 16 * 9)
                    for k in range(KT):
                        t = it.x + k
                        big_slot(t)
                        for n in range(8):
                            pe.transpose(big(t)[:, n // 4, (n % 4) * P:(n % 4) * P + P], x_tok[:, n, k * P:k * P + P], ident)
                        pe.transpose(big(t)[:, 2, 0:S_TOK], xs_tok[:, k * P:k * P + P], ident[0:S_TOK, 0:S_TOK])\
                            .then_inc(big_ready, 1)
                    pe.wait_ge(tab_made, 1)
                    for n in range(12):
                        q = it.rel + n
                        misc_slot(q)
                        pe.matmul(misc(q)[:, 0:REL], tab_b[:, n, :], oh_p[:, n // HPG, :], start=True, stop=True)\
                            .then_inc(misc_ready, 1)
                    for n in range(2):
                        q = it.rels + n
                        misc_slot(q)
                        for s in range(3):
                            mm = pe.matmul(misc(q)[:, 160 * s:160 * s + 160],
                                           tab_s[:, max(0, 3 * n + s - 3)].rearrange("k h t -> k (h t)"),
                                           oh_s[:, 3 * n + s, :], start=True, stop=True)
                        mm.then_inc(misc_ready, 1)
                elif it.kind == "ada":
                    r = it.raw
                    pe.wait_ge(raw_loaded[r % NRAW], 16 * (r // NRAW + 1))
                    misc_slot(it.misc)
                    w = w_raw[r % NRAW].rearrange("p (k n) -> p k n", k=KT)
                    for m in range(2):
                        for k in range(KT):
                            mm = pe.matmul(misc(it.misc)[:, 9 * m:9 * m + 9], w[:, k, m * P:m * P + P], csT[:, k, :],
                                           start=(k == 0), stop=(k == KT - 1))
                    mm.then_inc(misc_ready, 1)
                elif it.kind in ("norm", "final"):
                    pe.wait_ge(sq_summed, 7 * (it.n + 1))
                    mean(it.big, tmp[:, 2, :])
                    if it.kind == "final":
                        pe.wait_ge(y_scaled, KT)
                        for n in range(9):
                            t, rows = it.out + n, P if n < 8 else S_TOK
                            big_slot(t)
                            for k in range(KT):
                                mm = pe.transpose(big(t)[0:rows, k // 4, (k % 4) * P:(k % 4) * P + P],
                                                  nt[:, k, n * P:n * P + rows], ident)
                            mm.then_inc(big_ready, 1)
                elif it.kind == "project":
                    project(it.unit, it.big, first=it.first)
                elif it.kind == "down":
                    pe.wait_ge(mixed_ready, it.ready)
                    if it.src == "mid":
                        down(it.unit, it.big, mid_hi[:, it.slot], mid_lo[:, it.slot])
                    else:
                        down(it.unit, it.big, h_hi[:, 2 * it.slot:2 * it.slot + 2, :], h_lo[:, 2 * it.slot:2 * it.slot + 2, :])
                elif it.kind == "a_state":
                    for s in range(2):
                        big_evacuated(pe, by_role["a_lin", 0].big + s)
                    misc_slot(it.misc)
                    for m in range(2):
                        mm = pe.transpose(misc(it.misc)[0:EXT_A, m * P:m * P + P], ext_p[:, m, SEQ:SEQ + EXT_A], ident)
                    mm.then_inc(misc_ready, 1)
                    pe.wait_ge(st_packed, 1)
                    misc_slot(it.misc + 1)
                    for half in range(2):
                        for m in range(2):
                            at_ = 256 * half + P * m
                            mm = pe.transpose(misc(it.misc + 1)[0:120, at_:at_ + P],
                                              st_fm[:, 240 * m + 120 * half:240 * m + 120 * half + 120], ident)
                    mm.then_inc(misc_ready, 1)
                elif it.kind == "tokens":
                    g = it.g
                    for role in "qkv":
                        for s in range(2):
                            big_evacuated(pe, by_role[role, g].big + s)
                    for sb in range(8):
                        misc_slot(it.v + sb)
                        for m in range(2):
                            mm = pe.transpose(misc(it.v + sb)[:, m * P:m * P + P], qkv[:, 4 + m, sb * P:sb * P + P], ident)
                        mm.then_inc(misc_ready, 1)
                    misc_slot(it.new)
                    for m in range(2):
                        pe.transpose(misc(it.new)[0:S_TOK, m * P:m * P + P], k_new[:, g, m, :], ident)
                        mm = pe.transpose(misc(it.new)[0:S_TOK, 256 + m * P:256 + m * P + P], v_new[:, m, :], ident)
                    mm.then_inc(misc_ready, 1)
                    for n, sb in enumerate(it.k_tiles):
                        misc_slot(it.k + n)
                        for m in range(2):
                            mm = pe.transpose(misc(it.k + n)[:, m * P:m * P + P], qkv[:, 2 + m, sb * P:sb * P + P], ident)
                        mm.then_inc(misc_ready, 1)
                elif it.kind == "attend":
                    g = it.g
                    for i in range(16 + 2):
                        if i < 16:
                            sb, a, n, q = i // 2, i % 2, key_tiles(g, i // 2), it.qk[i]
                            misc_slot(q)
                            for h in range(2):
                                at_ = slice(64 * h, 64 * h + 64)
                                if h:
                                    mm.then_inc(qk_half, 1)
                                    pe.wait_ge(qk_half, 16 * g + i + 1)
                                mm = pe.matmul(misc(q)[:, h * n * P:(h + 1) * n * P], qkv[at_, a, P * sb:P * sb + P],
                                               qkv[at_, 2 + a, P * (sb + 1 - n):P * (sb + 1)], start=True, stop=True)
                            mm.then_inc(misc_ready, 1)
                        if 0 <= i - 1 < 16:
                            j, n, q = i - 1, key_tiles(g, (i - 1) // 2), it.tr[i - 1]
                            pe.wait_ge(exp_done, 16 * g + j + 1)
                            misc_slot(q)
                            for c in range(2 * n):
                                mm = pe.transpose(misc(q)[:, c * P:c * P + P], sc[:, j % 2, c * P:c * P + P], ident)
                            mm.then_inc(misc_ready, 1)
                        if i >= 2:
                            j, n, q = i - 2, key_tiles(g, (i - 2) // 2), it.pv[i - 2]
                            sb, a = j // 2, j % 2
                            misc_evacuated(pe, it.tr[j])
                            misc_slot(q)
                            for h in range(2):
                                for c in range(n):
                                    mm = pe.matmul(misc(q)[:, h * DH:h * DH + DH], pt[:, j % 2, (h * n + c) * P:(h * n + c) * P + P],
                                                   v_tok[:, sb + 1 - n + c, (2 * a + h) * DH:(2 * a + h + 1) * DH],
                                                   start=(c == 0), stop=(c == n - 1))
                            mm.then_inc(misc_ready, 1)
                elif it.kind == "ln":
                    s = tmp[:, 0, :] if it.which == "a" else ln_t[:, 0, :]
                    pe.wait_ge(ln_sum, 1 if it.which == "a" else 2)
                    mean(it.big, s)
                    pe.wait_ge(ln_sqsum, 1 if it.which == "a" else 4)
                    mean(it.big + 1, s)
                elif it.kind == "sample":
                    misc_slot(it.new)
                    for h in (0, 2, 1, 3):
                        if h == 1:
                            mm.then_inc(qk_half, 1)
                            pe.wait_ge(qk_half, 16 * 3 + 1)
                        for g in range(3):
                            at_ = slice(64 * (h % 2), 64 * (h % 2) + 64)
                            mm = pe.matmul(misc(it.new)[32 * h:32 * h + 32, 32 * g:32 * g + 32], q_new[at_, g, h // 2, :],
                                           k_new[at_, g, h // 2, :], start=True, stop=True)
                    mm.then_inc(misc_ready, 1)
                    pe.wait_ge(qd_made, 1)
                    big_slot(it.qk)
                    scores = big(it.qk)[:, 0, 0:384].rearrange("p (g r) -> p g r", g=3)
                    for n in range(41):
                        if n < 40:
                            b, c = divmod(n, 5)
                            if c == 0:
                                pe.wait_ge(cache_loaded[b % 3], 48 * (b // 3 + 1))
                            misc_slot(it.kt + n)
                            for j in range(2 if c == 4 else 4):
                                mm = pe.transpose(misc(it.kt + n)[:, j * P:j * P + P],
                                                  cache[:, b % 3, 2 * c + j // 2, (j % 2) * P:(j % 2) * P + P], ident)
                            mm.then_inc(misc_ready, 1)
                        if n >= 1:
                            b, c = divmod(n - 1, 5)
                            misc_evacuated(pe, it.kt + n - 1)
                            for j in range(2 if c == 4 else 4):
                                g, s = CACHE_TILES[2 * c + j // 2]
                                mm = pe.matmul(cache_cols(scores[:, g], g, j % 2, b, s),
                                               kTs[:, (n - 1) % 2, j * P:j * P + P],
                                               q_diag[:, g, j % 2, :, NS * b:NS * b + NS] if g == 0 else
                                               q_diag[:, g, j % 2, :, NS * b + s:NS * b + s + 1], start=True, stop=True)
                    mm.then_inc(big_ready, 1)
                    big_evacuated(pe, it.qk)
                    misc_slot(it.rows)
                    for g in range(3):
                        mm = pe.transpose(misc(it.rows)[:, g * P:g * P + P], sT_s[:, g, :], ident)
                    mm.then_inc(misc_ready, 1)
                    pe.wait_ge(s_norm, 1)
                    misc_slot(it.tp)
                    for g in range(3):
                        mm = pe.transpose(misc(it.tp)[:, g * P:g * P + P], p_s[:, g, 0:P], ident)
                    mm.then_inc(misc_ready, 1)
                    misc_slot(it.tn)
                    for g in range(3):
                        mm = pe.transpose(misc(it.tn)[0:S_TOK, g * P:g * P + P], p_s[:, g, P:160], ident)
                    mm.then_inc(misc_ready, 1)
                    big_slot(it.pv)
                    acc = big(it.pv)[:, 0, 0:128].rearrange("p (a r) -> p a r", a=2)
                    pe.wait_ge(smp_loaded, 32)
                    misc_evacuated(pe, it.tp)
                    misc_evacuated(pe, it.tn)
                    for a in range(2):
                        for g in range(3):
                            pe.matmul(acc[:, a, :], kv_s[:, g, 1, a * P:a * P + P], pT_n[:, g, 64 * a:64 * a + 64],
                                      start=(a == 0 and g == 0), stop=False, skip_group_check=True)
                    for b in range(NB):
                        c = NB + b
                        pe.wait_ge(cache_loaded[c % 3], 48 * (c // 3 + 1))
                        for tile, (g, s) in enumerate(CACHE_TILES):
                            for a in range(2):
                                out = acc[:, a, :].rearrange("p (h t) -> p h t", h=2)
                                out = out[:, :, NS * b:NS * b + NS] if g == 0 else out[:, :, NS * b + s:NS * b + s + 1]
                                last = b == NB - 1 and tile == 8 and a == 1
                                mm = pe.matmul(out, cache[:, c % 3, tile, a * P:a * P + P], cache_cols(pT_s[:, g], g, a, b, s),
                                               start=False, stop=last, skip_group_check=True)
                        if b < NB - 1:
                            mm.then_inc(v_used, 1)
                    mm.then_inc(big_ready, 1)
                elif it.kind == "combine":
                    pe.wait_ge(comb_done, 1)
                    for a in range(2):
                        big_slot(it.big + a)
                        for n in range(8):
                            mm = pe.transpose(big(it.big + a)[:, n // 4, (n % 4) * P:(n % 4) * P + P], nat[:, 0, n, a, 0:P], ident)
                        mm.then_inc(big_ready, 1)
                elif it.kind == "ffn":
                    first, u = 2 * GROUPS * it.layer, it.unit
                    project(u, it.big, first=it.first)
                    project(u + 1, it.big + 2)
                    with pe.Fori(0, PAIRS) as i:
                        for k in range(2):
                            t = it.big + 4 + 12 * k
                            project(u + 2 + 3 * k, t, i)
                            project(u + 3 + 3 * k, t + 2, i)
                            pe.wait_ge(hid_lo, steps(i, first + 2 * k + 2, 4))
                            down(u + 4 + 3 * k, t + 4, mid_hi[:, k], mid_lo[:, k], i)
                    pe.wait_ge(hid_lo, first + 2 * GROUPS)
                    down(u + 3 * GROUPS - 1, it.big + 4 + 24 * PAIRS, mid_hi[:, 0], mid_lo[:, 0])
                elif it.kind == "c_state_in":
                    pe.wait_ge(c_loaded, 16)
                    misc_slot(it.misc)
                    for m in range(2):
                        mm = pe.transpose(misc(it.misc)[:, 16 * m:16 * m + 16],
                                          cst_rows[:, 256 * it.j + P * m:256 * it.j + P * m + P], ident[0:16, 0:16])
                    mm.then_inc(misc_ready, 1)
                elif it.kind == "c_conv":
                    for s in range(2):
                        big_evacuated(pe, by_role["c_in", it.j].big + s)
                    misc_slot(it.misc)
                    for m in range(2):
                        mm = pe.transpose(misc(it.misc)[0:EXT_C, m * P:m * P + P], cext_p[:, m, SEQ:SEQ + EXT_C], ident)
                    mm.then_inc(misc_ready, 1)
                    pe.wait_ge(c_packed, it.j + 1)
                    misc_slot(it.misc + 1)
                    for m in range(2):
                        mm = pe.transpose(misc(it.misc + 1)[0:16, m * P:m * P + P], c_pack[:, 16 * m:16 * m + 16], ident)
                    mm.then_inc(misc_ready, 1)
                elif it.kind == "d_load":
                    pe.wait_ge(d_loaded, 32)
                    misc_slot(it.misc)
                    for g in range(4):
                        mm = pe.transpose(misc(it.misc)[:, g * P:g * P + P], ws_raw[:, g, :], ident)
                    mm.then_inc(misc_ready, 1)
                elif it.kind == "spatial":
                    pe.wait_ge(ln_out, 2 + 4)
                    for n in range(9):
                        q, rows = it.tok + n, P if n < 8 else S_TOK
                        misc_slot(q)
                        for g in range(4):
                            mm = pe.transpose(misc(q)[0:rows, g * P:g * P + P], tmp[:, g, n * P:n * P + rows], ident)
                        mm.then_inc(misc_ready, 1)
                    misc_evacuated(pe, it.tok + 7)
                    misc_evacuated(pe, it.tok + 8)
                    pe.wait_ge(wsT_made, 1)
                    pe.wait_ge(wsS_loaded, 16 * NB)
                    for g in range(4):
                        t = it.big + g
                        big_slot(t)
                        for n in range(8):
                            pe.matmul(big(t)[:, n // 4, (n % 4) * P:(n % 4) * P + P], vd_tok[:, n, g * P:g * P + P],
                                      wsT[:, g, :], start=True, stop=True)
                        pe.matmul(big(t)[:, 2, 0:S_TOK], vd_new[:, g * P:g * P + P], wsS[:, g, :], start=True, stop=True)\
                            .then_inc(big_ready, 1)


_OUTS = [("y_prompt", (1, 1024, 1024)), ("y_sample", (8, 4, 1024)), ("a_conv_prompt", (1, 1, 30, 256)),
         ("a_conv_sample", (1, 8, 30, 256)), ("kv0_prompt", (1, 1, 128, 2, 4, 64)), ("kv0_sample", (1, 8, 128, 2, 4, 64)),
         ("kv1_prompt", (1, 1, 512, 2, 4, 64)), ("kv1_sample", (1, 8, 512, 2, 4, 64)),
         ("kv2_prompt", (1, 1, 1024, 2, 4, 64)), ("kv2_sample", (1, 8, 2048, 2, 4, 64)),
         ("c_conv_prompt", (1, 1, 2, 512)), ("c_conv_sample", (1, 8, 2, 512)), ("d_v_sample", (1, 8, 4, 512))]


def kernel(**inputs):
    import concourse.bacc as bacc
    from concourse.bass_utils import run_bass_kernel_spmd

    nc = bacc.Bacc("TRN2", target_bir_lowering=False, num_devices=1)
    arrays, A, O = {}, {}, {}
    for name, a in {**inputs, **shape_constants()}.items():
        a = np.ascontiguousarray(a)
        arrays[f"in_{name}"] = a
        A[name] = nc.dram_tensor(f"in_{name}", a.shape, mybir.dt.from_np(a.dtype), kind="ExternalInput").ap()
    for name, shape in _OUTS:
        O[name] = nc.dram_tensor(f"out_{name}", shape, F32, kind="ExternalOutput").ap()
    build_trunk(nc, A, O)
    r = run_bass_kernel_spmd(nc, [arrays], core_ids=[0])
    return tuple(r.results[0][f"out_{name}"] for name, _ in _OUTS)
```

```python
from contextlib import ExitStack
from dataclasses import dataclass

import numpy as np

import concourse.bass as bass
from concourse import mybir

F32 = mybir.dt.float32
F32R = mybir.dt.float32r
ALU = mybir.AluOpType
ACT = mybir.ActivationFunctionType
AX_X = mybir.AxisListType.X

P = 128
D_MODEL = 1024
KT = D_MODEL // P
SEQ = 1024
NB, NS = 8, 4
S_TOK = NB * NS
TOK = SEQ + S_TOK
BLK = TOK // 3
LAST = SEQ - 2 * BLK
DILATIONS = (1, 4, 16)
WINDOWS = (128, 512, 2048)
HPG, DH = 4, 64
A_CH, A_CONV = 256, 31
C_CONV = 3
FFN = 2816
GROUPS = FFN // 256
N_BUCKETS, MAX_DISTANCE = 32, 2048
EPS = 1e-6
MASKED = -1e30
REL = 383
EXT_A = A_CONV - 1
EXT_C = C_CONV - 1
ADA_UNITS = 2 * 6 * D_MODEL // 256

V_ADA, V_MIX, V_FFN, V_FIN, V_AW, V_AB, V_ALG, V_ALB, V_CW, V_CB, V_DLG, V_DLB, V_ALL = (
    0, 96, 112, 128, 136, 198, 200, 202, 204, 216, 220, 224, 228)


def t5_bucket(dist):
    n = np.maximum(np.asarray(dist, dtype=np.int64), 0)
    exact = N_BUCKETS // 2
    large = exact + (np.log(np.maximum(n, 1) / exact) / np.log(MAX_DISTANCE / exact)
                     * (N_BUCKETS - exact)).astype(np.int32)
    return np.where(n < exact, n, np.minimum(large, N_BUCKETS - 1)).astype(np.int32)


def shape_constants():
    ident = np.eye(P, dtype=np.float32)
    rel = 255 - np.arange(REL)
    ok = (rel >= 0) & (rel <= P)
    prompt = np.zeros((N_BUCKETS + 1, 3, REL), np.float32)
    for g, d in enumerate(DILATIONS):
        prompt[t5_bucket(rel * d)[ok], g, np.nonzero(ok)[0]] = 1.0
        prompt[N_BUCKETS, g, ~ok] = MASKED
    onehot = np.zeros((N_BUCKETS, 6, 160), np.float32)
    mask = np.zeros((P, 3, 160), np.float32)
    steps = np.zeros((P, NS), np.float32)
    row_b, row_s = np.arange(P) % S_TOK // NS, np.arange(P) % NS
    j = np.arange(P)
    col_b, col_s = np.arange(S_TOK) // NS, np.arange(S_TOK) % NS
    for s in range(NS):
        steps[row_s == s, s] = 1.0
        dist = np.clip(np.concatenate([P + s - j, s - col_s]), 0, P)
        onehot[t5_bucket(dist), s, np.arange(160)] = 1.0
    for g in (1, 2):
        dist = np.concatenate([(P - j) * DILATIONS[g], np.zeros(S_TOK, np.int64)])
        onehot[t5_bucket(dist), 3 + g, np.arange(160)] = 1.0
    mask[:, 0, :P] = np.where(j[None, :] >= row_s[:, None], 0.0, MASKED)
    mask[:, 0, P:] = np.where((col_b[None] == row_b[:, None]) & (col_s[None] <= row_s[:, None]), 0.0, MASKED)
    own = (col_b[None] == row_b[:, None]) & (col_s[None] == row_s[:, None])
    mask[:, 1:, P:] = np.where(own, 0.0, MASKED)[:, None]
    return {"ident": ident, "rel_prompt": prompt, "rel_sample": onehot, "mask_sample": mask, "row_step": steps,
            "pair_sum": np.tile(np.eye(9, dtype=np.float32), (2, 1))}


@dataclass(eq=False)
class Item:
    kind: str
    unit: int = None
    big: int = None
    misc: int = None
    weights: str = ""
    col: int = 0
    role: str = ""
    layer: int = 0
    gate: int = 0
    src: str = ""
    slot: int = 0
    ready: int = 0
    first: int = None
    g: int = None
    i: int = 0
    j: int = None
    n: int = 0
    which: object = 0
    nt: int = 0
    taps: tuple = ()
    k: int = 0
    k_tiles: list = None
    vec: int = 0
    c: int = 0
    ext: int = 0
    rel: int = 0
    rels: int = 0
    x: int = 0
    v: int = 0
    new: int = 0
    qk: object = None
    tr: dict = None
    pv: object = None
    kt: int = 0
    rows: int = 0
    tp: int = 0
    tn: int = 0
    tok: int = 0
    out: int = 0


def key_tiles(g, sb):
    return 2 if (g == 0 and sb > 0) or (g == 1 and sb % 2 == 1) else 1


def make_plan():
    n = {"unit": 0, "big": 0, "misc": 0, "norm": 0}

    def take(what, count=1):
        n[what] += count
        return n[what] - count

    items = []
    ada_units, ada_open = [], []

    def ada_out():
        while ada_open:
            items.append(Item("ada_out", k=ada_open.pop().k, misc=take("misc")))

    def ada():
        ada_out()
        if len(ada_units) < ADA_UNITS:
            ada_units.append(Item("ada", k=len(ada_units), unit=take("unit"), misc=take("misc")))
            ada_open.append(ada_units[-1])
            items.append(ada_units[-1])

    def dense(kind, weights, col, **kw):
        items.append(Item(kind, weights=weights, col=col, unit=take("unit"),
                          big=take("big", 2 if kind == "project" else 8), **kw))

    items.append(Item("setup", vec=take("misc"), c=take("misc"), ext=take("misc")))
    for k in range(KT):
        ada()
        items.append(Item("x_in", k=k, x=take("big")))
    ada_out()
    items.append(Item("rel", rel=take("misc", 12), rels=take("misc", 2)))

    def norm(layer, which):
        items.append(Item("norm", layer=layer, which=which, n=take("norm"), big=take("big")))

    norm(0, 0)
    dense("project", "e_w_in", 1, role="a_gate", first=0)
    dense("project", "e_w_in", 0, role="a_lin")
    items.append(Item("a_state", misc=take("misc", 2)))
    tap = 0
    for g in range(3):
        for j, role in enumerate("qkv"):
            if g == 2 and role == "v":
                items.append(Item("ln_sum", which="a", nt=2))
            dense("project", "e_w_in", 2 + 3 * j + g, role=role, g=g)
            if tap < A_CONV and role != "v":
                last_tap = min(A_CONV, tap + (6 if role == "q" else 5))
                items.append(Item("conv", taps=(tap, last_tap)))
                tap = last_tap
        if g == 2:
            items.append(Item("ln_mean", which="a", nt=2, big=take("big")))
        k_tiles = {0: [7], 1: [1, 3, 5, 7], 2: list(range(8))}[g]
        items.append(Item("tokens", g=g, v=take("misc", 8), new=take("misc"), k_tiles=k_tiles,
                          k=take("misc", len(k_tiles))))
        if g == 2:
            items.append(Item("ln_var", which="a", nt=2, big=take("big")))
        qk, tr, pv = {}, {}, {}
        for i in range(16 + 3):
            if i % 4 != 3 and i < 18:
                ada()
            if i < 16:
                qk[i] = take("misc")
            if 0 <= i - 1 < 16:
                tr[i - 1] = take("misc")
            if 0 <= i - 2 < 16:
                pv[i - 2] = take("misc")
            items.append(Item("attend", g=g, i=i, qk=qk, tr=tr, pv=pv))
    while len(ada_units) < ADA_UNITS:
        ada()
    ada_out()
    items.append(Item("x_back"))
    items.append(Item("sample", new=take("misc"), qk=take("big"), kt=take("misc", 8 * 5), rows=take("misc"),
                      tp=take("misc"), tn=take("misc"), pv=take("big")))
    dense("down", "e_w_out", 0, layer=0, gate=2, src="mid", slot=0, ready=1)
    items.append(Item("combine", big=take("big", 2)))
    dense("down", "e_w_out", 1, layer=0, gate=2, src="mid", slot=1, ready=2)
    items.append(Item("gate_sample", layer=0, gate=2))

    def ffn(layer):
        norm(layer, 1)
        items.append(Item("ffn", layer=layer, first=n["norm"] - 1,
                          unit=take("unit", 3 * GROUPS), big=take("big", 12 * GROUPS)))
        items.append(Item("gate_sample", layer=layer, gate=5))

    ffn(0)
    norm(1, 0)
    items.append(Item("c_load"))
    for j in range(2):
        dense("project", "o_w_in", 2 + j, role="c_gate", j=j, **({"first": n["norm"] - 1} if j == 0 else {}))
        items.append(Item("c_state_in", j=j, misc=take("misc")))
        dense("project", "o_w_in", 4 + j, role="c_in", j=j)
        items.append(Item("c_conv", j=j, misc=take("misc", 2)))
        dense("project", "o_w_in", 0 + j, role="c_out", j=j)
    for j in range(2):
        dense("project", "o_w_in", 8 + j, role="d_v", j=j)
    dense("down", "o_w_out", 0, layer=1, gate=2, src="mid", slot=0, ready=3)
    items.append(Item("ln_sum", which="d", nt=4))
    dense("down", "o_w_out", 1, layer=1, gate=2, src="mid", slot=1, ready=4)
    items.append(Item("ln_mean", which="d", nt=4, big=take("big")))
    dense("project", "o_w_in", 6, role="d_u", j=0)
    items.append(Item("d_load", misc=take("misc")))
    items.append(Item("ln_var", which="d", nt=4, big=take("big")))
    dense("project", "o_w_in", 7, role="d_u", j=1)
    items.append(Item("spatial", tok=take("misc", 9), big=take("big", 4)))
    for j in range(2):
        dense("down", "o_w_out", 2 + j, layer=1, gate=2, src="h", slot=j, ready=5 + j)
    items.append(Item("gate_sample", layer=1, gate=2))
    ffn(1)
    items.append(Item("final", n=take("norm"), big=take("big"), out=take("big", 9)))
    return items


def build_trunk(nc: bass.Bass, A: dict, O: dict):
    plan = make_plan()
    NRAW = 2

    def align(n):
        return (n + 31) // 32 * 32

    base = (nc.sbuf_base + 31) // 32 * 32
    top = [base]
    TILE4 = TOK * 4

    def region(nbytes):
        top[0] += nbytes
        return top[0] - nbytes

    R_X, R_HH, R_HL = region(KT * TILE4), region(KT * TILE4), region(KT * TILE4)
    R_MH, R_ML = region(4 * TILE4), region(4 * TILE4)
    R_W = region(6 * 8192)
    R_T = region(KT * TILE4 // 2)

    def at(name, off, shape, dt=F32):
        return nc.alloc_sbuf_tensor_at(name, shape, dt, offset=off)[:]

    small = [top[0]]

    def keep(name, shape, dt=F32):
        size = (int(np.prod(shape[1:])) * 4 + 31) // 32 * 32
        small[0] += size
        return at(name, small[0] - size, shape, dt)

    x = at("x", R_X, [P, KT, TOK])
    h_hi = at("h_hi", R_HH, [P, KT, TOK], F32R)
    h_lo = at("h_lo", R_HL, [P, KT, TOK], F32R)
    mid_hi = at("mid_hi", R_MH, [P, 2, 2, TOK], F32R)
    mid_lo = at("mid_lo", R_ML, [P, 2, 2, TOK], F32R)
    w_raw = [at(f"w_raw{s}", R_W + 8192 * s, [P, 2048]) for s in range(NRAW)]
    w_hi = [at(f"w_hi{s}", R_W + 8192 * (2 + s), [P, 2048], F32R) for s in range(2)]
    w_lo = [at(f"w_lo{s}", R_W + 8192 * (4 + s), [P, 2048], F32R) for s in range(2)]
    tmp = at("tmp", R_T, [P, 4, TOK])
    ident = keep("ident_sb", [P, P])
    mean_w = keep("mean_w", [P, P])
    eps = keep("eps", [P, 1])
    pair_sum = keep("pair_sum_sb", [18, 9])
    vecs = keep("vecs", [P, V_ALL])
    cs = keep("cs", [P, KT, 2, 9], F32R)
    small_cs = small[0] - 576
    mod = keep("mod", [P, 12, KT, 9])
    acc_s = keep("acc_s", [P, KT, S_TOK])
    new_qk = keep("new_qk", [P, 512])
    q_new = at("q_new", small[0] - 2048, [P, 3, 2, S_TOK])
    k_new = at("k_new", small[0] - 2048 + 768, [P, 3, 2, S_TOK])
    cst_out = at("cst_out", small[0] - 2048, [NB * EXT_C, 2, 256])
    v_new = keep("v_new", [P, 2, S_TOK])
    c_pack = keep("c_pack", [P, 2 * NB * EXT_C])
    stage = keep("stage", [P, 512])
    kv_rows = at("kv_rows", small[0] - 2048, [S_TOK, 2, 256])
    cst_rows = at("cst_rows", small[0] - 2048, [NB * EXT_C, 512])
    assert small[0] <= nc.sbuf_usable_end, (small[0], nc.sbuf_usable_end)

    x_tok = at("x_tok", R_MH, [P, 8, D_MODEL])
    xs_tok = at("xs_tok", R_T, [S_TOK, D_MODEL])
    c_rows = at("c_rows", R_T + 4096, [9, D_MODEL])
    st_fm = at("st_fm", small[0] - 2048, [P, 2 * NB * EXT_A])
    st_rows = at("st_rows", R_HH + 22528, [120, 2, A_CH])
    vrow = at("vrow", R_HH, [P, 3, P])
    tab = at("tab", R_HH + 1536, [N_BUCKETS, 12])
    tab_b = at("tab_b", R_HH + 2048, [N_BUCKETS + 1, 12, P])
    oh_p = at("oh_p", R_HH + 8192, [N_BUCKETS + 1, 3, REL])
    oh_s = at("oh_s", R_HH + 12800, [N_BUCKETS, 6, 160])
    mask_s = at("mask_s", R_HH + 16640, [P, 3, 160])
    row_step = at("row_step", R_HH + 18560, [P, NS])
    bias_s0 = at("bias_s0", R_HH + 18592, [P, 3, 160])
    tab_s = at("tab_s", R_HH + 20512, [N_BUCKETS, 3, HPG, S_TOK])
    ada_rows = [at("ada_rows0", R_HH + 25600, [18, 256]), at("ada_rows1", R_X + 32768, [18, 256])]
    sq_first = at("sq_first", R_HL + 18432, [P, TOK])
    rel_rep = at("rel_rep", R_HL, [P, 12, 384])

    qkv = at("qkv", R_X, [P, 6, SEQ])
    v_tok = at("v_tok", R_X + 24576, [P, 8, 256])
    conv_a = at("conv_a", R_MH + 2 * TILE4, [P, 2, TOK])
    sig = at("sig", R_ML + 2 * TILE4, [P, 2, TOK])
    st_out = at("st_out", R_ML + 2 * TILE4, [P, 3, 256])
    k_rows = at("k_rows", R_ML + 2 * TILE4, [P, 8, 256])
    sc = at("sc", R_ML + 2 * TILE4, [P, 2, 512])
    pt = at("pt", R_ML + 2 * TILE4 + 4096, [P, 2, 512])
    ext_p = at("ext_p", R_T, [P, 2, EXT_A + SEQ])
    ext_s = at("ext_s", R_T + align(2 * (EXT_A + SEQ) * 4), [P, 2, NB, EXT_A + NS])
    bias = at("bias", R_T + 10624, [P, HPG, 256])
    o_rows = at("o_rows", R_T + 14720, [P, 4, 132])
    cache = at("cache", R_HH, [P, 3, 9, 256])
    kTs = at("kTs", R_HH + 27648, [P, 2, 512])
    q_diag = at("q_diag", R_HH + 31744, [P, 3, 2, 2, S_TOK])
    kv_s = at("kv_s", R_T, [S_TOK, 3, 2, 256])
    bias_s = at("bias_s", R_T + 6144, [P, 3, 160])
    p_s = at("p_s", R_T + 8064, [P, 3, 160])
    pT_s = at("pT_s", R_T + 9984, [P, 3, P])
    pT_n = at("pT_n", R_T + 11520, [S_TOK, 3, P])
    sT_s = at("sT_s", R_T + 13056, [P, 3, P])
    att_s = at("att_s", R_T + 14592, [P, 2, S_TOK])
    den_s = at("den_s", R_T + 14848, [P, 4])
    nat = at("nat", R_HL, [P, 3, 8, 2, 132])
    comb = at("comb", R_HL + 25344, [P, 8, 16, 2])
    cext_p = at("cext_p", R_T + 2 * TILE4, [P, 2, EXT_C + SEQ])
    cext_s = at("cext_s", small_cs, [P, 2, NB, EXT_C + NS])
    u_fm = at("u_fm", R_MH, [P, 4, TOK])
    ln_t = at("ln_t", R_ML, [P, 2, TOK])
    ws_raw = at("ws_raw", R_ML + 2 * TILE4, [P, 4, P])
    wsT = at("wsT", R_ML + 2 * TILE4 + 2048, [P, 4, P])
    wsS = at("wsS", R_ML + 2 * TILE4 + 4096, [S_TOK, 4, S_TOK])
    bs_b = at("bs_b", R_ML + 2 * TILE4 + 4608, [P, 4, P])
    vd_tok = at("vd_tok", R_HH + 4 * TILE4, [P, 8, 512])
    vd_new = at("vd_new", R_HL + 4 * TILE4, [S_TOK, 512])
    nt = at("nt", R_MH, [P, KT, TOK])
    y_rows = at("y_rows", R_HH, [P, 9, D_MODEL])
    assert small[0] <= nc.sbuf_usable_end, (small[0], nc.sbuf_usable_end)

    d_x = nc.dram_tensor("scratch_x", (P, KT * TOK), F32, kind="Internal").ap()
    d_rel = nc.dram_tensor("scratch_rel", (12, P * 384), F32, kind="Internal").ap()
    d_bias = nc.dram_tensor("scratch_bias_s", (P, 480), F32, kind="Internal").ap()
    d_o = nc.dram_tensor("scratch_o", (3, SEQ, 264), F32, kind="Internal").ap()
    d_kv = nc.dram_tensor("scratch_kv", (3, S_TOK, 512), F32, kind="Internal").ap()

    with ExitStack() as ctx:
        ps = ctx.enter_context(nc.psum_tensor("ps", [P, 8, 512], F32))

        def big(t):
            return ps[:, 3 * (t % 2):3 * (t % 2) + 3, :]

        def misc(q):
            return ps[:, 6 + q % 2, :]

        def sem(name):
            return ctx.enter_context(nc.semaphore(name))

        in_loaded, x_loaded, tabs_loaded = sem("in_loaded"), sem("x_loaded"), sem("tabs_loaded")
        raw_loaded = [sem(f"raw_loaded{s}") for s in range(NRAW)]
        w_hi_done, w_lo_done = sem("w_hi_done"), sem("w_lo_done")
        w_lo_half = sem("w_lo_half")
        x_done = sem("x_done")
        big_ready, misc_ready = sem("big_ready"), sem("misc_ready")
        big_free = [sem(f"big_free{s}") for s in range(2)]
        misc_free = [sem(f"misc_free{s}") for s in range(2)]
        act_link, dve_link, pool_link = sem("act_link"), sem("dve_link"), sem("pool_link")
        c_silu, consts_made, tab_made, rel_made = sem("c_silu"), sem("consts_made"), sem("tab_made"), sem("rel_made")
        rel_stored, x_stored, x_back = sem("rel_stored"), sem("x_stored"), sem("x_back")
        sq_made, sq_summed, rs_made, xn_made = sem("sq_made"), sem("sq_summed"), sem("rs_made"), sem("xn_made")
        xs_made = sem("xs_made")
        scales_made, aff_made, affs_made = sem("scales_made"), sem("aff_made"), sem("affs_made")
        nhi_act, nhi_dve = sem("nhi_act"), sem("nhi_dve")
        h_pool, h_dve = sem("h_pool"), sem("h_dve")
        ln_rs = sem("ln_rs")
        ln_sum, ln_sq, ln_sqsum, ln_scaled, ln_out = (
            sem("ln_sum"), sem("ln_sq"), sem("ln_sqsum"), sem("ln_scaled"), sem("ln_out"))
        mixed_hi, mixed_ready = sem("mixed_hi"), sem("mixed_ready")
        hid_hi, hid_lo = sem("hid_hi"), sem("hid_lo")
        st_packed, c_packed = sem("st_packed"), sem("c_packed")
        conv_step, st_stored = sem("conv_step"), sem("st_stored")
        bias_loaded, bias_fixed, k_stored, kv_stored = (
            sem("bias_loaded"), sem("bias_fixed"), sem("k_stored"), sem("kv_stored"))
        qk_half, sc_max, exp_done = sem("qk_half"), sem("sc_max"), sem("exp_done")
        o_stored = [sem(f"o_stored{s}") for s in range(4)]
        smp_loaded, qd_zero, qd_made = sem("smp_loaded"), sem("qd_zero"), sem("qd_made")
        cache_loaded = [sem(f"cache_loaded{s}") for s in range(3)]
        s_max, s_exp, s_norm, v_used = sem("s_max"), sem("s_exp"), sem("s_norm"), sem("v_used")
        nat_loaded, comb_m, comb_e, comb_done = sem("nat_loaded"), sem("comb_m"), sem("comb_e"), sem("comb_done")
        c_loaded, cpad_made, cst_stored, cconv_done = sem("c_loaded"), sem("cpad_made"), sem("cst_stored"), sem("cconv_done")
        d_loaded, wsT_made, wsS_loaded, vd_stored, yd_made = (
            sem("d_loaded"), sem("wsT_made"), sem("wsS_loaded"), sem("vd_stored"), sem("yd_made"))
        y_scaled, y_stored, caches_moved = sem("y_scaled"), sem("y_stored"), sem("caches_moved")

        def big_evacuated(e, t):
            e.wait_ge(big_free[t % 2], t // 2 + 1)

        def misc_evacuated(e, q):
            e.wait_ge(misc_free[q % 2], q // 2 + 1)

        def in_blocks(dst, tile, do):
            do(dst[:, 0:2 * BLK].rearrange("p (b n) -> p b n", b=2), tile[:, 0:2, 0:BLK])
            return do(dst[:, 2 * BLK:TOK], tile[:, 2, 0:BLK])

        def blocks(ap):
            return ap.rearrange("p (b n) -> p b n", b=3)

        unit_end = {}
        for it in plan:
            if it.kind == "ada":
                unit_end[it.unit] = (misc_ready, it.misc + 1)
            elif it.kind in ("project", "down"):
                unit_end[it.unit] = (big_ready, it.big + (2 if it.kind == "project" else 8))
            elif it.kind == "ffn":
                unit_end[it.unit], unit_end[it.unit + 1] = (big_ready, it.big + 2), (big_ready, it.big + 4)
                for g in range(1, GROUPS + 1):
                    for n, t in enumerate((2, 4, 12) if g < GROUPS else (8,)):
                        unit_end[it.unit + 3 * g - 1 + n] = (big_ready, it.big + 4 + 12 * (g - 1) + t)
        attends = [it for it in plan if it.kind == "attend"]
        dense_items = [it for it in plan if it.kind in ("project", "down")]
        HI_DVE, LO_DVE = (3, 7), (1, 3, 5, 7)

        def hi_made(e, n, k):
            own = [j for j in range(KT) if (j in HI_DVE) == (k in HI_DVE)]
            e.wait_ge(nhi_dve if k in HI_DVE else nhi_act, len(own) * n + own.index(k) + 1)

        def lo_made(e, n, k):
            own = [j for j in range(KT) if (j in LO_DVE) == (k in LO_DVE)]
            e.wait_ge(h_dve if k in LO_DVE else h_pool, len(own) * n + own.index(k) + 1)

        squares_after = {}
        for i, it in enumerate(plan):
            if it.kind == "gate_sample":
                last = plan[i - 1]
                squares_after[last.big + (0 if last.kind == "down" else 4 + 24 * ((GROUPS - 1) // 2))] = plan[i + 1].n

        def sq_tile(n, k):
            return tmp[:, 2, 0:SEQ] if k == 0 else tmp[:, 3, 0:SEQ] if k % 2 else (sq_first if n == 0 else tmp[:, 0, :])[:, 0:SEQ]

        ada_outs = [it for it in plan if it.kind == "ada_out"]
        x_tiles = [it.x for it in plan if it.kind == "x_in"]
        ada_number = {it.unit: it.k for it in plan if it.kind == "ada"}
        ada_misc = {it.k: it.misc for it in plan if it.kind == "ada"}
        by_role = {(it.role, it.j or it.g or 0): it for it in dense_items if it.kind == "project"}
        K_STORES = (2, 4, 8)
        PAIRS = (GROUPS - 1) // 2

        def steps(i, first, per_turn):
            return first if i is None else i * per_turn + first

        def positions(g, ap):
            return ap.rearrange("p (r n) -> p r n", r=DILATIONS[g])

        def cache_cols(ap, g, a, b, s):
            v = ap.rearrange("p (h t) -> p h t", h=HPG)[:, 2 * a:2 * a + 2, :]
            return v[:, :, NS * b:NS * b + NS] if g == 0 else v[:, :, NS * b + s:NS * b + s + 1]

        CACHE_TILES = [(0, 0)] + [(1, s) for s in range(NS)] + [(2, s) for s in range(NS)]

        sample_item = next(it for it in plan if it.kind == "sample")
        state_item = next(it for it in plan if it.kind == "a_state")
        c_in_misc = {it.j: it.misc for it in plan if it.kind == "c_state_in"}
        c_conv_misc = {it.j: it.misc for it in plan if it.kind == "c_conv"}

        def o_stores(step):
            return 16 * sum(2 if n >= 32 else 1 for n in range(step % 4, step + 1, 4))

        block = ctx.enter_context(nc.Block())

        @block.sync
        def _(sp):
            def as_project(w):
                return w.rearrange("p (k n) -> p k n", k=KT)

            def as_down(w):
                return w.rearrange("p (k n) -> p k n", k=2)

            def load_raw(r, view, src):
                if r >= NRAW:
                    sp.wait_ge(w_lo_done, r - NRAW + 1)
                    if r - NRAW in ada_number:
                        sp.wait_ge(w_lo_half, ada_number[r - NRAW] + 1)
                sp.dma_start(view(w_raw[r % NRAW]), src).then_inc(raw_loaded[r % NRAW], 16)

            def columns(w, c):
                return w.rearrange("(k p) n -> p k n", p=P)[:, :, 256 * c:256 * c + 256]

            sp.dma_start(ident, A["ident"]).then_inc(in_loaded, 16)
            sp.dma_start(pair_sum, A["pair_sum"]).then_inc(in_loaded, 16)
            for set_, names in enumerate((
                    ("ada_b",), ("norm_mix_g", "norm_ffn_g", "final_norm_g"),
                    ("a_conv_w", "a_conv_b", "a_ln_g", "a_ln_b", "c_conv_w", "c_conv_b", "d_ln_g", "d_ln_b"))):
                row = 0
                for name in names:
                    flat = A[name]
                    if len(flat.shape) == 2:
                        flat = flat.rearrange("a b -> (a b)")
                    elif len(flat.shape) == 3:
                        flat = flat.rearrange("a b c -> (a b c)")
                    k = flat.shape[0] // P
                    sp.dma_start(vrow[row:row + k, set_, :], flat.rearrange("(r n) -> r n", n=P)).then_inc(in_loaded, 16)
                    row += k
            sp.dma_start(c_rows[0:1, :], A["c_prompt"]).then_inc(in_loaded, 16)
            sp.dma_start(c_rows[1:9, :], A["c_sample"]).then_inc(in_loaded, 16)
            loads = sorted((it for it in plan if it.unit is not None), key=lambda it: it.unit)
            smp = next(it for it in plan if it.kind == "sample")
            last_before_sample = next(it for it in dense_items if it.weights == "e_w_out" and it.col == 1)
            for it in loads:
                if it.unit == 1:
                    for n in range(8):
                        sp.dma_start(x_tok[:, n, :], A["x_prompt"][0, n * P:(n + 1) * P, :]).then_inc(x_loaded, 16)
                    sp.dma_start(xs_tok, A["x_sample"].rearrange("b s d -> (b s) d")).then_inc(x_loaded, 16)
                if it.kind == "ada":
                    layer, cb = divmod(it.k, 24)
                    load_raw(it.unit, as_project, columns(A["ada_w"][layer], cb))
                elif it.kind == "project":
                    load_raw(it.unit, as_project, columns(A[it.weights][0], it.col))
                elif it.kind == "down":
                    load_raw(it.unit, as_down, A[it.weights][0][256 * it.col:256 * it.col + 256, :]
                             .rearrange("(k p) n -> p k n", p=P))
                elif it.kind == "ffn":
                    up = A["ffn_w_gate_up"][it.layer].rearrange("(k p) n -> p k n", p=P)
                    down = A["ffn_w_down"][it.layer].rearrange("(k p) n -> p k n", p=P)
                    load_raw(it.unit, as_project, up[:, :, 0:256])
                    load_raw(it.unit + 1, as_project, up[:, :, FFN:FFN + 256])
                    with sp.Fori(0, PAIRS) as i:
                        for n in range(6):
                            r, k = it.unit + 2 + n, n // 3
                            sp.wait_ge(w_lo_done, i * 6 + (it.unit + 3 + n - NRAW))
                            if n % 3 == 2:
                                sp.dma_start(as_down(w_raw[r % NRAW]), down[:, bass.ds(i * 4 + 2 * k, 2), :])\
                                    .then_inc(raw_loaded[r % NRAW], 16)
                            else:
                                col = i * 512 + (256 * (1 + k) + (FFN if n % 3 else 0))
                                sp.dma_start(as_project(w_raw[r % NRAW]), up[:, :, bass.ds(col, 256)])\
                                    .then_inc(raw_loaded[r % NRAW], 16)
                    load_raw(it.unit + 3 * GROUPS - 1, as_down, down[:, 2 * GROUPS - 2:2 * GROUPS, :])
                if it is last_before_sample:
                    sp.wait_ge(big_ready, by_role["v", 2].big + 2)
                    for c in range(2 * NB):
                        kv, b = divmod(c, NB)
                        if 3 <= c < NB + 3:
                            sp.wait_ge(misc_ready, smp.kt + 5 * (c - 3) + 5)
                        elif c >= NB + 3:
                            sp.wait_ge(v_used, c - 3 - NB + 1)
                        rows = [A[f"cache_b_kv{g}"][0, b, :, kv].rearrange("w h e -> w (h e)") for g in range(3)]
                        sp.dma_start(cache[:, c % 3, 0, :], rows[0]).then_inc(cache_loaded[c % 3], 16)
                        sp.dma_start(cache[:, c % 3, 1:5, :], rows[1].rearrange("(j s) e -> j s e", s=4))\
                            .then_inc(cache_loaded[c % 3], 16)
                        sp.dma_start(cache[:, c % 3, 5:9, :], rows[2].rearrange("(j s) e -> j s e", s=16)[:, 0:NS, :])\
                            .then_inc(cache_loaded[c % 3], 16)
            fin = plan[-1]
            for n in range(9):
                big_evacuated(sp, fin.out + n)
                if n < 8:
                    sp.dma_start(O["y_prompt"][0, n * P:(n + 1) * P, :], y_rows[:, n, :]).then_inc(y_stored, 16)
                else:
                    sp.dma_start(O["y_sample"].rearrange("b s d -> (b s) d"), y_rows[0:S_TOK, n, :])\
                        .then_inc(y_stored, 16)
            sp.wait_ge(y_stored, 16 * 9)
            sp.wait_ge(st_stored, 16 * 2)
            sp.wait_ge(kv_stored, 16 * 6)
            sp.wait_ge(k_stored, 16 * K_STORES[2])
            sp.wait_ge(cst_stored, 16 * 4)
            sp.wait_ge(vd_stored, 16)
            sp.wait_ge(caches_moved, 16 * 3 * NB)
            sp.wait_ge(x_stored, 16)
            sp.wait_ge(rel_stored, 32)
            for s in range(4):
                sp.wait_ge(o_stored[s], o_stores(47 - 3 + s))

        @block.scalar
        def _(act):
            link = [0]

            def own(ins):
                link[0] += 1
                ins.then_inc(act_link, 1)
                act.wait_ge(act_link, link[0])

            def split_hi(u, i=None, raw_turn=0):
                act.wait_ge(raw_loaded[u % NRAW], steps(i, 16 * (u // NRAW + 1), 16 * 6 // NRAW))
                if u >= 2:
                    act.wait_ge(unit_end[u - 2][0], steps(i, unit_end[u - 2][1], 24))
                act.activation(w_hi[u % 2], w_raw[u % NRAW], ACT.Copy).then_inc(w_hi_done, 1)

            def evacuate(t, func, dst, i=None, **kw):
                act.wait_ge(big_ready, steps(i, t + 1, 24))
                return act.activation(blocks(dst), big(t)[:, :, 0:BLK], func, **kw).then_inc(big_free[t % 2], 1)

            def square(n, k):
                if k >= 3:
                    act.wait_ge(sq_summed, 8 * n + k - 2)
                act.activation(sq_tile(n, k), x[:, k, 0:SEQ], ACT.Square).then_inc(sq_made, 1)

            def squares(t0):
                if t0 in squares_after:
                    for m in range(KT):
                        big_evacuated(act, t0 + m)
                        square(squares_after[t0], m)

            for it in plan:
                if it.kind == "setup":
                    act.wait_ge(in_loaded, 16 * 16)
                    act.activation(c_rows, c_rows, ACT.Silu).then_inc(c_silu, 1)
                    split_hi(0)
                elif it.kind == "ada":
                    split_hi(it.unit + 1)
                    if it.k == 8:
                        act.wait_ge(x_stored, 16)
                    act.wait_ge(misc_ready, it.misc + 1)
                    act.activation(ada_rows[it.k >= 8], misc(it.misc)[0:18, 0:256], ACT.Copy)\
                        .then_inc(misc_free[it.misc % 2], 1)
                elif it.kind == "x_in":
                    if it.k % 2:
                        act.wait_ge(big_ready, it.x + 1)
                        act.activation(x[:, it.k, 0:SEQ].rearrange("p (b n) -> p b n", b=2), big(it.x)[:, 0:2, :], ACT.Copy)
                        act.activation(x[:, it.k, SEQ:TOK], big(it.x)[:, 2, 0:S_TOK], ACT.Copy)\
                            .then_inc(big_free[it.x % 2], 1)
                    big_evacuated(act, it.x)
                    square(0, it.k)
                elif it.kind in ("norm", "final"):
                    n = it.n
                    evacuate(it.big, ACT.Ln, tmp[:, 3, :], bias=eps[:, 0:1])
                    big_evacuated(act, it.big)
                    act.activation(tmp[:, 3, :], tmp[:, 3, :], ACT.Exp, scale=-0.5).then_inc(rs_made, 1)
                    for k in range(KT):
                        act.wait_ge(xn_made, 8 * n + k + 1)
                        if it.kind == "final":
                            act.activation(nt[:, k, :], nt[:, k, :], ACT.Identity,
                                           scale=vecs[:, V_FIN + k:V_FIN + k + 1]).then_inc(y_scaled, 1)
                            continue
                        c = 6 * it.layer + 3 * it.which
                        if k == 0:
                            act.wait_ge(scales_made, n + 1)
                        act.activation(nt[:, k, 0:SEQ], nt[:, k, 0:SEQ], ACT.Identity, bias=mod[:, c, k, 0:1],
                                       scale=mod[:, c + 1, k, 0:1]).then_inc(aff_made, 1)
                        if k not in HI_DVE:
                            if k == 0:
                                act.wait_ge(affs_made, n + 1)
                            act.wait_ge(aff_made, 8 * n + k + 1)
                            act.activation(h_hi[:, k, :], nt[:, k, :], ACT.Copy).then_inc(nhi_act, 1)
                    if it.kind == "final":
                        for m in range(1, 9, 2):
                            t = it.out + m
                            act.wait_ge(big_ready, t + 1)
                            act.activation(y_rows[:, m, :].rearrange("p (b n) -> p b n", b=2), big(t)[:, 0:2, :], ACT.Copy)\
                                .then_inc(big_free[t % 2], 1)
                elif it.kind == "project":
                    if it.unit + 1 in unit_end:
                        split_hi(it.unit + 1)
                    for m in range(2):
                        t = it.big + m
                        if it.role == "a_gate":
                            evacuate(t, ACT.Sigmoid, sig[:, m, :])
                        elif it.role == "q":
                            d, g = DILATIONS[it.g], it.g
                            if m == 0 and g == 0:
                                act.wait_ge(x_stored, 16)
                            act.wait_ge(big_ready, t + 1)
                            for b, n in enumerate((BLK, BLK, LAST)):
                                act.activation(positions(g, qkv[:, m, :])[:, :, BLK // d * b:BLK // d * b + n // d],
                                               big(t)[:, b, 0:n].rearrange("p (j r) -> p r j", r=d), ACT.Copy, scale=DH ** -0.5)
                            act.activation(q_new[:, g, m, :], big(t)[:, 2, LAST:BLK], ACT.Copy, scale=DH ** -0.5)\
                                .then_inc(big_free[t % 2], 1)
                        elif it.role == "c_gate":
                            if it.j and m == 0:
                                act.wait_ge(mixed_ready, 3)
                            evacuate(t, ACT.Copy, tmp[:, m, :])
                        elif it.role == "d_v":
                            if it.j == 0 and m == 0:
                                act.wait_ge(mixed_ready, 4)
                            evacuate(t, ACT.Gelu_apprx_tanh, tmp[:, 2 * it.j + m, :])
                        elif it.role == "d_u":
                            if it.j and m == 0:
                                act.wait_ge(wsT_made, 2)
                                for b in range(NB):
                                    act.dma_start(wsS[NS * b:NS * b + NS, :, NS * b:NS * b + NS], wsT[0:NS, :, 0:NS])\
                                        .then_inc(wsS_loaded, 16)
                            evacuate(t, ACT.Gelu_apprx_tanh, u_fm[:, 2 * it.j + m, :])
                        elif it.role == "c_out":
                            big_evacuated(act, t)
                            act.activation(mid_hi[:, it.j, m, :], tmp[:, m, :], ACT.Copy).then_inc(mixed_hi, 1)
                elif it.kind == "down":
                    if it.unit + 1 in unit_end:
                        split_hi(it.unit + 1)
                    squares(it.big)
                elif it.kind == "a_state":
                    for m, (n, w) in enumerate(((EXT_A, 256), (120, 512))):
                        act.wait_ge(misc_ready, it.misc + m + 1)
                        act.activation(st_out[0:n, m:m + w // 256, :].rearrange("p a n -> p (a n)"),
                                       misc(it.misc + m)[0:n, 0:w], ACT.Copy).then_inc(misc_free[(it.misc + m) % 2], 1)
                    misc_evacuated(act, it.misc)
                    act.dma_start(O["a_conv_prompt"][0, 0], st_out[0:EXT_A, 0, :]).then_inc(st_stored, 16)
                    misc_evacuated(act, it.misc + 1)
                    act.dma_start(O["a_conv_sample"][0].rearrange("(h b) t c -> (b t) h c", h=2), st_out[0:120, 1:3, :])\
                        .then_inc(st_stored, 16)
                elif it.kind == "tokens":
                    g = it.g
                    if g == 0:
                        act.wait_ge(st_stored, 32)
                    for n in range(len(it.k_tiles)):
                        q = it.k + n
                        act.wait_ge(misc_ready, q + 1)
                        act.activation(k_rows[:, n, :], misc(q)[:, 0:256], ACT.Copy).then_inc(misc_free[q % 2], 1)
                    for q in (it.v + 6, it.v + 7, it.new, it.k + len(it.k_tiles) - 1, it.k + max(0, len(it.k_tiles) - 2)):
                        misc_evacuated(act, q)
                    dst = O[f"kv{g}_prompt"][0, 0].rearrange("t k h e -> t k (h e)")
                    for kv, src in ((0, k_rows), (1, v_tok)):
                        if g == 0:
                            act.dma_start(dst[:, kv, :], src[:, 0 if kv == 0 else 7, :]).then_inc(k_stored, 16)
                        elif g == 1:
                            rows = src[:, 0:4, :] if kv == 0 else src[:, 1:8:2, :]
                            act.dma_start(dst[:, kv, :].rearrange("(i r) c -> i r c", r=4), rows).then_inc(k_stored, 16)
                        else:
                            to = dst[:, kv, :].rearrange("(i n r) c -> r i n c", n=8, r=2)
                            for r in range(2):
                                act.dma_start(to[r], src[64 * r:64 * r + 64, :, :]).then_inc(k_stored, 16)
                    act.dma_start(d_kv[g], kv_rows.rearrange("p k c -> p (k c)")).then_inc(kv_stored, 16)
                    W = WINDOWS[g]
                    act.dma_start(O[f"kv{g}_sample"][0, :, W - NS:W].rearrange("b s k h e -> b s (k h e)"),
                                  kv_rows.rearrange("p k c -> p (k c)")).then_inc(kv_stored, 16)
                elif it.kind == "attend":
                    g = it.g

                    def store(j):
                        step, sb, a = 16 * g + j, j // 2, j % 2
                        misc_evacuated(act, it.pv[j])
                        rows = d_o[g][:, 132 * a:132 * a + 132]
                        src = o_rows[:, step % 4, :]
                        if g == 0:
                            act.dma_start(rows[P * sb:P * sb + P, :], src).then_inc(o_stored[step % 4], 16)
                        elif g == 1:
                            act.dma_start(rows.rearrange("(i r) c -> r i c", r=4)[sb // 2, P * (sb % 2):P * (sb % 2) + P, :],
                                          src).then_inc(o_stored[step % 4], 16)
                        else:
                            for r in range(2):
                                act.dma_start(rows.rearrange("(i r) c -> r i c", r=16)[2 * sb + r], src[64 * r:64 * r + 64, :])\
                                    .then_inc(o_stored[step % 4], 16)

                    for i in (it.i,):
                        if 0 <= i - 1 < 16:
                            j = i - 1
                            w = 256 * key_tiles(g, j // 2)
                            act.wait_ge(misc_ready, it.tr[j] + 1)
                            act.activation(pt[:, j % 2, 0:w], misc(it.tr[j])[:, 0:w], ACT.Copy)\
                                .then_inc(misc_free[it.tr[j] % 2], 1)
                        if i < 16:
                            step, nk = 16 * g + i, P * key_tiles(g, i // 2)
                            act.wait_ge(sc_max, step + 1)
                            for h in range(2):
                                o = o_rows[:, step % 4, :]
                                last = act.activation(sc[:, i % 2, h * nk:h * nk + nk], sc[:, i % 2, h * nk:h * nk + nk],
                                                      ACT.Exp, bias=o[:, 130 + h:131 + h], accum_out=o[:, 128 + h:129 + h])
                            last.then_inc(exp_done, 1)
                        if 0 <= i - 3:
                            store(i - 3)
                elif it.kind == "ln_mean":
                    v, s, q = (conv_a, tmp[:, 0, :], tmp[:, 1, :]) if it.which == "a" else (tmp, ln_t[:, 0, :], ln_t[:, 1, :])
                    if it.which == "d":
                        down_c = next(d for d in dense_items if d.weights == "o_w_out" and d.col == 1)
                        act.wait_ge(big_ready, down_c.big + 8)
                        act.dma_start(ws_raw, A["d_spatial_w"][0].rearrange("g i j -> i g j")).then_inc(d_loaded, 16)
                        act.dma_start(bs_b.rearrange("p g n -> p (g n)"),
                                      A["d_spatial_b"].rearrange("a g n -> a (g n)").to_broadcast([P, 512])).then_inc(d_loaded, 16)
                    big_evacuated(act, it.big)
                    for m in range(it.nt):
                        if m >= 2:
                            act.wait_ge(ln_sqsum, (0 if it.which == "a" else 1) + m - 1)
                        act.activation(s if m == 0 else q, v[:, m, :], ACT.Square).then_inc(ln_sq, 1)
                elif it.kind == "ln_var":
                    C, first = it.nt * P, 0 if it.which == "a" else 2
                    v, s, q = (conv_a, tmp[:, 0, :], tmp[:, 1, :]) if it.which == "a" else (tmp, ln_t[:, 0, :], ln_t[:, 1, :])
                    evacuate(it.big, ACT.Ln, q, bias=eps[:, 0:1], scale=float(D_MODEL // C))
                    big_evacuated(act, it.big)
                    act.activation(q, q, ACT.Exp, scale=-0.5).then_inc(ln_rs, 1)
                    for m in range(it.nt):
                        act.wait_ge(ln_scaled, 2 if it.which == "a" else first + m + 1)
                        G, B = (V_ALG, V_ALB) if it.which == "a" else (V_DLG, V_DLB)
                        if it.which == "a":
                            act.activation(s if m == 0 else q, v[:, m, :], ACT.Silu, bias=vecs[:, B + m:B + m + 1],
                                           scale=vecs[:, G + m:G + m + 1]).then_inc(ln_out, 1)
                            act.wait_ge(ln_out, m + 1)
                            act.activation(mid_hi[:, 0, m, :], s if m == 0 else q, ACT.Copy).then_inc(mixed_hi, 1)
                        else:
                            act.activation(v[:, m, :], v[:, m, :], ACT.Identity, bias=vecs[:, B + m:B + m + 1],
                                           scale=vecs[:, G + m:G + m + 1]).then_inc(ln_out, 1)
                elif it.kind == "sample":
                    for n in range(1, 40, 2):
                        q = it.kt + n
                        act.wait_ge(misc_ready, q + 1)
                        w = P * (2 if n % 5 == 4 else 4)
                        act.activation(kTs[:, n % 2, 0:w], misc(q)[:, 0:w], ACT.Copy).then_inc(misc_free[q % 2], 1)
                    act.wait_ge(s_max, 1)
                    act.activation(p_s, p_s, ACT.Exp, bias=den_s[:, 0:1], accum_out=den_s[:, 1:2]).then_inc(s_exp, 1)
                    act.wait_ge(misc_ready, it.tp + 1)
                    act.activation(pT_s.rearrange("p g r -> p (g r)"), misc(it.tp)[:, 0:384], ACT.Copy)\
                        .then_inc(misc_free[it.tp % 2], 1)
                    act.wait_ge(comb_m, 1)
                    act.activation(comb[:, 1:4, :, :], comb[:, 1:4, :, :], ACT.Exp).then_inc(comb_e, 1)
                elif it.kind == "combine":
                    for a in range(2):
                        t = it.big + a
                        act.wait_ge(big_ready, t + 1)
                        act.activation(mid_hi[:, 1, a, 0:SEQ].rearrange("p (b n) -> p b n", b=2), big(t)[:, 0:2, :], ACT.Copy)
                        if a == 0:
                            big_evacuated(act, sample_item.pv)
                        act.activation(mid_hi[:, 1, a, SEQ:TOK], att_s[:, a, :], ACT.Copy).then_inc(mixed_hi, 1)
                elif it.kind == "ffn":
                    first = 2 * GROUPS * it.layer

                    def hidden(g, t, i, later):
                        for m in range(2):
                            if g:
                                act.wait_ge(hid_lo, steps(i, first + 2 * (g - 1) + m + 1, 4))
                            evacuate(t + m, ACT.Silu, tmp[:, m, :], i)
                        later()
                        for m in range(2):
                            act.wait_ge(big_free[t % 2] if m == 0 else big_free[(t + 1) % 2],
                                        steps(i, (t + 2 + m) // 2 + 1, 12))
                            act.activation(mid_hi[:, g % 2, m, :], tmp[:, m, :], ACT.Copy).then_inc(hid_hi, 1)

                    u = it.unit
                    split_hi(u + 1)
                    hidden(0, it.big, None, lambda: split_hi(u + 2))
                    with act.Fori(0, PAIRS) as i:
                        for k in range(2):
                            v0 = u + 2 + 3 * k
                            split_hi(v0 + 1, i)
                            hidden(1 + k, it.big + 4 + 12 * k, i, lambda: split_hi(v0 + 2, i))
                            split_hi(v0 + 3, i)
                    if u + 3 * GROUPS in unit_end:
                        split_hi(u + 3 * GROUPS)
                    squares(it.big + 4 + 24 * PAIRS)
                elif it.kind == "c_conv":
                    if it.j:
                        act.wait_ge(cst_stored, 32)
                    for m, n in enumerate((EXT_C, NB * EXT_C)):
                        act.wait_ge(misc_ready, it.misc + m + 1)
                        act.activation(cst_out[0:n, m, :], misc(it.misc + m)[0:n, 0:256], ACT.Copy)\
                            .then_inc(misc_free[(it.misc + m) % 2], 1)
                    misc_evacuated(act, it.misc)
                    act.dma_start(O["c_conv_prompt"][0, 0][:, 256 * it.j:256 * it.j + 256], cst_out[0:EXT_C, 0, :])\
                        .then_inc(cst_stored, 16)
                    misc_evacuated(act, it.misc + 1)
                    act.dma_start(O["c_conv_sample"][0].rearrange("b t c -> (b t) c")[:, 256 * it.j:256 * it.j + 256],
                                  cst_out[:, 1, :]).then_inc(cst_stored, 16)
                elif it.kind == "spatial":
                    for n in range(1, 8, 2):
                        q = it.tok + n
                        act.wait_ge(misc_ready, q + 1)
                        act.activation(vd_tok[:, n, :], misc(q), ACT.Copy).then_inc(misc_free[q % 2], 1)
                    misc_evacuated(act, it.tok + 8)
                    act.dma_start(O["d_v_sample"][0].rearrange("b s c -> (b s) c"), vd_new).then_inc(vd_stored, 16)
                    for g in range(4):
                        act.wait_ge(yd_made, g + 1)
                        act.activation(h_hi[:, g, :], ln_t[:, g % 2, :], ACT.Copy).then_inc(mixed_hi, 1)

        @block.vector
        def _(dve):
            link = [0]

            def own(ins):
                link[0] += 1
                ins.then_inc(dve_link, 1)
                dve.wait_ge(dve_link, link[0])

            ln_adds, x_dones = [0], [0]

            def add_square(n, k):
                if k >= 1:
                    dve.wait_ge(sq_made, 8 * n + k + 1)
                    if k >= 2:
                        dve.wait_ge(sq_summed, 8 * n + k - 1)
                    dve.tensor_tensor(tmp[:, 2, 0:SEQ], tmp[:, 2, 0:SEQ], sq_tile(n, k), ALU.add).then_inc(sq_summed, 1)

            def evacuate_down(t0, layer, gate, i=None):
                for m in range(KT):
                    t, g = t0 + m, mod[:, 6 * layer + gate, m, 0:1]
                    dve.wait_ge(big_ready, steps(i, t + 1, 24))
                    for dst, src in ((x[:, m, 0:2 * BLK].rearrange("p (b n) -> p b n", b=2), big(t)[:, 0:2, 0:BLK]),
                                     (x[:, m, 2 * BLK:SEQ], big(t)[:, 2, 0:LAST])):
                        dve.scalar_tensor_tensor(dst, src, g, dst, ALU.mult, ALU.add)
                    dve.tensor_tensor(acc_s[:, m, :], big(t)[:, 2, LAST:BLK], acc_s[:, m, :], ALU.add)\
                        .then_inc(big_free[t % 2], 1)
                    if t0 in squares_after and i is None and m >= 1:
                        add_square(squares_after[t0], m - 1)

            def low(dst, hi, src):
                return dve.tensor_tensor(dst, src, hi.bitcast(F32), ALU.subtract)

            def split_lo_half(u):
                if u in ada_number:
                    dve.wait_ge(w_hi_done, u + 1)
                    low(w_lo[u % 2][:, 1024:2048], w_hi[u % 2][:, 1024:2048], w_raw[u % NRAW][:, 1024:2048])\
                        .then_inc(w_lo_half, 1)

            for it in plan:
                if it.kind in ("ada", "project", "down"):
                    split_lo_half(it.unit + 1)
                if it.kind == "setup":
                    dve.memset(mean_w, 1.0 / D_MODEL)
                    dve.memset(eps, EPS)
                    dve.memset(tab_b[N_BUCKETS:N_BUCKETS + 1, :, :], 1.0)
                    dve.memset(acc_s, 0.0).then_inc(consts_made, 1)
                    dve.wait_ge(misc_ready, it.vec + 1)
                    dve.tensor_copy(vecs, misc(it.vec)[:, 0:V_ALL]).then_inc(misc_free[it.vec % 2], 1)
                    dve.wait_ge(misc_ready, it.c + 1)
                    c_tile = misc(it.c)[:, 0:9 * KT].rearrange("p (k c) -> p k c", k=KT)
                    own(dve.tensor_copy(cs[:, :, 0, :], c_tile))
                    low(cs[:, :, 1, :], cs[:, :, 0, :], c_tile).then_inc(misc_free[it.c % 2], 1)
                    dve.wait_ge(tabs_loaded, 16 * 6)
                    dve.wait_ge(misc_ready, it.ext + 1)
                    own(dve.tensor_copy(st_fm, misc(it.ext)[:, 0:2 * NB * EXT_A]))
                    dve.tensor_copy(tab_s, tab.rearrange("k (g h) -> k g h", g=3).unsqueeze(3)
                                    .to_broadcast([N_BUCKETS, 3, HPG, S_TOK])).then_inc(misc_free[it.ext % 2], 1)
                    split_lo_half(0)
                    dve.tensor_copy(tab_b[0:N_BUCKETS], tab.unsqueeze(2).to_broadcast([N_BUCKETS, 12, P])).then_inc(tab_made, 1)
                elif it.kind == "x_in":
                    if it.k % 2 == 0:
                        dve.wait_ge(big_ready, it.x + 1)
                        dve.tensor_copy(x[:, it.k, 0:SEQ].rearrange("p (b n) -> p b n", b=2), big(it.x)[:, 0:2, :])
                        dve.tensor_copy(x[:, it.k, SEQ:TOK], big(it.x)[:, 2, 0:S_TOK]).then_inc(big_free[it.x % 2], 1)
                    if it.k:
                        add_square(0, it.k - 1)
                elif it.kind == "rel":
                    for n in range(12):
                        q = it.rel + n
                        dve.wait_ge(misc_ready, q + 1)
                        dve.tensor_copy(rel_rep[:, n, 0:REL], misc(q)[:, 0:REL]).then_inc(misc_free[q % 2], 1)
                    for n in range(2):
                        q = it.rels + n
                        dve.wait_ge(misc_ready, q + 1)
                        for s in range(3 * n, min(3 * n + 3, NS)):
                            own(dve.scalar_tensor_tensor(bias_s0[:, 0, :], misc(q)[:, 160 * (s % 3):160 * (s % 3) + 160],
                                                         row_step[:, s:s + 1], mask_s[:, 0, :] if s == 0 else bias_s0[:, 0, :],
                                                         ALU.mult, ALU.add))
                        if n == 1:
                            own(dve.tensor_tensor(bias_s0[:, 1:3, :], misc(q)[:, 160:480].rearrange("p (g n) -> p g n", g=2),
                                                  mask_s[:, 1:3, :], ALU.add))
                        dve.engine_nop().then_inc(misc_free[q % 2], 1)
                elif it.kind == "ada_out":
                    layer, cb = divmod(it.k, 24)
                    dve.wait_ge(misc_ready, it.misc + 1)
                    col = V_ADA + 48 * layer + 2 * cb
                    dve.tensor_tensor(mod[:, 6 * layer + cb // 4, 2 * (cb % 4):2 * (cb % 4) + 2, :],
                                      misc(it.misc)[:, 0:18].rearrange("p (m c) -> p m c", m=2),
                                      vecs[:, col:col + 2].unsqueeze(2).to_broadcast([P, 2, 9]), ALU.add)\
                        .then_inc(misc_free[it.misc % 2], 1)
                elif it.kind in ("norm", "final"):
                    n, final = it.n, it.kind == "final"
                    rs = tmp[:, 3, :]
                    if n == 0:
                        for t in x_tiles:
                            big_evacuated(dve, t)
                    add_square(n, KT - 1)
                    own(dve.tensor_tensor(acc_s, x[:, :, SEQ:TOK], x[:, :, SEQ:TOK], ALU.mult))
                    dve.tensor_reduce(tmp[:, 2, SEQ:TOK], acc_s.rearrange("p k s -> p s k"), AX_X, ALU.add).then_inc(sq_summed, 1)
                    dve.wait_ge(sq_summed, 8 * n + 8)
                    own(dve.memset(acc_s, 0.0))
                    if not final:
                        c = 6 * it.layer + 3 * it.which + 1
                        g0 = (V_FFN if it.which else V_MIX) + 8 * it.layer
                        misc_evacuated(dve, ada_outs[4 * c + 3].misc)
                        dve.scalar_tensor_tensor(mod[:, c, :, :], mod[:, c, :, :], 1.0,
                                                 vecs[:, g0:g0 + KT].unsqueeze(2).to_broadcast([P, KT, 9]), ALU.add, ALU.mult)\
                            .then_inc(scales_made, 1)
                    dve.wait_ge(rs_made, n + 1)
                    if n == 0:
                        dve.wait_ge(rel_stored, 32)

                    def scaled(k):
                        cols = slice(0, TOK if final else SEQ)
                        dve.tensor_tensor(nt[:, k, cols], x[:, k, cols], rs[:, cols], ALU.mult).then_inc(xn_made, 1)

                    if not final:
                        dve.tensor_tensor(nt[:, :, SEQ:TOK], x[:, :, SEQ:TOK],
                                          rs[:, SEQ:TOK].unsqueeze(1).to_broadcast([P, KT, S_TOK]), ALU.mult).then_inc(xs_made, 1)
                    if final:
                        for k in range(KT):
                            scaled(k)
                        for m in range(0, 9, 2):
                            t = it.out + m
                            dve.wait_ge(big_ready, t + 1)
                            rows = P if m < 8 else S_TOK
                            dve.tensor_copy(y_rows[0:rows, m, :].rearrange("p (b n) -> p b n", b=2), big(t)[0:rows, 0:2, :])\
                                .then_inc(big_free[t % 2], 1)
                        continue
                    scaled(0)
                    scaled(1)
                    for k in range(KT + 1):
                        if k in HI_DVE:
                            dve.wait_ge(aff_made, 8 * n + k + 1)
                            dve.wait_ge(affs_made, n + 1)
                            dve.tensor_copy(h_hi[:, k, :], nt[:, k, :]).then_inc(nhi_dve, 1)
                        if k + 2 < KT:
                            scaled(k + 2)
                        if k - 1 in LO_DVE:
                            hi_made(dve, n, k - 1)
                            low(h_lo[:, k - 1, :], h_hi[:, k - 1, :], nt[:, k - 1, :]).then_inc(h_dve, 1)
                elif it.kind == "project":
                    for m in range(2):
                        t = it.big + m
                        if it.role in ("a_gate", "q", "c_gate", "d_v", "d_u"):
                            continue
                        dve.wait_ge(big_ready, t + 1)
                        T = big(t)
                        if it.role in ("k", "v"):
                            d, g, place = DILATIONS[it.g], it.g, (2 if it.role == "k" else 4) + m
                            if g == 0 and it.role == "k" and m == 0:
                                dve.wait_ge(x_stored, 16)
                            for b, n in enumerate((BLK, BLK, LAST)):
                                dve.tensor_copy(positions(g, qkv[:, place, :])[:, :, BLK // d * b:BLK // d * b + n // d],
                                                T[:, b, 0:n].rearrange("p (j r) -> p r j", r=d))
                            dve.tensor_copy(k_new[:, g, m, :] if it.role == "k" else v_new[:, m, :], T[:, 2, LAST:BLK])\
                                .then_inc(big_free[t % 2], 1)
                        elif it.role in ("a_lin", "c_in"):
                            if it.role == "a_lin":
                                ep, es, gate, E = ext_p[:, m], ext_s[:, m], sig[:, m, :], EXT_A
                                if m == 0:
                                    own(dve.memset(ext_p[:, :, 0:EXT_A], 0.0))
                                    own(dve.tensor_copy(ext_s[:, :, :, 0:EXT_A],
                                                        st_fm.rearrange("p (m b t) -> p m b t", m=2, b=NB)))
                                big_evacuated(dve, t - 2)
                            else:
                                ep, es, gate, E = cext_p[:, m], cext_s[:, m], tmp[:, m, :], EXT_C
                                big_evacuated(dve, by_role["c_gate", it.j].big + m)
                            dve.tensor_tensor(ep[:, E:E + 2 * BLK].rearrange("p (b n) -> p b n", b=2), T[:, 0:2, 0:BLK],
                                              gate[:, 0:2 * BLK].rearrange("p (b n) -> p b n", b=2), ALU.mult)
                            dve.tensor_tensor(ep[:, E + 2 * BLK:E + SEQ], T[:, 2, 0:LAST], gate[:, 2 * BLK:SEQ], ALU.mult)
                            dve.tensor_tensor(es[:, :, E:E + NS], T[:, 2, LAST:BLK].rearrange("p (b s) -> p b s", b=NB),
                                              gate[:, SEQ:TOK].rearrange("p (b s) -> p b s", b=NB), ALU.mult)\
                                .then_inc(big_free[t % 2], 1)
                        elif it.role == "c_out":
                            if m == 0:
                                dve.wait_ge(cconv_done, 4 * C_CONV * (it.j + 1))
                            dve.tensor_tensor(blocks(tmp[:, m, :]), T[:, :, 0:BLK], blocks(tmp[:, m, :]), ALU.mult)\
                                .then_inc(big_free[t % 2], 1)
                    if it.role == "c_out":
                        for m in range(2):
                            dve.wait_ge(mixed_hi, 4 + 2 * it.j + m + 1)
                            ins = low(mid_lo[:, it.j, m, :], mid_hi[:, it.j, m, :], tmp[:, m, :])
                        ins.then_inc(mixed_ready, 1)
                elif it.kind == "a_state":
                    for m in range(2):
                        big_evacuated(dve, by_role["a_lin", 0].big + m)
                    dve.tensor_copy(st_fm.rearrange("p (m b t) -> p m b t", m=2, b=NB), ext_s[:, :, :, NS:NS + EXT_A])\
                        .then_inc(st_packed, 1)
                elif it.kind in ("conv", "c_conv"):
                    if it.kind == "conv":
                        ep, es, out, done, w0, width, b0 = ext_p, ext_s, conv_a, conv_step, V_AW, 2, V_AB
                        taps, before, col = range(*it.taps), 4 * it.taps[0], 0
                        for s in range(2):
                            big_evacuated(dve, by_role["a_lin", 0].big + s)
                    else:
                        ep, es, out, done, w0, width, b0 = cext_p, cext_s, tmp, cconv_done, V_CW, 4, V_CB
                        taps, before, col = range(C_CONV), 4 * C_CONV * it.j, 2 * it.j
                        for s in range(2):
                            big_evacuated(dve, by_role["c_in", it.j].big + s)
                            misc_evacuated(dve, c_in_misc[it.j])
                        if it.j:
                            misc_evacuated(dve, c_conv_misc[0] + 1)
                        dve.tensor_copy(c_pack.rearrange("p (m b t) -> p m b t", m=2, b=NB), cext_s[:, :, :, NS:NS + EXT_C])\
                            .then_inc(c_packed, 1)
                    for k in taps:
                        for m in range(2):
                            w = vecs[:, w0 + width * k + col + m:w0 + width * k + col + m + 1]
                            for sample in range(2):
                                if sample:
                                    src, dst = es[:, m, :, k:k + NS], out[:, m, SEQ:TOK].rearrange("p (b s) -> p b s", b=NB)
                                else:
                                    src, dst = ep[:, m, k:k + SEQ], out[:, m, 0:SEQ]
                                if k == 0:
                                    ins = dve.tensor_scalar(dst, src, w, vecs[:, b0 + col + m:b0 + col + m + 1], ALU.mult, ALU.add)
                                else:
                                    dve.wait_ge(done, before - 4 + 2 * m + sample + 1)
                                    ins = dve.scalar_tensor_tensor(dst, src, w, dst, ALU.mult, ALU.add)
                                ins.then_inc(done, 1)
                        before += 4
                elif it.kind == "tokens":
                    g = it.g
                    if g:
                        dve.wait_ge(k_stored, 16 * K_STORES[g - 1])
                        dve.wait_ge(kv_stored, 32 * g)
                    for sb in range(8):
                        q = it.v + sb
                        dve.wait_ge(misc_ready, q + 1)
                        dve.tensor_copy(v_tok[:, sb, :], misc(q)[:, 0:256]).then_inc(misc_free[q % 2], 1)
                    dve.wait_ge(misc_ready, it.new + 1)
                    dve.tensor_copy(kv_rows.rearrange("p k c -> p (k c)"), misc(it.new)[0:S_TOK, :])\
                        .then_inc(misc_free[it.new % 2], 1)
                elif it.kind == "attend":
                    g = it.g
                    if it.i == 0:
                        dve.wait_ge(k_stored, 16 * K_STORES[g])
                        if g == 2:
                            dve.wait_ge(bias_fixed, 1)
                        else:
                            dve.wait_ge(bias_loaded, 16 * (g + 1))
                    for i in (it.i,):
                        if i < 16:
                            step, a, n = 16 * g + i, i % 2, key_tiles(g, i // 2)
                            nk, q = P * n, it.qk[i]
                            s = sc[:, i % 2, 0:2 * nk].rearrange("p (h k) -> p h k", h=2)
                            dve.wait_ge(misc_ready, q + 1)
                            ins = dve.tensor_tensor(s, misc(q)[:, 0:2 * nk].rearrange("p (h k) -> p h k", h=2),
                                                    bias[:, 2 * a:2 * a + 2, 256 - nk:256], ALU.add)
                            ins.then_inc(misc_free[q % 2], 1)
                            misc_evacuated(dve, q)
                            if step >= 4:
                                dve.wait_ge(o_stored[step % 4], o_stores(step - 4))
                            dve.tensor_reduce(o_rows[:, step % 4, 130:132], s, AX_X, ALU.max, negate=True).then_inc(sc_max, 1)
                        if 2 <= i < 18:
                            step, q = 16 * g + i - 2, it.pv[i - 2]
                            dve.wait_ge(misc_ready, q + 1)
                            dve.tensor_copy(o_rows[:, step % 4, 0:128], misc(q)[:, 0:128]).then_inc(misc_free[q % 2], 1)
                elif it.kind == "ln_sum":
                    v, s = (conv_a, tmp[:, 0, :]) if it.which == "a" else (tmp, ln_t[:, 0, :])
                    if it.which == "a":
                        dve.wait_ge(conv_step, 4 * A_CONV)
                        misc_evacuated(dve, state_item.misc)
                        misc_evacuated(dve, state_item.misc + 1)
                    else:
                        for m in range(4):
                            big_evacuated(dve, by_role["d_v", m // 2].big + m % 2)
                    for m in range(1, it.nt):
                        ins = dve.tensor_tensor(s, v[:, 0, :] if m == 1 else s, v[:, m, :], ALU.add)
                        if m < it.nt - 1:
                            own(ins)
                    ins.then_inc(ln_sum, 1)
                elif it.kind == "ln_mean":
                    C, first = it.nt * P, 0 if it.which == "a" else 2
                    v, s, q = (conv_a, tmp[:, 0, :], tmp[:, 1, :]) if it.which == "a" else (tmp, ln_t[:, 0, :], ln_t[:, 1, :])
                    dve.wait_ge(big_ready, it.big + 1)
                    for m in range(it.nt):
                        ins = dve.scalar_tensor_tensor(blocks(v[:, m, :]), big(it.big)[:, :, 0:BLK], -float(D_MODEL // C),
                                                       blocks(v[:, m, :]), ALU.mult, ALU.add)
                    ins.then_inc(big_free[it.big % 2], 1)
                    for m in range(1, it.nt):
                        dve.wait_ge(ln_sq, first + m + 1)
                        dve.tensor_tensor(s, s, q, ALU.add).then_inc(ln_sqsum, 1)
                        ln_adds[0] += 1
                        dve.wait_ge(ln_sqsum, ln_adds[0])
                elif it.kind == "ln_var":
                    v, s, q = (conv_a, tmp[:, 0, :], tmp[:, 1, :]) if it.which == "a" else (tmp, ln_t[:, 0, :], ln_t[:, 1, :])
                    dve.wait_ge(ln_rs, 1 if it.which == "a" else 2)
                    for m in range(it.nt):
                        dve.tensor_tensor(v[:, m, :], v[:, m, :], q, ALU.mult).then_inc(ln_scaled, 1)
                    if it.which == "a":
                        for m in range(2):
                            dve.wait_ge(mixed_hi, m + 1)
                            ins = low(mid_lo[:, 0, m, :], mid_hi[:, 0, m, :], s if m == 0 else q)
                        ins.then_inc(mixed_ready, 1)
                elif it.kind == "down":
                    if it.weights == "e_w_out" and it.col == 0:
                        dve.wait_ge(x_back, 16)
                    evacuate_down(it.big, it.layer, it.gate)
                elif it.kind == "gate_sample":
                    gate = mod[:, 6 * it.layer + it.gate, :, 1:9].unsqueeze(3).to_broadcast([P, KT, NB, NS])
                    last = plan[plan.index(it) - 1]
                    tail = last.big + (8 if last.kind == "down" else 12 * GROUPS)
                    big_evacuated(dve, tail - 1)
                    big_evacuated(dve, tail - 2)
                    own(dve.tensor_tensor(acc_s.rearrange("p k (b s) -> p k b s", b=NB),
                                          acc_s.rearrange("p k (b s) -> p k b s", b=NB), gate, ALU.mult))
                    dve.tensor_tensor(x[:, :, SEQ:TOK], x[:, :, SEQ:TOK], acc_s, ALU.add).then_inc(x_done, 1)
                    x_dones[0] += 1
                    dve.wait_ge(x_done, x_dones[0])
                elif it.kind == "sample":
                    dve.wait_ge(qd_zero, 1)
                    dve.tensor_copy(q_diag[0:64, :, :, 0, :], q_new[0:64])
                    dve.tensor_copy(q_diag[64:128, :, :, 1, :], q_new[64:128]).then_inc(qd_made, 1)
                    dve.wait_ge(smp_loaded, 16 * 2)
                    dve.wait_ge(misc_ready, it.new + 1)
                    dve.tensor_tensor(p_s[:, :, P:160], misc(it.new)[:, 0:96].rearrange("p (g n) -> p g n", g=3),
                                      bias_s[:, :, P:160], ALU.add).then_inc(misc_free[it.new % 2], 1)
                    for n in range(0, 40, 2):
                        q = it.kt + n
                        dve.wait_ge(misc_ready, q + 1)
                        w = P * (2 if n % 5 == 4 else 4)
                        dve.tensor_copy(kTs[:, n % 2, 0:w], misc(q)[:, 0:w]).then_inc(misc_free[q % 2], 1)
                    dve.wait_ge(big_ready, it.qk + 1)
                    dve.tensor_copy(sT_s.rearrange("p g r -> p (g r)"), big(it.qk)[:, 0, 0:384]).then_inc(big_free[it.qk % 2], 1)
                    dve.wait_ge(misc_ready, it.rows + 1)
                    dve.tensor_tensor(p_s[:, :, 0:P], misc(it.rows)[:, 0:384].rearrange("p (g n) -> p g n", g=3),
                                      bias_s[:, :, 0:P], ALU.add).then_inc(misc_free[it.rows % 2], 1)
                    misc_evacuated(dve, it.new)
                    misc_evacuated(dve, it.rows)
                    dve.tensor_reduce(den_s[:, 0:1], p_s.rearrange("p g n -> p (g n)"), AX_X, ALU.max, negate=True)\
                        .then_inc(s_max, 1)
                    dve.wait_ge(s_exp, 1)
                    own(dve.reciprocal(den_s[:, 2:3], den_s[:, 1:2]))
                    dve.tensor_scalar(p_s, p_s, den_s[:, 2:3], None, ALU.mult).then_inc(s_norm, 1)
                    dve.wait_ge(misc_ready, it.tn + 1)
                    dve.tensor_copy(pT_n.rearrange("p g r -> p (g r)"), misc(it.tn)[0:S_TOK, 0:384])\
                        .then_inc(misc_free[it.tn % 2], 1)
                    rows = nat.rearrange("p g n a c -> p g (n a) c")
                    C = comb
                    dve.wait_ge(nat_loaded, 48)
                    own(dve.tensor_tensor(C[:, 0], rows[:, 0, :, 130:132], rows[:, 1, :, 130:132], ALU.min))
                    own(dve.tensor_tensor(C[:, 0], C[:, 0], rows[:, 2, :, 130:132], ALU.min))
                    for g in range(3):
                        ins = dve.tensor_tensor(C[:, 1 + g], C[:, 0], rows[:, g, :, 130:132], ALU.subtract)
                    ins.then_inc(comb_m, 1)
                    dve.wait_ge(comb_e, 1)
                    for g in range(3):
                        ins = dve.tensor_tensor(C[:, 4 + g], C[:, 1 + g], rows[:, g, :, 128:130], ALU.mult)
                    own(ins)
                    own(dve.tensor_tensor(C[:, 4], C[:, 4], C[:, 5], ALU.add))
                    own(dve.tensor_tensor(C[:, 4], C[:, 4], C[:, 6], ALU.add))
                    own(dve.reciprocal(C[:, 7], C[:, 4]))
                    for g in range(3):
                        ins = dve.tensor_tensor(C[:, 1 + g], C[:, 1 + g], C[:, 7], ALU.mult)
                    own(ins)
                    O_ = [rows[:, g, :, 0:128].rearrange("p n (h d) -> p n h d", h=2) for g in range(3)]
                    for g in range(3):
                        ins = dve.tensor_tensor(O_[g], O_[g], C[:, 1 + g].unsqueeze(3).to_broadcast([P, 16, 2, DH]), ALU.mult)
                    own(ins)
                    own(dve.tensor_tensor(O_[0], O_[0], O_[1], ALU.add))
                    dve.tensor_tensor(O_[0], O_[0], O_[2], ALU.add).then_inc(comb_done, 1)
                    dve.wait_ge(big_ready, it.pv + 1)
                    acc = big(it.pv)[:, 0, 0:128].rearrange("p (a h t) -> p a h t", a=2, h=2)
                    dve.tensor_copy(att_s[0:64], acc[0:64, :, 0, :])
                    dve.tensor_copy(att_s[64:128], acc[64:128, :, 1, :]).then_inc(big_free[it.pv % 2], 1)
                elif it.kind == "combine":
                    for a in range(2):
                        t = it.big + a
                        dve.wait_ge(mixed_hi, 3 + a)
                        dve.tensor_tensor(mid_lo[:, 1, a, 0:SEQ].rearrange("p (b n) -> p b n", b=2), big(t)[:, 0:2, :],
                                          mid_hi[:, 1, a, 0:SEQ].rearrange("p (b n) -> p b n", b=2).bitcast(F32), ALU.subtract)\
                            .then_inc(big_free[t % 2], 1)
                        ins = low(mid_lo[:, 1, a, SEQ:TOK], mid_hi[:, 1, a, SEQ:TOK], att_s[:, a, :])
                    ins.then_inc(mixed_ready, 1)
                elif it.kind == "ffn":
                    first = 2 * GROUPS * it.layer

                    def hidden(g, t, i):
                        for m in range(2):
                            dve.wait_ge(big_ready, steps(i, t + m + 1, 24))
                            dve.wait_ge(big_free[t % 2 if m == 0 else (t + 1) % 2], steps(i, (t - 2 + m) // 2 + 1, 12))
                            dve.tensor_tensor(blocks(tmp[:, m, :]), big(t + m)[:, :, 0:BLK], blocks(tmp[:, m, :]), ALU.mult)\
                                .then_inc(big_free[(t + m) % 2], 1)
                        for m in range(2):
                            dve.wait_ge(hid_hi, steps(i, first + 2 * g + m + 1, 4))
                            low(mid_lo[:, g % 2, m, :], mid_hi[:, g % 2, m, :], tmp[:, m, :]).then_inc(hid_lo, 1)

                    hidden(0, it.big + 2, None)
                    with dve.Fori(0, PAIRS) as i:
                        for k in range(2):
                            t = it.big + 4 + 12 * k
                            hidden(1 + k, t + 2, i)
                            evacuate_down(t + 4, it.layer, 5, i)
                    evacuate_down(it.big + 4 + 24 * PAIRS, it.layer, 5)
                elif it.kind == "c_load":
                    dve.memset(cext_p[:, :, 0:EXT_C], 0.0).then_inc(cpad_made, 1)
                    dve.wait_ge(cpad_made, 1)
                elif it.kind == "c_state_in":
                    dve.wait_ge(misc_ready, it.misc + 1)
                    if it.j:
                        misc_evacuated(dve, c_conv_misc[0])
                        misc_evacuated(dve, c_conv_misc[0] + 1)
                    dve.tensor_copy(cext_s[:, :, :, 0:EXT_C],
                                    misc(it.misc)[:, 0:2 * NB * EXT_C].rearrange("p (m b t) -> p m b t", m=2, b=NB))\
                        .then_inc(misc_free[it.misc % 2], 1)
                elif it.kind == "d_load":
                    dve.wait_ge(misc_ready, it.misc + 1)
                    dve.tensor_copy(wsT.rearrange("p g n -> p (g n)"), misc(it.misc)).then_inc(misc_free[it.misc % 2], 1)
                elif it.kind == "spatial":
                    for n in range(0, 9, 2):
                        q = it.tok + n
                        dve.wait_ge(misc_ready, q + 1)
                        if n < 8:
                            dve.tensor_copy(vd_tok[:, n, :], misc(q)).then_inc(misc_free[q % 2], 1)
                        else:
                            dve.tensor_copy(vd_new, misc(q)[0:S_TOK, :]).then_inc(misc_free[q % 2], 1)

                    def mixed(g):
                        t, y = it.big + g, ln_t[:, g % 2, :]
                        dve.wait_ge(big_ready, t + 1)
                        dve.tensor_tensor(y[:, 0:SEQ].rearrange("p (n i) -> p n i", i=P),
                                          big(t)[:, 0:2, :].rearrange("p b (n i) -> p (b n) i", i=P),
                                          bs_b[:, g, :].unsqueeze(1).to_broadcast([P, 8, P]), ALU.add)
                        dve.tensor_tensor(y[:, SEQ:TOK].rearrange("p (b s) -> p b s", b=NB),
                                          big(t)[:, 2, 0:S_TOK].rearrange("p (b s) -> p b s", b=NB),
                                          bs_b[:, g, 0:NS].unsqueeze(1).to_broadcast([P, NB, NS]), ALU.add)\
                            .then_inc(big_free[t % 2], 1)
                        big_evacuated(dve, t)
                        dve.tensor_tensor(y, y, u_fm[:, g, :], ALU.mult).then_inc(yd_made, 1)

                    def mixed_lo(g):
                        dve.wait_ge(mixed_hi, 8 + g + 1)
                        dve.wait_ge(yd_made, g + 1)
                        ins = low(h_lo[:, g, :], h_hi[:, g, :], ln_t[:, g % 2, :])
                        if g % 2:
                            ins.then_inc(mixed_ready, 1)
                        else:
                            own(ins)

                    dve.wait_ge(d_loaded, 32)
                    for s in range(2):
                        for m in range(2):
                            big_evacuated(dve, by_role["d_u", s].big + m)
                    mixed(0)
                    for g in range(1, 4):
                        if g >= 2:
                            if (g - 2) % 2:
                                dve.wait_ge(mixed_ready, 5)
                        mixed(g)
                        mixed_lo(g - 1)
                    mixed_lo(3)

        @block.gpsimd
        def _(pool):
            link = [0]

            def own(ins):
                link[0] += 1
                ins.then_inc(pool_link, 1)
                pool.wait_ge(pool_link, link[0])

            splits = [0]

            def split_lo(u, i=None):
                pool.wait_ge(w_hi_done, steps(i, u + 1, 6))
                cols = slice(0, 1024 if u in ada_number else 2048)
                pool.tensor_tensor(w_lo[u % 2][:, cols], w_raw[u % NRAW][:, cols], w_hi[u % 2][:, cols].bitcast(F32), ALU.subtract)\
                    .then_inc(w_lo_done, 1)
                splits[0] = u + 1

            def splits_done():
                pool.wait_ge(w_lo_done, splits[0])

            def move_caches(b):
                for g in range(3):
                    W = WINDOWS[g]
                    src = A[f"cache_b_kv{g}"][0, b, NS:W].rearrange("w k h e -> (w k h e)")
                    dst = O[f"kv{g}_sample"][0, b, 0:W - NS].rearrange("w k h e -> (w k h e)")
                    pool.dma_start(dst.rearrange("(n c) -> n c", c=2048), src.rearrange("(n c) -> n c", c=2048))\
                        .then_inc(caches_moved, 16)

            moved = [0]
            for it in plan:
                if it.kind == "setup":
                    pool.dma_start(tab, A["rel_bias_table"]).then_inc(tabs_loaded, 16)
                    pool.dma_start(oh_p, A["rel_prompt"]).then_inc(tabs_loaded, 16)
                    pool.dma_start(oh_s, A["rel_sample"]).then_inc(tabs_loaded, 16)
                    pool.dma_start(mask_s, A["mask_sample"]).then_inc(tabs_loaded, 16)
                    pool.dma_start(row_step, A["row_step"]).then_inc(tabs_loaded, 16)
                    pool.dma_start(st_rows, A["state_a_conv"][0].rearrange("(h b) t c -> (b t) h c", h=2))\
                        .then_inc(tabs_loaded, 16)
                    split_lo(0)
                elif it.kind == "ada":
                    split_lo(it.unit + 1)
                elif it.kind == "rel":
                    for t in x_tiles:
                        big_evacuated(pool, t)
                    pool.dma_start(d_x, x.rearrange("p k n -> p (k n)")).then_inc(x_stored, 16)
                    misc_evacuated(pool, it.rel + 11)
                    misc_evacuated(pool, it.rel + 10)
                    pool.dma_start(d_rel.rearrange("g (p n) -> p g n", n=384)[:, :, 0:REL], rel_rep[:, :, 0:REL])\
                        .then_inc(rel_stored, 16)
                    misc_evacuated(pool, it.rels + 1)
                    misc_evacuated(pool, it.rels)
                    pool.dma_start(d_bias, bias_s0.rearrange("p g n -> p (g n)")).then_inc(rel_stored, 16)
                elif it.kind == "norm":
                    n, c = it.n, 6 * it.layer + 3 * it.which
                    if n == 0:
                        pool.wait_ge(rel_stored, 32)
                    if n == 3:
                        pool.wait_ge(vd_stored, 16)
                    pool.wait_ge(scales_made, n + 1)
                    pool.wait_ge(xs_made, n + 1)
                    s = nt[:, :, SEQ:TOK].rearrange("p k (b s) -> p k b s", b=NB)
                    for op, row in ((ALU.mult, c + 1), (ALU.add, c)):
                        ins = pool.tensor_tensor(s, s, mod[:, row, :, 1:9].unsqueeze(3).to_broadcast([P, KT, NB, NS]), op)
                        if op == ALU.mult:
                            own(ins)
                    ins.then_inc(affs_made, 1)
                    pool.wait_ge(affs_made, n + 1)
                    for k in range(KT):
                        if k not in LO_DVE:
                            hi_made(pool, n, k)
                            pool.tensor_tensor(h_lo[:, k, :], nt[:, k, :], h_hi[:, k, :].bitcast(F32), ALU.subtract)\
                                .then_inc(h_pool, 1)
                elif it.kind in ("project", "down"):
                    if it.unit + 1 in unit_end:
                        split_lo(it.unit + 1)
                    if it.kind == "project" and it.weights == "o_w_in" and moved[0] < NB:
                        move_caches(moved[0])
                        moved[0] += 1
                elif it.kind == "tokens":
                    g = it.g
                    if g:
                        pool.wait_ge(sc_max, 16 * g)
                    else:
                        pool.wait_ge(rel_stored, 32)
                    src = d_rel[HPG * g:HPG * g + HPG, 0:P * REL].rearrange("h (p n) -> p h n", n=REL)[:, :, 127:REL]
                    pool.dma_start(bias, src).then_inc(bias_loaded, 16)
                    if g == 2:
                        pool.wait_ge(bias_loaded, 48)
                        splits_done()
                        pool.memset(bias[64:128, :, 128:192], MASKED).then_inc(bias_fixed, 1)
                        pool.wait_ge(bias_fixed, 1)
                elif it.kind == "x_back":
                    last = attends[-1]
                    misc_evacuated(pool, last.pv[15])
                    misc_evacuated(pool, last.pv[14])
                    misc_evacuated(pool, ada_outs[-1].misc)
                    pool.wait_ge(x_stored, 16)
                    pool.wait_ge(k_stored, 16 * K_STORES[2])
                    pool.dma_start(x.rearrange("p k n -> p (k n)"), d_x).then_inc(x_back, 16)
                elif it.kind == "sample":
                    pool.wait_ge(big_ready, by_role["v", 2].big + 2)
                    splits_done()
                    pool.memset(q_diag, 0.0).then_inc(qd_zero, 1)
                    for s in range(4):
                        pool.wait_ge(o_stored[s], o_stores(44 + s))
                    for g in range(3):
                        pool.dma_start(nat[:, g].rearrange("p n a c -> p n (a c)"),
                                       d_o[g].rearrange("(n p) c -> p n c", p=P)).then_inc(nat_loaded, 16)
                    pool.wait_ge(mixed_ready, 1)
                    pool.wait_ge(kv_stored, 16 * 6)
                    pool.dma_start(kv_s.rearrange("p g k c -> p g (k c)"), d_kv.rearrange("g t c -> t g c")).then_inc(smp_loaded, 16)
                    pool.dma_start(bias_s.rearrange("p g n -> p (g n)"), d_bias).then_inc(smp_loaded, 16)
                elif it.kind == "ffn":
                    u = it.unit
                    split_lo(u + 1)
                    split_lo(u + 2)
                    with pool.Fori(0, PAIRS) as i:
                        for n in range(6):
                            split_lo(u + 3 + n, i)
                    if u + 3 * GROUPS in unit_end:
                        split_lo(u + 3 * GROUPS)
                elif it.kind == "c_load":
                    pool.dma_start(cst_rows, A["state_c_conv"][0].rearrange("b t c -> (b t) c")).then_inc(c_loaded, 16)
                elif it.kind == "d_load":
                    misc_evacuated(pool, it.misc)
                    pool.affine_select(out=wsT, in_=wsT, compare_op=ALU.is_ge, fill=0.0, base=0,
                                       pattern=[[0, 4], [1, P]], channel_multiplier=-1).then_inc(wsT_made, 1)
                    pool.wait_ge(wsT_made, 1)
                    pool.memset(wsS, 0.0).then_inc(wsT_made, 1)
                    pool.wait_ge(wsT_made, 2)

        @block.tensor
        def _(pe):
            def big_slot(t, i=None):
                if t >= 2:
                    pe.wait_ge(big_free[t % 2], steps(i, t // 2, 12))

            def misc_slot(q):
                if q >= 2:
                    pe.wait_ge(misc_free[q % 2], q // 2)

            def dense_tile(t, K, w, x_hi, x_lo, i=None, ready=None):
                big_slot(t, i)
                for k in range(K):
                    if ready is not None:
                        ready(k)
                    for n, (wt, xt) in enumerate(((w(w_hi_s, k), x_hi), (w(w_hi_s, k), x_lo), (w(w_lo_s, k), x_hi))):
                        for b in range(3):
                            mm = pe.matmul(big(t)[:, b, 0:BLK], wt, xt[:, k, b * BLK:b * BLK + BLK],
                                           start=(k == 0 and n == 0), stop=(k == K - 1 and n == 2))
                mm.then_inc(big_ready, 1)

            w_hi_s, w_lo_s = 0, 1

            def project(u, t, i=None, first=None):
                pe.wait_ge(w_lo_done, steps(i, u + 1, 6))
                halves = [w[u % 2].rearrange("p (k n) -> p k n", k=KT) for w in (w_hi, w_lo)]
                for m in range(2):
                    dense_tile(t + m, KT, lambda s, k: halves[s][:, k, m * P:m * P + P], h_hi, h_lo, i,
                               (lambda k: lo_made(pe, first, k)) if first is not None and m == 0 else None)

            def down(u, t, x_hi, x_lo, i=None):
                pe.wait_ge(w_lo_done, steps(i, u + 1, 6))
                halves = [w[u % 2].rearrange("p (k n) -> p k n", k=2) for w in (w_hi, w_lo)]
                for m in range(KT):
                    dense_tile(t + m, 2, lambda s, k: halves[s][:, k, m * P:m * P + P], x_hi, x_lo, i)

            def mean(t, src):
                big_slot(t)
                for b in range(3):
                    mm = pe.matmul(big(t)[:, b, 0:BLK], mean_w, src[:, b * BLK:b * BLK + BLK], start=True, stop=True)
                mm.then_inc(big_ready, 1)

            for it in plan:
                if it.kind == "setup":
                    pe.wait_ge(in_loaded, 16 * 16)
                    pe.wait_ge(consts_made, 1)
                    col = 0
                    for set_, n in enumerate((V_MIX, V_AW - V_MIX, V_ALL - V_AW)):
                        mm = pe.transpose(misc(it.vec)[:, col:col + n], vrow[0:n, set_, :], ident[0:n, 0:n])
                        col += n
                    mm.then_inc(misc_ready, 1)
                    pe.wait_ge(c_silu, 1)
                    for k in range(KT):
                        mm = pe.transpose(misc(it.c)[:, 9 * k:9 * k + 9], c_rows[0:9, k * P:k * P + P], ident[0:9, 0:9])
                    mm.then_inc(misc_ready, 1)
                    pe.wait_ge(tabs_loaded, 16 * 6)
                    misc_slot(it.ext)
                    for m in range(2):
                        for half in range(2):
                            at_ = 240 * m + 120 * half
                            mm = pe.transpose(misc(it.ext)[:, at_:at_ + 120], st_rows[0:120, half, m * P:m * P + P],
                                              ident[0:120, 0:120])
                    mm.then_inc(misc_ready, 1)
                elif it.kind == "x_in":
                    k, t = it.k, it.x
                    pe.wait_ge(x_loaded, 16 * 9)
                    big_slot(t)
                    for n in range(8):
                        pe.transpose(big(t)[:, n // 4, (n % 4) * P:(n % 4) * P + P], x_tok[:, n, k * P:k * P + P], ident)
                    pe.transpose(big(t)[:, 2, 0:S_TOK], xs_tok[:, k * P:k * P + P], ident[0:S_TOK, 0:S_TOK])\
                        .then_inc(big_ready, 1)
                elif it.kind == "rel":
                    pe.wait_ge(tab_made, 1)
                    for n in range(12):
                        q = it.rel + n
                        misc_slot(q)
                        pe.matmul(misc(q)[:, 0:REL], tab_b[:, n, :], oh_p[:, n // HPG, :], start=True, stop=True)\
                            .then_inc(misc_ready, 1)
                    for n in range(2):
                        q = it.rels + n
                        misc_slot(q)
                        for s in range(3):
                            mm = pe.matmul(misc(q)[:, 160 * s:160 * s + 160],
                                           tab_s[:, max(0, 3 * n + s - 3)].rearrange("k h t -> k (h t)"),
                                           oh_s[:, 3 * n + s, :], start=True, stop=True)
                        mm.then_inc(misc_ready, 1)
                elif it.kind == "ada":
                    pe.wait_ge(w_lo_done, it.unit + 1)
                    pe.wait_ge(w_lo_half, it.k + 1)
                    misc_slot(it.misc)
                    halves = [w[it.unit % 2].rearrange("p (k n) -> p k n", k=KT) for w in (w_hi, w_lo)]
                    for k in range(KT):
                        pe.matmul(misc(it.misc)[0:18, 0:256], cs[:, k].rearrange("p a c -> p (a c)"), halves[0][:, k, :],
                                  start=(k == 0), stop=False, skip_group_check=True)
                    for k in range(KT):
                        mm = pe.matmul(misc(it.misc)[0:9, 0:256], cs[:, k, 0, :], halves[1][:, k, :],
                                       start=False, stop=(k == KT - 1), skip_group_check=True)
                    mm.then_inc(misc_ready, 1)
                elif it.kind == "ada_out":
                    misc_evacuated(pe, ada_misc[it.k])
                    misc_slot(it.misc)
                    for m in range(2):
                        mm = pe.matmul(misc(it.misc)[:, 9 * m:9 * m + 9], ada_rows[it.k >= 8][:, m * P:m * P + P], pair_sum,
                                       start=True, stop=True)
                    mm.then_inc(misc_ready, 1)
                elif it.kind in ("norm", "final"):
                    pe.wait_ge(sq_summed, 8 * (it.n + 1))
                    mean(it.big, tmp[:, 2, :])
                    if it.kind == "final":
                        pe.wait_ge(y_scaled, KT)
                        for n in range(9):
                            t, rows = it.out + n, P if n < 8 else S_TOK
                            big_slot(t)
                            for k in range(KT):
                                mm = pe.transpose(big(t)[0:rows, k // 4, (k % 4) * P:(k % 4) * P + P],
                                                  nt[:, k, n * P:n * P + rows], ident)
                            mm.then_inc(big_ready, 1)
                elif it.kind == "project":
                    project(it.unit, it.big, first=it.first)
                elif it.kind == "down":
                    pe.wait_ge(mixed_ready, it.ready)
                    if it.src == "mid":
                        down(it.unit, it.big, mid_hi[:, it.slot], mid_lo[:, it.slot])
                    else:
                        down(it.unit, it.big, h_hi[:, 2 * it.slot:2 * it.slot + 2, :], h_lo[:, 2 * it.slot:2 * it.slot + 2, :])
                elif it.kind == "a_state":
                    for s in range(2):
                        big_evacuated(pe, by_role["a_lin", 0].big + s)
                    misc_slot(it.misc)
                    for m in range(2):
                        mm = pe.transpose(misc(it.misc)[0:EXT_A, m * P:m * P + P], ext_p[:, m, SEQ:SEQ + EXT_A], ident)
                    mm.then_inc(misc_ready, 1)
                    pe.wait_ge(st_packed, 1)
                    misc_slot(it.misc + 1)
                    for half in range(2):
                        for m in range(2):
                            at_ = 256 * half + P * m
                            mm = pe.transpose(misc(it.misc + 1)[0:120, at_:at_ + P],
                                              st_fm[:, 240 * m + 120 * half:240 * m + 120 * half + 120], ident)
                    mm.then_inc(misc_ready, 1)
                elif it.kind == "tokens":
                    g = it.g
                    for role in "qkv":
                        for s in range(2):
                            big_evacuated(pe, by_role[role, g].big + s)
                    for sb in range(8):
                        misc_slot(it.v + sb)
                        for m in range(2):
                            mm = pe.transpose(misc(it.v + sb)[:, m * P:m * P + P], qkv[:, 4 + m, sb * P:sb * P + P], ident)
                        mm.then_inc(misc_ready, 1)
                    misc_slot(it.new)
                    for m in range(2):
                        pe.transpose(misc(it.new)[0:S_TOK, m * P:m * P + P], k_new[:, g, m, :], ident)
                        mm = pe.transpose(misc(it.new)[0:S_TOK, 256 + m * P:256 + m * P + P], v_new[:, m, :], ident)
                    mm.then_inc(misc_ready, 1)
                    for n, sb in enumerate(it.k_tiles):
                        misc_slot(it.k + n)
                        for m in range(2):
                            mm = pe.transpose(misc(it.k + n)[:, m * P:m * P + P], qkv[:, 2 + m, sb * P:sb * P + P], ident)
                        mm.then_inc(misc_ready, 1)
                elif it.kind == "attend":
                    g = it.g
                    for i in (it.i,):
                        if i < 16:
                            sb, a, n, q = i // 2, i % 2, key_tiles(g, i // 2), it.qk[i]
                            misc_slot(q)
                            for h in range(2):
                                at_ = slice(64 * h, 64 * h + 64)
                                if h:
                                    mm.then_inc(qk_half, 1)
                                    pe.wait_ge(qk_half, 16 * g + i + 1)
                                mm = pe.matmul(misc(q)[:, h * n * P:(h + 1) * n * P], qkv[at_, a, P * sb:P * sb + P],
                                               qkv[at_, 2 + a, P * (sb + 1 - n):P * (sb + 1)], start=True, stop=True)
                            mm.then_inc(misc_ready, 1)
                        if 0 <= i - 1 < 16:
                            j, n, q = i - 1, key_tiles(g, (i - 1) // 2), it.tr[i - 1]
                            pe.wait_ge(exp_done, 16 * g + j + 1)
                            misc_slot(q)
                            for c in range(2 * n):
                                mm = pe.transpose(misc(q)[:, c * P:c * P + P], sc[:, j % 2, c * P:c * P + P], ident)
                            mm.then_inc(misc_ready, 1)
                        if 2 <= i < 18:
                            j, n, q = i - 2, key_tiles(g, (i - 2) // 2), it.pv[i - 2]
                            sb, a = j // 2, j % 2
                            misc_evacuated(pe, it.tr[j])
                            misc_slot(q)
                            for h in range(2):
                                for c in range(n):
                                    mm = pe.matmul(misc(q)[:, h * DH:h * DH + DH], pt[:, j % 2, (h * n + c) * P:(h * n + c) * P + P],
                                                   v_tok[:, sb + 1 - n + c, (2 * a + h) * DH:(2 * a + h + 1) * DH],
                                                   start=(c == 0), stop=(c == n - 1))
                            mm.then_inc(misc_ready, 1)
                elif it.kind in ("ln_mean", "ln_var"):
                    if it.kind == "ln_mean":
                        pe.wait_ge(ln_sum, 1 if it.which == "a" else 2)
                    else:
                        pe.wait_ge(ln_sqsum, 1 if it.which == "a" else 4)
                    mean(it.big, tmp[:, 0, :] if it.which == "a" else ln_t[:, 0, :])
                elif it.kind == "sample":
                    misc_slot(it.new)
                    for h in (0, 2, 1, 3):
                        if h == 1:
                            mm.then_inc(qk_half, 1)
                            pe.wait_ge(qk_half, 16 * 3 + 1)
                        for g in range(3):
                            at_ = slice(64 * (h % 2), 64 * (h % 2) + 64)
                            mm = pe.matmul(misc(it.new)[32 * h:32 * h + 32, 32 * g:32 * g + 32], q_new[at_, g, h // 2, :],
                                           k_new[at_, g, h // 2, :], start=True, stop=True)
                    mm.then_inc(misc_ready, 1)
                    pe.wait_ge(qd_made, 1)
                    big_slot(it.qk)
                    scores = big(it.qk)[:, 0, 0:384].rearrange("p (g r) -> p g r", g=3)
                    for n in range(41):
                        if n < 40:
                            b, c = divmod(n, 5)
                            if c == 0:
                                pe.wait_ge(cache_loaded[b % 3], 48 * (b // 3 + 1))
                            misc_slot(it.kt + n)
                            for j in range(2 if c == 4 else 4):
                                mm = pe.transpose(misc(it.kt + n)[:, j * P:j * P + P],
                                                  cache[:, b % 3, 2 * c + j // 2, (j % 2) * P:(j % 2) * P + P], ident)
                            mm.then_inc(misc_ready, 1)
                        if n >= 1:
                            b, c = divmod(n - 1, 5)
                            misc_evacuated(pe, it.kt + n - 1)
                            for j in range(2 if c == 4 else 4):
                                g, s = CACHE_TILES[2 * c + j // 2]
                                mm = pe.matmul(cache_cols(scores[:, g], g, j % 2, b, s),
                                               kTs[:, (n - 1) % 2, j * P:j * P + P],
                                               q_diag[:, g, j % 2, :, NS * b:NS * b + NS] if g == 0 else
                                               q_diag[:, g, j % 2, :, NS * b + s:NS * b + s + 1], start=True, stop=True)
                    mm.then_inc(big_ready, 1)
                    big_evacuated(pe, it.qk)
                    misc_slot(it.rows)
                    for g in range(3):
                        mm = pe.transpose(misc(it.rows)[:, g * P:g * P + P], sT_s[:, g, :], ident)
                    mm.then_inc(misc_ready, 1)
                    pe.wait_ge(s_norm, 1)
                    misc_slot(it.tp)
                    for g in range(3):
                        mm = pe.transpose(misc(it.tp)[:, g * P:g * P + P], p_s[:, g, 0:P], ident)
                    mm.then_inc(misc_ready, 1)
                    misc_slot(it.tn)
                    for g in range(3):
                        mm = pe.transpose(misc(it.tn)[0:S_TOK, g * P:g * P + P], p_s[:, g, P:160], ident)
                    mm.then_inc(misc_ready, 1)
                    big_slot(it.pv)
                    acc = big(it.pv)[:, 0, 0:128].rearrange("p (a r) -> p a r", a=2)
                    pe.wait_ge(smp_loaded, 32)
                    misc_evacuated(pe, it.tp)
                    misc_evacuated(pe, it.tn)
                    for a in range(2):
                        for g in range(3):
                            pe.matmul(acc[:, a, :], kv_s[:, g, 1, a * P:a * P + P], pT_n[:, g, 64 * a:64 * a + 64],
                                      start=(a == 0 and g == 0), stop=False, skip_group_check=True)
                    for b in range(NB):
                        c = NB + b
                        pe.wait_ge(cache_loaded[c % 3], 48 * (c // 3 + 1))
                        for tile, (g, s) in enumerate(CACHE_TILES):
                            for a in range(2):
                                out = acc[:, a, :].rearrange("p (h t) -> p h t", h=2)
                                out = out[:, :, NS * b:NS * b + NS] if g == 0 else out[:, :, NS * b + s:NS * b + s + 1]
                                last = b == NB - 1 and tile == 8 and a == 1
                                mm = pe.matmul(out, cache[:, c % 3, tile, a * P:a * P + P], cache_cols(pT_s[:, g], g, a, b, s),
                                               start=False, stop=last, skip_group_check=True)
                        if b < NB - 1:
                            mm.then_inc(v_used, 1)
                    mm.then_inc(big_ready, 1)
                elif it.kind == "combine":
                    pe.wait_ge(comb_done, 1)
                    for a in range(2):
                        big_slot(it.big + a)
                        for n in range(8):
                            mm = pe.transpose(big(it.big + a)[:, n // 4, (n % 4) * P:(n % 4) * P + P], nat[:, 0, n, a, 0:P], ident)
                        mm.then_inc(big_ready, 1)
                elif it.kind == "ffn":
                    first, u = 2 * GROUPS * it.layer, it.unit
                    project(u, it.big, first=it.first)
                    project(u + 1, it.big + 2)
                    with pe.Fori(0, PAIRS) as i:
                        for k in range(2):
                            t = it.big + 4 + 12 * k
                            project(u + 2 + 3 * k, t, i)
                            project(u + 3 + 3 * k, t + 2, i)
                            pe.wait_ge(hid_lo, steps(i, first + 2 * k + 2, 4))
                            down(u + 4 + 3 * k, t + 4, mid_hi[:, k], mid_lo[:, k], i)
                    pe.wait_ge(hid_lo, first + 2 * GROUPS)
                    down(u + 3 * GROUPS - 1, it.big + 4 + 24 * PAIRS, mid_hi[:, 0], mid_lo[:, 0])
                elif it.kind == "c_state_in":
                    pe.wait_ge(c_loaded, 16)
                    misc_slot(it.misc)
                    for m in range(2):
                        mm = pe.transpose(misc(it.misc)[:, 16 * m:16 * m + 16],
                                          cst_rows[:, 256 * it.j + P * m:256 * it.j + P * m + P], ident[0:16, 0:16])
                    mm.then_inc(misc_ready, 1)
                elif it.kind == "c_conv":
                    for s in range(2):
                        big_evacuated(pe, by_role["c_in", it.j].big + s)
                    misc_slot(it.misc)
                    for m in range(2):
                        mm = pe.transpose(misc(it.misc)[0:EXT_C, m * P:m * P + P], cext_p[:, m, SEQ:SEQ + EXT_C], ident)
                    mm.then_inc(misc_ready, 1)
                    pe.wait_ge(c_packed, it.j + 1)
                    misc_slot(it.misc + 1)
                    for m in range(2):
                        mm = pe.transpose(misc(it.misc + 1)[0:16, m * P:m * P + P], c_pack[:, 16 * m:16 * m + 16], ident)
                    mm.then_inc(misc_ready, 1)
                elif it.kind == "d_load":
                    pe.wait_ge(d_loaded, 32)
                    misc_slot(it.misc)
                    for g in range(4):
                        mm = pe.transpose(misc(it.misc)[:, g * P:g * P + P], ws_raw[:, g, :], ident)
                    mm.then_inc(misc_ready, 1)
                elif it.kind == "spatial":
                    pe.wait_ge(ln_out, 2 + 4)
                    for n in range(9):
                        q, rows = it.tok + n, P if n < 8 else S_TOK
                        misc_slot(q)
                        for g in range(4):
                            mm = pe.transpose(misc(q)[0:rows, g * P:g * P + P], tmp[:, g, n * P:n * P + rows], ident)
                        mm.then_inc(misc_ready, 1)
                    misc_evacuated(pe, it.tok + 7)
                    misc_evacuated(pe, it.tok + 8)
                    pe.wait_ge(wsT_made, 2)
                    pe.wait_ge(wsS_loaded, 16 * NB)
                    for g in range(4):
                        t = it.big + g
                        big_slot(t)
                        for n in range(8):
                            pe.matmul(big(t)[:, n // 4, (n % 4) * P:(n % 4) * P + P], vd_tok[:, n, g * P:g * P + P],
                                      wsT[:, g, :], start=True, stop=True)
                        pe.matmul(big(t)[:, 2, 0:S_TOK], vd_new[:, g * P:g * P + P], wsS[:, g, :], start=True, stop=True)\
                            .then_inc(big_ready, 1)


_OUTS = [("y_prompt", (1, 1024, 1024)), ("y_sample", (8, 4, 1024)), ("a_conv_prompt", (1, 1, 30, 256)),
         ("a_conv_sample", (1, 8, 30, 256)), ("kv0_prompt", (1, 1, 128, 2, 4, 64)), ("kv0_sample", (1, 8, 128, 2, 4, 64)),
         ("kv1_prompt", (1, 1, 512, 2, 4, 64)), ("kv1_sample", (1, 8, 512, 2, 4, 64)),
         ("kv2_prompt", (1, 1, 1024, 2, 4, 64)), ("kv2_sample", (1, 8, 2048, 2, 4, 64)),
         ("c_conv_prompt", (1, 1, 2, 512)), ("c_conv_sample", (1, 8, 2, 512)), ("d_v_sample", (1, 8, 4, 512))]


def kernel(**inputs):
    import concourse.bacc as bacc
    from concourse.bass_utils import run_bass_kernel_spmd

    nc = bacc.Bacc("TRN2", target_bir_lowering=False, num_devices=1)
    arrays, A, O = {}, {}, {}
    for name, a in {**inputs, **shape_constants()}.items():
        a = np.ascontiguousarray(a)
        arrays[f"in_{name}"] = a
        A[name] = nc.dram_tensor(f"in_{name}", a.shape, mybir.dt.from_np(a.dtype), kind="ExternalInput").ap()
    for name, shape in _OUTS:
        O[name] = nc.dram_tensor(f"out_{name}", shape, F32, kind="ExternalOutput").ap()
    build_trunk(nc, A, O)
    r = run_bass_kernel_spmd(nc, [arrays], core_ids=[0])
    return tuple(r.results[0][f"out_{name}"] for name, _ in _OUTS)
```
